# Optimizing a Trainium2 kernel written in Bass

```python
import math
import jax, jax.numpy as jnp
from jax import lax
import numpy as np

D_MODEL = 1024
BATCH = 1
SEQ = 512
DEPTH = 1
DEC_BATCH = 8
DEC_SEQ = 1
PAST_LEN = 4096
PAGE_SIZE = 128

RW_HEADS = 8
RW_HEAD_DIM = 64
RW_WIDTH = RW_HEADS * RW_HEAD_DIM
RW_DECAY_RANK = 64
RW_A_RANK = 64
RW_GATE_RANK = 128
RW_GN_EPS = RW_HEAD_DIM * 1e-5
RW_COLS = 3 * RW_WIDTH + RW_DECAY_RANK + RW_A_RANK + RW_GATE_RANK
RW_SPLITS = (RW_WIDTH, 2 * RW_WIDTH, 3 * RW_WIDTH,
             3 * RW_WIDTH + RW_DECAY_RANK, 3 * RW_WIDTH + RW_DECAY_RANK + RW_A_RANK)
GD_HEADS = 4
GD_HEAD_DIM = 128
GD_WIDTH = GD_HEADS * GD_HEAD_DIM
GD_QKV = 3 * GD_WIDTH
GD_CONV = 4
GD_CHUNK = 64
GD_COLS = GD_QKV + GD_WIDTH + 2 * GD_HEADS
GD_EPS = 1e-6
GATE_COLS = 2 * D_MODEL
P_TOTAL = RW_COLS + GD_COLS + GATE_COLS
PEER_HEADS = 8
PEER_KEY_DIM = 256
PEER_HALF = PEER_KEY_DIM // 2
N_KEYS = 128
N_EXPERTS = N_KEYS * N_KEYS
PEER_TOPK = 16
PEER_BLOCK = 128
DN_ALPHA = (2 * DEPTH) ** 0.25
DN_BETA = (8 * DEPTH) ** -0.25
LN_EPS = 1e-5

kernel_name = 'hybrid_rwkv7_gdn_peer_step'

F32 = jnp.float32

def layer_norm(x, g, b):
    xf = x.astype(F32)
    mu = jnp.mean(xf, axis=-1, keepdims=True)
    xc = xf - mu
    var = jnp.mean(xc * xc, axis=-1, keepdims=True)
    return (xc * lax.rsqrt(var + LN_EPS) * g + b).astype(x.dtype)

def l2norm(t, eps):
    return t * lax.rsqrt(jnp.sum(t * t, axis=-1, keepdims=True) + eps)

def token_shift(cur, prev):
    return jnp.concatenate([prev[:, None].astype(cur.dtype), cur[:, :-1]], axis=1)

def causal_conv(x, buf, w):
    L = x.shape[1]
    xp = jnp.concatenate([buf.astype(x.dtype), x], axis=1)
    out = sum(xp[:, j:j + L] * w[j] for j in range(GD_CONV))
    return out, xp[:, -(GD_CONV - 1):]

def rwkv7_scan(S0, r, decay, k, v, kk, a):
    def step(S, xs):
        r_t, w_t, k_t, v_t, kk_t, a_t = xs
        sa = jnp.einsum('bhvk,bhk->bhv', S, -kk_t)
        S = (S * w_t[:, :, None, :] + sa[..., None] * (kk_t * a_t)[:, :, None, :]
             + v_t[..., None] * k_t[:, :, None, :])
        return S, jnp.einsum('bhvk,bhk->bhv', S, r_t)
    xs = tuple(jnp.moveaxis(t, 1, 0) for t in (r, decay, k, v, kk, a))
    S, o = lax.scan(step, S0, xs)
    return jnp.moveaxis(o, 0, 1), S

def rwkv_branch(p, prev, S0, lp):
    B, L, _ = p.shape
    ps = (p + (token_shift(p, prev) - p) * lp['rwkv_mu']).astype(F32)
    r, k, v, xw, xa, xg = jnp.split(ps, RW_SPLITS, axis=-1)
    w = -jax.nn.softplus(-(lp['rwkv_w0'] + jnp.tanh(xw) @ lp['rwkv_w2'])) - 0.5
    decay = jnp.exp(-jnp.exp(w))
    a = jax.nn.sigmoid(lp['rwkv_a0'] + xa @ lp['rwkv_a2'])
    g = jax.nn.sigmoid(xg) @ lp['rwkv_g2']
    heads = lambda t: t.reshape(B, L, RW_HEADS, RW_HEAD_DIM)
    kk = l2norm(heads(k * lp['rwkv_k_k']), 1e-12)
    k = k * (1.0 + (a - 1.0) * lp['rwkv_k_a'])
    rh, kh, vh = heads(r), heads(k), heads(v)
    o, S = rwkv7_scan(S0.astype(F32), rh, heads(decay), kh, vh, kk, heads(a))
    mu = jnp.mean(o, axis=-1, keepdims=True)
    oc = o - mu
    on = oc * lax.rsqrt(jnp.mean(oc * oc, axis=-1, keepdims=True) + RW_GN_EPS)
    on = on.reshape(B, L, RW_WIDTH) * lp['rwkv_ln_w'] + lp['rwkv_ln_b']
    bonus = jnp.sum(rh * kh * lp['rwkv_r_k'], axis=-1, keepdims=True) * vh
    out = (on + bonus.reshape(B, L, RW_WIDTH)) * g
    return out, p[:, -1], S

def gdn_chunked(q, k, v, g, beta, S0):
    B, L, H, _ = q.shape
    C = GD_CHUNK
    N = L // C
    chunks = lambda t: t.reshape(B, N, C, H, -1).transpose(1, 0, 3, 2, 4)
    per_head = lambda t: t.reshape(B, N, C, H).transpose(1, 0, 3, 2)
    qc, kc, vc = chunks(q), chunks(k), chunks(v)
    gc = jnp.cumsum(per_head(g), axis=-1)
    bc = per_head(beta)
    kb = kc * bc[..., None]
    vb = vc * bc[..., None]
    causal = jnp.tril(jnp.ones((C, C), bool))
    strict = jnp.tril(jnp.ones((C, C), bool), -1)
    decay = jnp.exp(jnp.where(causal, gc[..., :, None] - gc[..., None, :], -jnp.inf))
    lower = jnp.where(strict, jnp.einsum('nbhid,nbhjd->nbhij', kb, kc) * decay, 0.0)
    eye = jnp.eye(C, dtype=F32)
    tinv = lax.linalg.triangular_solve(eye + lower, jnp.broadcast_to(eye, lower.shape),
                                       left_side=True, lower=True, unit_diagonal=True)
    u = tinv @ vb
    wk = tinv @ (kb * jnp.exp(gc)[..., None])
    intra = jnp.where(causal, jnp.einsum('nbhid,nbhjd->nbhij', qc, kc) * decay, 0.0)
    qg = qc * jnp.exp(gc)[..., None]
    kdec = kc * jnp.exp(gc[..., -1:] - gc)[..., None]
    glast = jnp.exp(gc[..., -1])

    def step(S, xs):
        u_n, w_n, qg_n, intra_n, kdec_n, gl_n = xs
        vnew = u_n - w_n @ S
        o = qg_n @ S + intra_n @ vnew
        S = S * gl_n[..., None, None] + jnp.einsum('bhcd,bhce->bhde', kdec_n, vnew)
        return S, o

    S, o = lax.scan(step, S0, (u, wk, qg, intra, kdec, glast))
    o = o.transpose(1, 0, 3, 2, 4).reshape(B, L, H, -1)
    return o, S

def gdn_recurrent(q, k, v, g, beta, S0):
    def step(S, xs):
        q_t, k_t, v_t, g_t, b_t = xs
        S = S * jnp.exp(g_t)[..., None, None]
        kv = jnp.einsum('bhde,bhd->bhe', S, k_t)
        delta = (v_t - kv) * b_t[..., None]
        S = S + k_t[..., None] * delta[..., None, :]
        return S, jnp.einsum('bhde,bhd->bhe', S, q_t)
    xs = tuple(jnp.moveaxis(t, 1, 0) for t in (q, k, v, g, beta))
    S, o = lax.scan(step, S0, xs)
    return jnp.moveaxis(o, 0, 1), S

def gdn_branch(p, conv_buf, S0, lp, chunked):
    B, L, _ = p.shape
    qkv = p[..., :GD_QKV]
    z = p[..., GD_QKV:GD_QKV + GD_WIDTH]
    b_in = p[..., GD_QKV + GD_WIDTH:GD_QKV + GD_WIDTH + GD_HEADS]
    a_in = p[..., GD_QKV + GD_WIDTH + GD_HEADS:]
    qkv_c, new_buf = causal_conv(qkv, conv_buf, lp['gdn_conv_w'])
    qkv_c = jax.nn.silu(qkv_c).astype(F32)
    heads = lambda t: t.reshape(B, L, GD_HEADS, GD_HEAD_DIM)
    q, k, v = (heads(t) for t in jnp.split(qkv_c, 3, axis=-1))
    q = l2norm(q, GD_EPS) * (GD_HEAD_DIM ** -0.5)
    k = l2norm(k, GD_EPS)
    beta = jax.nn.sigmoid(b_in.astype(F32))
    g = -jnp.exp(lp['gdn_a_log']) * jax.nn.softplus(a_in.astype(F32) + lp['gdn_dt_bias'])
    if chunked:
        o, S = gdn_chunked(q, k, v, g, beta, S0.astype(F32))
    else:
        o, S = gdn_recurrent(q, k, v, g, beta, S0.astype(F32))
    on = o * lax.rsqrt(jnp.mean(o * o, axis=-1, keepdims=True) + GD_EPS) * lp['gdn_norm_w']
    on = on * jax.nn.silu(heads(z.astype(F32)))
    return on.reshape(B, L, GD_WIDTH), new_buf, S

def time_mix(h, shift_prev, wkv0, conv_buf, ssm0, lp, chunked):
    p = h @ lp['w_in']
    p_rw = p[..., :RW_COLS]
    p_gd = p[..., RW_COLS:RW_COLS + GD_COLS]
    gates = jax.nn.sigmoid(p[..., RW_COLS + GD_COLS:])
    ya, shift_new, wkv = rwkv_branch(p_rw, shift_prev, wkv0, lp)
    yb, conv_new, ssm = gdn_branch(p_gd, conv_buf, ssm0, lp, chunked)
    ya = ya.astype(h.dtype) @ lp['w_branch_a']
    yb = yb.astype(h.dtype) @ lp['w_branch_b']
    merged = gates[..., :D_MODEL] * ya + gates[..., D_MODEL:] * yb
    return merged @ lp['w_out'], (shift_new, wkv, conv_new, ssm)

def peer_ffn(x, wq, subkeys, u_tab, v_tab):
    B, L, D = x.shape
    T = B * L
    t = x.reshape(T, D)
    q = (t @ wq).astype(F32).reshape(T, PEER_HEADS, 2, PEER_HALF)
    s = jnp.einsum('thpc,hpnc->thpn', q, subkeys.astype(F32))
    s1, i1 = lax.top_k(s[:, :, 0], PEER_TOPK)
    s2, i2 = lax.top_k(s[:, :, 1], PEER_TOPK)
    cand = (s1[..., :, None] + s2[..., None, :]).reshape(T, PEER_HEADS, PEER_TOPK * PEER_TOPK)
    sc, ci = lax.top_k(cand, PEER_TOPK)
    expert = (jnp.take_along_axis(i1, ci // PEER_TOPK, axis=-1) * N_KEYS
              + jnp.take_along_axis(i2, ci % PEER_TOPK, axis=-1))
    gate = jax.nn.softmax(sc, axis=-1)
    expert = expert.reshape(T, PEER_HEADS * PEER_TOPK)
    gate = gate.reshape(T, PEER_HEADS * PEER_TOPK).astype(x.dtype)
    nb = -(-T // PEER_BLOCK)
    pad = nb * PEER_BLOCK - T
    tb = jnp.pad(t, ((0, pad), (0, 0))).reshape(nb, PEER_BLOCK, D)
    eb = jnp.pad(expert, ((0, pad), (0, 0))).reshape(nb, PEER_BLOCK, -1)
    gb = jnp.pad(gate, ((0, pad), (0, 0))).reshape(nb, PEER_BLOCK, -1)

    def apply(blk):
        x_b, e_b, g_b = blk
        hpre = jnp.einsum('tkd,td->tk', u_tab[e_b], x_b)
        return jnp.einsum('tk,tkd->td', g_b * jax.nn.gelu(hpre, approximate=False), v_tab[e_b])

    y = lax.map(apply, (tb, eb, gb))
    return y.reshape(nb * PEER_BLOCK, D)[:T].reshape(B, L, D)

def decoder_layer(x, shift_prev, wkv0, conv_buf, ssm0, lp, chunked):
    mix, st = time_mix(x, shift_prev, wkv0, conv_buf, ssm0, lp, chunked)
    x1 = layer_norm(DN_ALPHA * x + mix, lp['ln1_g'], lp['ln1_b'])
    ff = peer_ffn(x1, lp['peer_wq'], lp['peer_subkeys'], lp['peer_u'], lp['peer_v'])
    x2 = layer_norm(DN_ALPHA * x1 + ff, lp['ln2_g'], lp['ln2_b'])
    return x2, st

def setup_inputs(seed: int = 0) -> dict:
    key = jax.random.key(seed)
    ks = iter(jax.random.split(key, 48))
    nrm = lambda shape, scale: jax.random.normal(next(ks), shape, F32) * scale
    uni = lambda shape, lo, hi: jax.random.uniform(next(ks), shape, F32, lo, hi)
    Ld, D = DEPTH, D_MODEL
    dt = jnp.exp(uni((Ld, GD_HEADS), math.log(1e-3), math.log(1e-1)))
    return {
        'x_prompt': nrm((BATCH, SEQ, D), 1.0),
        'x_sample': nrm((DEC_BATCH, DEC_SEQ, D), 1.0),
        'state_rwkv_shift': nrm((Ld, DEC_BATCH, RW_COLS), 1.0),
        'state_rwkv_wkv': nrm((Ld, DEC_BATCH, RW_HEADS, RW_HEAD_DIM, RW_HEAD_DIM), 0.5),
        'state_gdn_conv': nrm((Ld, DEC_BATCH, GD_CONV - 1, GD_QKV), 1.0),
        'state_gdn_ssm': nrm((Ld, DEC_BATCH, GD_HEADS, GD_HEAD_DIM, GD_HEAD_DIM), 0.1),
        'w_in': nrm((Ld, D, P_TOTAL), D ** -0.5),
        'rwkv_mu': uni((Ld, RW_COLS), 0.0, 1.0),
        'rwkv_w0': uni((Ld, RW_WIDTH), -5.0, -1.0),
        'rwkv_w2': nrm((Ld, RW_DECAY_RANK, RW_WIDTH), 0.5 * RW_DECAY_RANK ** -0.5),
        'rwkv_a0': nrm((Ld, RW_WIDTH), 0.1),
        'rwkv_a2': nrm((Ld, RW_A_RANK, RW_WIDTH), 0.5 * RW_A_RANK ** -0.5),
        'rwkv_g2': nrm((Ld, RW_GATE_RANK, RW_WIDTH), RW_GATE_RANK ** -0.5),
        'rwkv_k_k': 0.85 + nrm((Ld, RW_WIDTH), 0.05),
        'rwkv_k_a': 1.0 + nrm((Ld, RW_WIDTH), 0.05),
        'rwkv_r_k': nrm((Ld, RW_HEADS, RW_HEAD_DIM), 0.1),
        'rwkv_ln_w': 1.0 + nrm((Ld, RW_WIDTH), 0.02),
        'rwkv_ln_b': nrm((Ld, RW_WIDTH), 0.02),
        'gdn_conv_w': nrm((Ld, GD_CONV, GD_QKV), GD_CONV ** -0.5),
        'gdn_a_log': jnp.log(uni((Ld, GD_HEADS), 1.0, 16.0)),
        'gdn_dt_bias': dt + jnp.log(-jnp.expm1(-dt)),
        'gdn_norm_w': 1.0 + nrm((Ld, GD_HEAD_DIM), 0.02),
        'w_branch_a': nrm((Ld, RW_WIDTH, D), DN_BETA * RW_WIDTH ** -0.5),
        'w_branch_b': nrm((Ld, GD_WIDTH, D), DN_BETA * GD_WIDTH ** -0.5),
        'w_out': nrm((Ld, D, D), DN_BETA * D ** -0.5),
        'ln1_g': 1.0 + nrm((Ld, D), 0.02),
        'ln1_b': nrm((Ld, D), 0.02),
        'peer_wq': nrm((Ld, D, PEER_HEADS * PEER_KEY_DIM), D ** -0.5),
        'peer_subkeys': nrm((Ld, PEER_HEADS, 2, N_KEYS, PEER_HALF), PEER_HALF ** -0.5),
        'peer_u': nrm((Ld, N_EXPERTS, D), D ** -0.5),
        'peer_v': nrm((Ld, N_EXPERTS, D), DN_BETA),
        'ln2_g': 1.0 + nrm((Ld, D), 0.02),
        'ln2_b': nrm((Ld, D), 0.02),
    }

def reference(x_prompt, x_sample, state_rwkv_shift, state_rwkv_wkv, state_gdn_conv, state_gdn_ssm,
              w_in, rwkv_mu, rwkv_w0, rwkv_w2, rwkv_a0, rwkv_a2, rwkv_g2, rwkv_k_k, rwkv_k_a,
              rwkv_r_k, rwkv_ln_w, rwkv_ln_b, gdn_conv_w, gdn_a_log, gdn_dt_bias, gdn_norm_w,
              w_branch_a, w_branch_b, w_out, ln1_g, ln1_b, peer_wq, peer_subkeys, peer_u, peer_v,
              ln2_g, ln2_b):
    hp, hs = x_prompt, x_sample
    p_shift, p_wkv, p_conv, p_ssm = [], [], [], []
    s_shift, s_wkv, s_conv, s_ssm = [], [], [], []
    for l in range(DEPTH):
        lp = dict(w_in=w_in[l], rwkv_mu=rwkv_mu[l], rwkv_w0=rwkv_w0[l], rwkv_w2=rwkv_w2[l],
                  rwkv_a0=rwkv_a0[l], rwkv_a2=rwkv_a2[l], rwkv_g2=rwkv_g2[l],
                  rwkv_k_k=rwkv_k_k[l], rwkv_k_a=rwkv_k_a[l], rwkv_r_k=rwkv_r_k[l],
                  rwkv_ln_w=rwkv_ln_w[l], rwkv_ln_b=rwkv_ln_b[l], gdn_conv_w=gdn_conv_w[l],
                  gdn_a_log=gdn_a_log[l], gdn_dt_bias=gdn_dt_bias[l], gdn_norm_w=gdn_norm_w[l],
                  w_branch_a=w_branch_a[l], w_branch_b=w_branch_b[l], w_out=w_out[l],
                  ln1_g=ln1_g[l], ln1_b=ln1_b[l], peer_wq=peer_wq[l], peer_subkeys=peer_subkeys[l],
                  peer_u=peer_u[l], peer_v=peer_v[l], ln2_g=ln2_g[l], ln2_b=ln2_b[l])
        B = hp.shape[0]
        hp, (a1, a2, a3, a4) = decoder_layer(
            hp, jnp.zeros((B, RW_COLS), hp.dtype),
            jnp.zeros((B, RW_HEADS, RW_HEAD_DIM, RW_HEAD_DIM), F32),
            jnp.zeros((B, GD_CONV - 1, GD_QKV), hp.dtype),
            jnp.zeros((B, GD_HEADS, GD_HEAD_DIM, GD_HEAD_DIM), F32), lp, True)
        hs, (b1, b2, b3, b4) = decoder_layer(
            hs, state_rwkv_shift[l], state_rwkv_wkv[l], state_gdn_conv[l], state_gdn_ssm[l],
            lp, False)
        p_shift.append(a1.astype(state_rwkv_shift.dtype))
        p_wkv.append(a2.astype(state_rwkv_wkv.dtype))
        p_conv.append(a3.astype(state_gdn_conv.dtype))
        p_ssm.append(a4.astype(state_gdn_ssm.dtype))
        s_shift.append(b1.astype(state_rwkv_shift.dtype))
        s_wkv.append(b2.astype(state_rwkv_wkv.dtype))
        s_conv.append(b3.astype(state_gdn_conv.dtype))
        s_ssm.append(b4.astype(state_gdn_ssm.dtype))
    return (hp, hs, jnp.stack(p_shift), jnp.stack(p_wkv), jnp.stack(p_conv), jnp.stack(p_ssm),
            jnp.stack(s_shift), jnp.stack(s_wkv), jnp.stack(s_conv), jnp.stack(s_ssm))


_drawn_inputs = setup_inputs


def setup_inputs(seed=0):
    import zlib

    import numpy as np

    out = dict(_drawn_inputs(seed))
    spreads = {}
    factors = {'rwkv_ln_w': 4.992, 'rwkv_ln_b': 5.004, 'gdn_norm_w': 3.52, 'ln2_g': 2.832, 'ln2_b': 2.743}
    for name, (base, spread) in spreads.items():
        noise = np.random.default_rng([zlib.crc32(name.encode()), seed]).standard_normal(out[name].shape)
        drawn = base * np.exp(spread * noise) if base else spread * noise
        out[name] = __import__('jax').numpy.asarray(drawn.astype(out[name].dtype))
    for name, factor in factors.items():
        out[name] = (out[name] * factor).astype(out[name].dtype)
    return out
```

```python
from contextlib import ExitStack

import numpy as np

import concourse.bass as bass
from concourse import mybir

ALU = mybir.AluOpType
ACT = mybir.ActivationFunctionType
AXX = mybir.AxisListType.X
F32 = mybir.dt.float32
BF16 = mybir.dt.bfloat16
U32 = mybir.dt.uint32

P = 128
D = 1024
KD = D // P
NP = 512
NS = 8
T = NP + NS
TH = T // 2
NT = NP // P
HR, CR = 8, 64
HG, CG = 4, 128
RW_COLS = 1792
RT_ = RW_COLS // P
QT = 12
ZT = 4
PT = RT_ + QT + ZT
GD_QKV = 1536
BA0 = PT * P
GATE0 = BA0 + 8
ALPHA = 2.0 ** 0.25
DECAY = float(np.exp(-0.5))
TAIL = 11
BG = 36

_C = {}


def _consts():
    cols = []

    def put(name, a):
        _C[name] = (sum(c.shape[1] for c in cols), a.shape[1])
        cols.append(a.astype(np.float32))

    i = np.arange(P)
    s, t = i[:, None], i[None, :]
    put("ident", np.eye(P))
    put("ones", np.ones((P, P)))
    put("blk64", (s // 64 == t // 64) * 1.0)
    for m in (1, 2, 4, 8, 16, 32, 64):
        put(f"lvl{m}", ((s // (2 * m) == t // (2 * m)) & (s // m % 2 == 0) & (t // m % 2 == 1)) * 1.0)
    one = np.ones((P, P))
    put("pair", np.concatenate([((s // 64 == t // 64) & (s < t)) * 1.0, ((s // 64 == t // 64) & (s <= t)) * 1.0], 1))
    put("incl", (s <= t) * 1.0)
    sel = np.zeros((P, 8, P))
    for h in range(4):
        sel[h, h] = 1.0
        sel[32 + h, 4 + h] = 1.0
    put("sel", sel.reshape(P, -1))
    put("keep64", np.broadcast_to((np.arange(NP) % 64 != 0) * 1.0, (P, NP)))
    put("keep128", np.broadcast_to((np.arange(NP) % 128 != 0) * 1.0, (P, NP)))
    put("sum4", (s % 32 == t % 32) * 1.0)
    put("iota16", np.broadcast_to(np.arange(16.0), (P, 16)))
    put("mod16", (s % 16) * 1.0)
    put("eps", np.broadcast_to(np.array([1e-12, 1e-6, 64e-5, 1e-5]), (P, 4)))
    return np.concatenate(cols, 1)


CONSTS = _consts()
EPS_KK, EPS_GD, EPS_GN, EPS_LN = range(4)

_PAR = {}
_n = 0
for _name, _rows in (("rwkv_mu", RT_), ("rwkv_w0", 4), ("rwkv_a0", 4), ("rwkv_k_k", 4), ("rwkv_k_a", 4),
                     ("rwkv_r_k", 4), ("rwkv_ln_w", 4), ("rwkv_ln_b", 4), ("gdn_conv_w", 4 * QT), ("gdn_norm_w", 1),
                     ("ln1_g", KD), ("ln1_b", KD)):
    _PAR[_name] = (_n, _rows)
    _n += _rows
NPAR = _n


class Steps:

    def __init__(self, eng, sem, start=0):
        self.eng, self.sem, self.n, self.base = eng, sem, start, 0

    def did(self, ins):
        ins.then_inc(self.sem, 1)
        self.n += 1

    def settled(self):
        self.eng.wait_ge(self.sem, self.base + self.n)

    def link(self, ins):
        self.did(ins)
        self.settled()


def program(nc, a):
    ctx = ExitStack()
    with ctx:
        def sb(name, shape, dt=F32):
            return ctx.enter_context(nc.sbuf_tensor(name, shape, dt))

        sems = {}

        def sem(name):
            if name not in sems:
                sems[name] = ctx.enter_context(nc.semaphore(name))
            return sems[name]

        ps = ctx.enter_context(nc.psum_tensor("ps", [P, 8, 512], F32))
        cst = sb("cst", [P, CONSTS.shape[1]])
        par = sb("par", [P, NPAR])
        xT = sb("xT", [P, KD, T])
        m = dict(nc=nc, a=a, sem=sem, ps=ps, cst=cst, par=par, xT=xT, saved=0)

        def phase(*steps):
            with ExitStack() as local:
                m["tmp"] = lambda name, shape, dt=F32: local.enter_context(nc.sbuf_tensor(name, shape, dt))
                for step in steps:
                    step(m)

        with ExitStack() as mixing:
            for name, shape in (("Praw", [P, PT, T]), ("mix", [P, RT_, T]), ("conv", [P, QT, T]), ("kk", [P, 4, T]),
                                ("scr", [P, 4, T]), ("bg", [BG, T]), ("gdpar", [BG, 4]), ("omka", [P, 4]),
                                ("Gend", [P, 4, NP // 64])):
                m[name] = mixing.enter_context(nc.sbuf_tensor(name, shape, F32))
            phase(load_inputs, project, tokenwise)
            phase(sample_rows)
            phase(recur)
            phase(sample_recur)
            phase(normalise)
            phase(merge)
        for name, shape, dt in (("x1row", [P, NT + 1, D], F32), ("idxT", [P, T], U32), ("gateT", [P, T], F32)):
            m[name] = sb(name, shape, dt)
        phase(norm1)
        phase(query, rows, select)
        phase(experts)
        phase(norm2)
    return m


def const(m, name):
    c0, n = _C[name]
    return m["cst"][:, c0:c0 + n]


def param(m, name, j=0):
    c = _PAR[name][0] + j
    return m["par"][:, c:c + 1]


def load_inputs(m):
    nc, a, tmp, sem, ps, cst, par, xT = (m[k] for k in ("nc", "a", "tmp", "sem", "ps", "cst", "par", "xT"))
    mix, conv, gdpar = m["mix"], m["conv"], m["gdpar"]
    m["shT"] = shT = tmp("shT", [P, RT_, NS])
    m["cbT"] = cbT = tmp("cbT", [P, QT, NS * 3])
    m["ring"] = ring = tmp("ring", [P, 3, KD, P])
    m["wba"] = wba = tmp("wba", [P, KD, BG])
    m["w2a2"] = w2a2 = tmp("w2a2", [P, 512])
    m["g2"] = g2 = tmp("g2", [P, 512])
    xrow = mix[:].rearrange("p a t -> p (a t)")[:, 0:4 * D].rearrange("p (n d) -> p n d", n=4)
    flat = conv[:].rearrange("p a t -> p (a t)")
    xsrow, shrow, cbrow = flat[0:NS, 0:D], flat[0:NS, D:D + RW_COLS], flat[0:24, 2816:2816 + GD_QKV]
    prow = flat[0:NPAR, 4352:4352 + P]
    x_in, small_in, w_in = sem("x_in"), sem("small_in"), [sem(f"weights{b}") for b in range(3)]
    ba_zero, turned, xT_ready = sem("ba_zero"), sem("turned"), sem("xT_ready")
    ident = const(m, "ident")
    n_small = 0
    with nc.Block() as block:
        @block.sync
        def _(sp):
            sp.dma_start(cst[:], a["consts"]).then_inc(sem("cst_in"), 16)
            for n in range(NT):
                sp.dma_start(xrow[:, n, :], a["x_prompt"][0, n * P:(n + 1) * P, :]).then_inc(x_in, 16)
            for b in range(3):
                sp.dma_start(ring[:, b], a["w_in"][0, :, b * P:(b + 1) * P].rearrange("(k p) c -> p k c", p=P)
                             ).then_inc(w_in[b], 16)

        @block.scalar
        def _(act):
            nonlocal n_small
            act.dma_start(xsrow, a["x_sample"].rearrange("b o d -> (b o) d")).then_inc(small_in, 16)
            act.dma_start(shrow, a["state_rwkv_shift"][0]).then_inc(small_in, 16)
            act.dma_start(cbrow, a["state_gdn_conv"][0].rearrange("b j c -> (b j) c")).then_inc(small_in, 16)
            n_small = 3
            for name, (r0, n) in _PAR.items():
                src = a[name][0]
                if name in ("rwkv_r_k", "gdn_conv_w"):
                    src = src.rearrange("a b -> (a b)")
                act.dma_start(prow[r0:r0 + n, :], src.rearrange("(n c) -> n c", c=P)).then_inc(small_in, 16)
                n_small += 1
            act.dma_start(w2a2[0:64, :], a["rwkv_w2"][0]).then_inc(small_in, 16)
            act.dma_start(w2a2[64:128, :], a["rwkv_a2"][0]).then_inc(small_in, 16)
            act.dma_start(g2[:], a["rwkv_g2"][0]).then_inc(small_in, 16)
            act.dma_start(gdpar[32:36, 0:1], a["gdn_a_log"].rearrange("o h -> h o")).then_inc(small_in, 16)
            act.dma_start(gdpar[32:36, 1:2], a["gdn_dt_bias"].rearrange("o h -> h o")).then_inc(small_in, 16)
            act.wait_ge(ba_zero, 1)
            ba = a["w_in"][0, :, BA0:BA0 + 8].rearrange("(k p) c -> p k c", p=P)
            act.dma_start(wba[:, :, 0:4], ba[:, :, 0:4]).then_inc(small_in, 16)
            act.dma_start(wba[:, :, 32:36], ba[:, :, 4:8]).then_inc(small_in, 16)
            n_small += 7
            for n in range(NT):
                act.wait_ge(turned, n + 1)
                act.activation(xT[:, :, n * P:(n + 1) * P], ps[:, 2 * n:2 * n + 2, :].rearrange("p b (k t) -> p (b k) t", t=P),
                               ACT.Copy).then_inc(xT_ready, 1)

        @block.gpsimd
        def _(pool):
            nc.gpsimd.memset(wba[:], 0.0).then_inc(ba_zero, 1)

        @block.tensor
        def _(pe):
            pe.wait_ge(sem("cst_in"), 16)
            pe.wait_ge(x_in, 16 * NT)
            for n in range(NT):
                for k in range(KD):
                    mm = pe.transpose(ps[:, 2 * n + k // 4, (k % 4) * P:(k % 4 + 1) * P], xrow[:, n, k * P:(k + 1) * P], ident)
                mm.then_inc(turned, 1)
            pe.wait_ge(small_in, 16 * n_small)
            pe.wait_ge(xT_ready, 1)
            for k in range(KD):
                pe.transpose(ps[:, 0, k * NS:(k + 1) * NS], xsrow[:, k * P:(k + 1) * P], ident[0:NS, 0:NS])
            pe.transpose(ps[:, 0, 64:64 + NPAR], prow, ident[0:NPAR, 0:NPAR])
            for j in range(RT_):
                pe.transpose(ps[:, 0, 192 + j * NS:192 + (j + 1) * NS], shrow[:, j * P:(j + 1) * P], ident[0:NS, 0:NS])
            for j in range(QT):
                mm = pe.transpose(ps[:, 1, j * 24:(j + 1) * 24], cbrow[:, j * P:(j + 1) * P], ident[0:24, 0:24])
            mm.then_inc(turned, 1)

        @block.vector
        def _(dve):
            dve.wait_ge(turned, NT + 1)
            done = sem("small_ready")
            dve.tensor_copy(xT[:, :, NP:T], ps[:, 0, 0:64].rearrange("p (k t) -> p k t", t=NS)).then_inc(done, 1)
            dve.tensor_copy(par[:], ps[:, 0, 64:64 + NPAR]).then_inc(done, 1)
            dve.tensor_copy(shT[:], ps[:, 0, 192:192 + RT_ * NS].rearrange("p (k t) -> p k t", t=NS)).then_inc(done, 1)
            dve.tensor_copy(cbT[:], ps[:, 1, 0:24 * QT].rearrange("p (k t) -> p k t", t=24)).then_inc(done, 1)


def half(ap):
    return ap.rearrange("p (h t) -> p h t", h=2)


def project(m):
    nc, a, tmp, sem, ps, par, xT = (m[k] for k in ("nc", "a", "tmp", "sem", "ps", "par", "xT"))
    Praw, mix, conv, kk, scr, shT, cbT, ring, wba, gdpar = (
        m[k] for k in ("Praw", "mix", "conv", "kk", "scr", "shT", "cbT", "ring", "wba", "gdpar"))
    w_in = [sem(f"weights{b}") for b in range(3)]
    tile_done = sem("tile_done")
    tile_out = sem("tile_out")
    ba_done, ba_out, bg_zero, mixed, low_in, conv_ready, silu_ready = (sem(n) for n in (
        "ba_done", "ba_out", "bg_zero", "mixed", "low_in", "conv_ready", "silu_ready"))
    ITS, PER = PT // 6, 6
    m["weights"] = [16 * PT // 3] * 3 + [0]
    bg, omka = m["bg"], m["omka"]
    m["spx"] = tmp("spx", [BG, T])
    m["tail"] = tail = tmp("tail", [P, RT_ + QT, TAIL])
    m["lrk"] = lrk = tmp("lrk", [P, 2, T])
    m["sq"] = sq = Praw[:, 18:26]

    with nc.Block() as block:
        @block.sync
        def _(sp):
            with sp.Fori(0, ITS - 1) as it:
                for t in range(PER):
                    sp.wait_ge(tile_done, it * PER + (t + 1))
                    sp.dma_start(ring[:, t % 3], a["w_in"][0, :, bass.ds(it * (PER * P) + (t + 3) * P, P)]
                                 .rearrange("(k p) c -> p k c", p=P)).then_inc(w_in[t % 3], 16)
            for t in range(PER - 3):
                n = (ITS - 1) * PER + t
                sp.wait_ge(tile_done, n + 1)
                sp.dma_start(ring[:, t % 3], a["w_in"][0, :, (n + 3) * P:(n + 4) * P]
                             .rearrange("(k p) c -> p k c", p=P)).then_inc(w_in[t % 3], 16)

        @block.tensor
        def _(pe):
            with pe.Fori(0, ITS) as it:
                for t in range(PER):
                    pe.wait_ge(w_in[t % 3], it * 32 + 16 * (t // 3 + 1))
                    pe.wait_ge(tile_out, it * PER + (t + 1))
                    for h in range(2):
                        for k in range(KD):
                            mm = pe.matmul(ps[:, 2 * (t % 2) + h, 0:TH], ring[:, t % 3, k, :], xT[:, k, h * TH:(h + 1) * TH],
                                           start=(k == 0), stop=(k == KD - 1))
                    mm.then_inc(tile_done, 1)
            for h in range(2):
                for k in range(KD):
                    mm = pe.matmul(ps[0:BG, 4 + h, 0:TH], wba[:, k, :], xT[:, k, h * TH:(h + 1) * TH],
                                   start=(k == 0), stop=(k == KD - 1))
            mm.then_inc(ba_done, 1)

        @block.scalar
        def _(act):
            act.sem_inc(tile_out, 2)
            with act.Fori(0, ITS) as it:
                for t in range(PER):
                    act.wait_ge(tile_done, it * PER + (t + 1))
                    act.activation(Praw[:, bass.ds(it * PER + t, 1), :].rearrange("p o (h t) -> p (o h) t", h=2),
                                   ps[:, 2 * (t % 2):2 * (t % 2) + 2, 0:TH], ACT.Copy).then_inc(tile_out, 1)
            act.wait_ge(mixed, 1)
            act.activation(lrk[0:64, 0], mix[0:64, 12], ACT.Tanh).then_inc(low_in, 1)
            act.activation(lrk[64:128, 0], mix[64:128, 12], ACT.Copy).then_inc(low_in, 1)
            act.activation(lrk[:, 1], mix[:, 13], ACT.Sigmoid).then_inc(low_in, 1)
            act.wait_ge(ba_done, 1)
            act.wait_ge(bg_zero, 1)
            act.activation(half(bg[0:4, :]), ps[0:4, 4:6, 0:TH], ACT.Sigmoid).then_inc(ba_out, 1)
            act.activation(half(bg[32:36, :]), ps[32:36, 4:6, 0:TH], ACT.Identity, bias=gdpar[32:36, 1:2]).then_inc(ba_out, 1)
            act.wait_ge(conv_ready, 1)
            for n in range(3):
                act.activation(conv[:, 4 * n:4 * n + 4, :], conv[:, 4 * n:4 * n + 4, :], ACT.Silu).then_inc(silu_ready, 1)

        @block.gpsimd
        def _(pool):
            nc.gpsimd.memset(bg[:], 0.0).then_inc(bg_zero, 1)

        @block.vector
        def _(dve):
            st = Steps(dve, sem("dve_step"))
            dve.wait_ge(tile_out, 2 + RT_)
            st.did(dve.tensor_tensor(mix[:, :, 1:NP], Praw[:, 0:RT_, 0:NP - 1], Praw[:, 0:RT_, 1:NP], ALU.subtract))
            st.did(dve.tensor_scalar(mix[:, :, 0:1], Praw[:, 0:RT_, 0:1], -1.0, None, ALU.mult))
            st.did(dve.tensor_tensor(mix[:, :, NP:T], shT[:], Praw[:, 0:RT_, NP:T], ALU.subtract))
            c0 = _PAR["rwkv_k_a"][0]
            st.did(dve.tensor_scalar(omka[:], par[:, c0:c0 + 4], -1.0, 1.0, ALU.mult, ALU.add))
            st.settled()
            for j in range(RT_):
                st.did(dve.scalar_tensor_tensor(out=mix[:, j], in0=mix[:, j], scalar=param(m, "rwkv_mu", j), in1=Praw[:, j],
                                                op0=ALU.mult, op1=ALU.add))
            st.settled()
            dve.sem_inc(mixed, 1)
            for j in range(4):
                st.did(dve.tensor_scalar(kk[:, j], mix[:, 4 + j], param(m, "rwkv_k_k", j), None, ALU.mult))
            st.settled()
            st.did(dve.tensor_tensor(scr[:], kk[:], kk[:], ALU.mult))
            for j in range(QT):
                r = Praw[:, RT_ + j]
                dve.wait_ge(tile_out, 2 + RT_ + j + 1)
                st.link(dve.tensor_scalar(conv[:, j, :], r, param(m, "gdn_conv_w", 3 * QT + j), None, ALU.mult))
                for back in (1, 2, 3):
                    tap = 3 - back
                    w = param(m, "gdn_conv_w", tap * QT + j)
                    st.did(dve.scalar_tensor_tensor(out=conv[:, j, back:NP], in0=r[:, 0:NP - back], scalar=w,
                                                    in1=conv[:, j, back:NP], op0=ALU.mult, op1=ALU.add))
                    st.link(dve.scalar_tensor_tensor(out=conv[:, j, NP:T], in0=cbT[:, j, tap:24:3], scalar=w,
                                                     in1=conv[:, j, NP:T], op0=ALU.mult, op1=ALU.add))
            dve.sem_inc(conv_ready, 1)
            st.did(dve.tensor_copy(tail[:], Praw[:, 0:RT_ + QT, NP - 3:T]))
            st.settled()
            for n in range(2):
                dve.wait_ge(silu_ready, n + 1)
                st.did(dve.tensor_tensor(sq[:, 4 * n:4 * n + 4], conv[:, 4 * n:4 * n + 4], conv[:, 4 * n:4 * n + 4], ALU.mult))
            st.settled()
            m["dve"] = st.n


def tokenwise(m):
    nc, a, sem, ps, par = (m[k] for k in ("nc", "a", "sem", "ps", "par"))
    Praw, mix, conv, kk, scr, w2a2, g2, gdpar, bg, spx, tail, omka, lrk, sq = (m[k] for k in (
        "Praw", "mix", "conv", "kk", "scr", "w2a2", "g2", "gdpar", "bg", "spx", "tail", "omka", "lrk", "sq"))
    ones, blk64, ident, eps = (const(m, n) for n in ("ones", "blk64", "ident", "eps"))
    m["sw"], m["aa"], m["gg"] = sw, aa, gg = Praw[:, 0:4], Praw[:, 4:8], Praw[:, 8:12]
    m["G"], m["Gi"], m["Gp"] = G, Gi, Gp = Praw[:, 14:18], Praw[:, 18:22], Praw[:, 22:26]
    Gend = m["Gend"]
    tailrow = m["tmp"]("tailrow", [TAIL, RW_COLS + GD_QKV])
    norm_mm, root, low_mm, low_out, tail_mm, tail_out, spl_in, spl, cum_ready, exps, bon_in, bon_mm, bon_out, out = (
        sem(n) for n in ("norm_mm", "root", "low_mm", "low_out", "tail_mm", "tail_out", "spl_in", "spl", "cum_ready",
                         "exps", "bon_in", "bon_mm", "bon_out", "saved"))
    bank2 = lambda b: ps[:, b:b + 2, 0:TH]
    TAILS = ((0, 8), (8, 16), (16, 24), (24, 26))

    with nc.Block() as block:
        @block.sync
        def _(sp):
            sp.dma_start(a["s_conv"][0, :, 0:2, :], a["state_gdn_conv"][0, :, 1:3, :]).then_inc(out, 16)
            sp.wait_ge(tail_out, 4)
            sp.dma_start(a["p_shift"][0], tailrow[2:3, 0:RW_COLS]).then_inc(out, 16)
            sp.dma_start(a["s_shift"][0], tailrow[3:11, 0:RW_COLS]).then_inc(out, 16)
            sp.dma_start(a["p_conv"][0, 0], tailrow[0:3, RW_COLS:]).then_inc(out, 16)
            sp.dma_start(a["s_conv"][0, :, 2, :], tailrow[3:11, RW_COLS:]).then_inc(out, 16)
            sp.wait_ge(out, m["saved"] + 16 * 5)
            m["saved"] += 16 * 5

        @block.tensor
        def _(pe):
            for n in range(12):
                if n >= 2:
                    pe.wait_ge(root, n - 1)
                w, x = (blk64, scr[:, n]) if n < 4 else (ones, sq[:, n - 4])
                for h in range(2):
                    mm = pe.matmul(ps[:, 2 * (n % 2) + h, 0:TH], w, x[:, h * TH:(h + 1) * TH], start=True, stop=True)
                mm.then_inc(norm_mm, 1)
            for n in range(12):
                j, kind = n // 3, n % 3
                if n >= 2:
                    pe.wait_ge(low_out, n - 1)
                w = (w2a2[0:64], w2a2[64:128], g2[:])[kind]
                r = (lrk[0:64, 0], lrk[64:128, 0], lrk[:, 1])[kind]
                for h in range(2):
                    mm = pe.matmul(ps[:, 4 + 2 * (n % 2) + h, 0:TH], w[:, j * P:(j + 1) * P], r[:, h * TH:(h + 1) * TH],
                                   start=True, stop=True)
                mm.then_inc(low_mm, 1)
            pe.wait_ge(root, 12)
            for n, (j0, j1) in enumerate(TAILS):
                if n >= 2:
                    pe.wait_ge(tail_out, n - 1)
                for j in range(j0, j1):
                    mm = pe.transpose(ps[0:TAIL, 2 * (n % 2) + (j - j0) // 4, (j % 4) * P:(j % 4 + 1) * P], tail[:, j, :], ident)
                mm.then_inc(tail_mm, 1)
            pe.wait_ge(bon_in, 1)
            pe.wait_ge(low_out, 12)
            for n in range(4):
                if n >= 2:
                    pe.wait_ge(bon_out, n - 1)
                for h in range(2):
                    mm = pe.matmul(ps[:, 4 + 2 * (n % 2) + h, 0:TH], blk64, scr[:, n, h * TH:(h + 1) * TH], start=True, stop=True)
                mm.then_inc(bon_mm, 1)

        @block.scalar
        def _(act):
            for n in range(12):
                act.wait_ge(norm_mm, n + 1)
                d, e = (scr[:, n], EPS_KK) if n < 4 else (sq[:, n - 4], EPS_GD)
                act.activation(half(d), bank2(2 * (n % 2)), ACT.Sqrt, bias=eps[:, e:e + 1]).then_inc(root, 1)
            for n in range(12):
                j, kind = n // 3, n % 3
                act.wait_ge(low_mm, n + 1)
                dst = half((sw, aa, gg)[kind][:, j, :])
                if kind < 2:
                    ins = act.activation(dst, bank2(4 + 2 * (n % 2)), ACT.Sigmoid, bias=param(m, ("rwkv_w0", "rwkv_a0")[kind], j))
                else:
                    ins = act.activation(dst, bank2(4 + 2 * (n % 2)), ACT.Copy)
                ins.then_inc(low_out, 1)
            act.wait_ge(cum_ready, 1)
            act.activation(Gi[:, :, 0:NP], G[:, :, 0:NP], ACT.Exp, scale=DECAY).then_inc(exps, 1)
            act.wait_ge(exps, 1)
            act.activation(G[:, :, 0:NP], G[:, :, 0:NP], ACT.Exp, scale=-DECAY).then_inc(exps, 1)
            act.activation(Gp[:, :, 0:NP], Gp[:, :, 0:NP], ACT.Exp, scale=-DECAY).then_inc(exps, 1)
            act.activation(G[:, :, NP:T], sw[:, :, NP:T], ACT.Exp, scale=-DECAY).then_inc(exps, 1)
            act.wait_ge(spl_in, 1)
            act.activation(spx[32:36, :], spx[32:36, :], ACT.Exp, scale=-1.0).then_inc(spl, 1)
            act.activation(gdpar[32:36, 2:3], gdpar[32:36, 0:1], ACT.Exp).then_inc(spl, 1)
            act.wait_ge(spl, 2)
            act.activation(spx[32:36, :], spx[32:36, :], ACT.Ln, bias=1.0).then_inc(spl, 1)

        @block.vector
        def _(dve):
            st = Steps(dve, sem("dve_step"), m["dve"])
            st.link(dve.tensor_scalar(spx[32:36, :], bg[32:36, :], -1.0, None, ALU.mult))
            st.did(dve.tensor_tensor(spx[32:36, :], spx[32:36, :], bg[32:36, :], ALU.max))
            st.settled()
            st.link(dve.tensor_scalar(bg[32:36, :], bg[32:36, :], 0.0, None, ALU.max))
            dve.sem_inc(spl_in, 1)
            dve.wait_ge(root, 4)
            st.link(dve.reciprocal(scr[:], scr[:]))
            st.link(dve.tensor_tensor(kk[:], kk[:], scr[:], ALU.mult))
            dve.wait_ge(root, 12)
            st.link(dve.reciprocal(sq[:], sq[:]))
            st.did(dve.tensor_tensor(conv[:, 4:8], conv[:, 4:8], sq[:, 4:8], ALU.mult))
            st.did(dve.scalar_tensor_tensor(out=conv[:, 0:4], in0=conv[:, 0:4], scalar=CG ** -0.5, in1=sq[:, 0:4],
                                            op0=ALU.mult, op1=ALU.mult))
            st.settled()
            dve.wait_ge(low_out, 12)
            for j in range(4):
                st.did(dve.tensor_tensor_scan(G[:, j, 0:NP], const(m, "keep64"), sw[:, j, 0:NP], 0.0, ALU.mult, ALU.add))
            st.settled()
            dve.tensor_tensor(Gp[:, :, 0:NP], G[:, :, 0:NP], sw[:, :, 0:NP], ALU.subtract).then_inc(cum_ready, 1)
            for j in range(4):
                st.did(dve.tensor_scalar(scr[:, j], aa[:, j], param(m, "rwkv_k_a", j), omka[:, j:j + 1], ALU.mult, ALU.add))
            st.settled()
            k2 = mix[:, 4:8]
            st.did(dve.tensor_tensor(k2, k2, scr[:], ALU.mult))
            st.did(dve.tensor_tensor(aa, aa, kk[:], ALU.mult))
            st.settled()
            for j in range(4):
                st.did(dve.scalar_tensor_tensor(out=scr[:, j], in0=mix[:, j], scalar=param(m, "rwkv_r_k", j), in1=k2[:, j],
                                                op0=ALU.mult, op1=ALU.mult))
            st.settled()
            dve.sem_inc(bon_in, 1)
            for n, (j0, j1) in enumerate(TAILS):
                dve.wait_ge(tail_mm, n + 1)
                b = 2 * (n % 2)
                if n < 3:
                    ins = dve.tensor_copy(tailrow[:, j0 * P:j1 * P].rearrange("p (b c) -> p b c", b=2), ps[0:TAIL, b:b + 2, :])
                else:
                    ins = dve.tensor_copy(tailrow[:, j0 * P:j1 * P], ps[0:TAIL, b, 0:2 * P])
                ins.then_inc(tail_out, 1)
            dve.wait_ge(exps, 4)
            st.did(dve.scalar_tensor_tensor(out=Gp[:, :, 0:NP], in0=Gp[:, :, 0:NP], scalar=-1.0, in1=kk[:, :, 0:NP],
                                            op0=ALU.mult, op1=ALU.mult))
            st.did(dve.tensor_tensor(aa[:, :, 0:NP], aa[:, :, 0:NP], Gi[:, :, 0:NP], ALU.mult))
            st.did(dve.tensor_tensor(k2[:, :, 0:NP], k2[:, :, 0:NP], Gi[:, :, 0:NP], ALU.mult))
            st.did(dve.tensor_tensor(mix[:, 0:4, 0:NP], mix[:, 0:4, 0:NP], G[:, :, 0:NP], ALU.mult))
            st.did(dve.tensor_copy(Gend[:], G[:, :, 63:NP:64]))
            for n in range(4):
                dve.wait_ge(bon_mm, n + 1)
                dve.tensor_tensor(half(scr[:, n]), bank2(4 + 2 * (n % 2)), half(mix[:, 8 + n]), ALU.mult).then_inc(bon_out, 1)
            dve.wait_ge(spl, 3)
            st.link(dve.tensor_tensor(bg[32:36, :], bg[32:36, :], spx[32:36, :], ALU.add))
            st.link(dve.tensor_scalar(spx[32:36, :], bg[32:36, :], gdpar[32:36, 2:3], -1.0, ALU.mult, ALU.mult))
            st.did(dve.tensor_tensor_scan(bg[32:36, 0:NP], const(m, "keep128")[32:36], spx[32:36, 0:NP], 0.0, ALU.mult, ALU.add))
            st.did(dve.tensor_copy(bg[32:36, NP:T], spx[32:36, NP:T]))
            st.settled()
            m["dve"] = st.n


def sample_rows(m):
    nc, a, sem, ps, tmp = (m[k] for k in ("nc", "a", "sem", "ps", "tmp"))
    mix, conv, kk, bg, G, aa = (m[k] for k in ("mix", "conv", "kk", "bg", "G", "aa"))
    ident = const(m, "ident")
    RWROW, GDROW = 6 * 512, GD_QKV + BG
    srow = tmp("srow", [NS, RWROW + GDROW])
    tiles = [src[:, j, NP:T] for src in (mix[:, 0:4], G, mix[:, 4:8], mix[:, 8:12], kk, aa) for j in range(4)]
    tiles += [conv[:, j, NP:T] for j in range(QT)]
    rows_mm, rows_out, rows_saved = sem("rows_mm"), sem("rows_out"), sem("saved")
    rounds = [(c, min(c + 2 * 512, RWROW + GD_QKV)) for c in range(0, RWROW + GD_QKV, 2 * 512)]
    m["RWROW"] = RWROW

    with nc.Block() as block:
        @block.tensor
        def _(pe):
            for n, (c0, c1) in enumerate(rounds):
                if n >= 4:
                    pe.wait_ge(rows_out, n - 3)
                for c in range(c0, c1, P):
                    mm = pe.transpose(ps[0:NS, 2 * (n % 4) + (c - c0) // 512, (c - c0) % 512:(c - c0) % 512 + P],
                                      tiles[c // P], ident)
                mm.then_inc(rows_mm, 1)
            pe.wait_ge(rows_out, len(rounds))
            pe.transpose(ps[0:NS, 0, 0:BG], bg[:, NP:T], ident[0:BG, 0:BG]).then_inc(rows_mm, 1)

        @block.vector
        def _(dve):
            for n, (c0, c1) in enumerate(rounds):
                dve.wait_ge(rows_mm, n + 1)
                for h in range((c1 - c0) // 512):
                    ins = dve.tensor_copy(srow[:, c0 + 512 * h:c0 + 512 * (h + 1)], ps[0:NS, 2 * (n % 4) + h, :])
                ins.then_inc(rows_out, 1)
            dve.wait_ge(rows_mm, len(rounds) + 1)
            dve.tensor_copy(srow[:, RWROW + GD_QKV:], ps[0:NS, 0, 0:BG]).then_inc(rows_out, 1)

        @block.sync
        def _(sp):
            sp.wait_ge(rows_out, len(rounds) + 1)
            sp.dma_start(a["rows_rw"].rearrange("q (b h) c -> b q (h c)", b=NS),
                         srow[:, 0:RWROW].rearrange("b (q c) -> b q c", q=6)).then_inc(rows_saved, 16)
            sp.dma_start(a["rows_gd"].rearrange("q (b h) c -> b q (h c)", b=NS),
                         srow[:, RWROW:RWROW + GD_QKV].rearrange("b (q c) -> b q c", q=3)).then_inc(rows_saved, 16)
            for n, c in enumerate((0, 32)):
                sp.dma_start(a["rows_bg"][n].rearrange("(b h) -> b h", b=NS),
                             srow[:, RWROW + GD_QKV + c:RWROW + GD_QKV + c + HG]).then_inc(rows_saved, 16)
            sp.wait_ge(rows_saved, m["saved"] + 64)
            m["saved"] += 64


def recur(m):
    nc, a, sem, ps, tmp = (m[k] for k in ("nc", "a", "sem", "ps", "tmp"))
    Praw, mix, conv, kk, bg, Gend = (m[k] for k in ("Praw", "mix", "conv", "kk", "bg", "Gend"))
    ident, pair, incl, sel = (const(m, n) for n in ("ident", "pair", "incl", "sel"))
    selv = sel.rearrange("p (h c) -> p h c", c=P)
    over4 = lambda ap: ap.unsqueeze(1).to_broadcast([P, 4, ap.shape[1]])
    flat = lambda ap, n: ap.rearrange("p a t -> p (a t)")[:, 0:n]
    AT, BT, KT, RT, VT = m["Gp"], m["aa"], mix[:, 4:8], mix[:, 0:4], mix[:, 8:12]
    oTr, oTg = m["oTr"], m["oTg"] = m["Gp"], conv[:, 0:4]
    AR = flat(Praw[:, 12:14], 1024).rearrange("p (j k t) -> p j k t", j=4, k=2)
    BK = flat(mix[:, 12:14], 1024).rearrange("p (j k t) -> p j k t", j=4, k=2)
    TTm = flat(m["sw"], 1536).rearrange("p (g h t) -> p g h t", g=3, h=4)
    TM = flat(m["Gi"], 1536).rearrange("p (g h t) -> p g h t", g=3, h=4)
    X = flat(m["G"], 1536).rearrange("p (g h t) -> p g h t", g=3, h=4)
    LM = flat(kk[:], 1536).rearrange("p (g h t) -> p g h t", g=3, h=4)
    VS, QKV, bgS = tmp("VS", [P, 4, P]), tmp("QKV", [P, QT, P]), tmp("bgS", [BG, P])
    Vt, Kt, Bt = tmp("Vt", [P, 512]), tmp("Kt", [P, 512]), tmp("Bt", [P, 512])
    rest = lambda ap: ap.rearrange("p a t -> p (a t)")[:, 1536:2048].rearrange("p (h t) -> p h t", h=4)
    gvt, gkd, kE, LG = rest(m["sw"]), rest(m["Gi"]), rest(m["G"]), rest(kk[:])
    bgt, E, qE = tmp("bgt", [P, BG]), tmp("E", [P, 4, P]), tmp("qE", [P, 4, P])
    dc, eC = tmp("dc", [P, 4]), tmp("eC", [P, 4])
    PR = tmp("PR", [P, HR, 4, P])
    W, U, gW, gU = tmp("W", [P, 512]), VS[:].rearrange("p j t -> p (j t)"), QKV[:, 8:12], QKV[:, 0:4]
    ST, S = tmp("ST", [P, 2, 4, 64]), tmp("S", [P, 4, P])
    wkv = W[0:64].rearrange("p (j k) -> p j k", j=4)
    LT = [PR[:, 0:4, 0], PR[:, 4:8, 0], LG]
    LEVELS = (2, 4, 8, 16, 32, 64)
    order = [(l, g) for l in range(6) for g in range(3) if l < 5 or g == 2]
    idx = {lg: n for n, lg in enumerate(order)}
    last = {0: 4, 1: 4, 2: 5}
    NL = len(order)
    K = dict(st_a=3, st_p=4, turn=3, tok=3, e_in=2, e_out=3, gv=1, pairs=3, pr=2, lg=1, intra=1, tt0=3, t_mm=3, t0=3,
             lm=NL, x_mm=NL, x_ev=NL, xt_mm=NL, upd=NL, wv_mm=1, wv=1, as_mm=2, w_ok=2, u_mm=2, u_ok=2, s_mm=2, s_ok=2,
             ost_mm=2, ost=4, ouv_mm=2, o_ok=2, gw_mm=1, gw=1, gu_mm=1, gu=1, go_mm=1, go=1, gs_mm=1, gs=1,
             bgt_ok=1, gkd_ok=1, qe=1, ke=1, ec=1)
    S_ = {n: sem("r_" + n) for n in K}

    def wait(eng, it, name, n):
        eng.wait_ge(S_[name], it * K[name] + n)

    def wait_ahead(eng, it, *signals):
        values = [eng.to_reg(it * K[name] + n) for name, n in signals]
        eng.wait_ge(sem("cst_in"), 16)
        for (name, _), value in zip(signals, values):
            eng.wait_ge(S_[name], value)

    tcols = lambda it: bass.ds(it * P, P)

    with nc.Block() as block:
        @block.scalar
        def _(act):
            cp = lambda o, i: act.activation(o, i, ACT.Copy)
            with act.Fori(0, NT) as it:
                wait_ahead(act, it, ("ouv_mm", 0))
                cp(AR[:, :, 0], AT[:, :, tcols(it)]).then_inc(S_["st_a"], 1)
                cp(AR[:, :, 1], RT[:, :, tcols(it)]).then_inc(S_["st_a"], 1)
                cp(VS[:], VT[:, :, tcols(it)]).then_inc(S_["st_a"], 1)
                wait(act, it, "turn", 1)
                for n, o in enumerate((Vt, Kt, Bt)):
                    cp(o[:], ps[:, n, :]).then_inc(S_["tok"], 1)
                wait(act, it, "e_in", 2)
                act.activation(kE, ps[:, 7, :].rearrange("p (h t) -> p h t", h=4), ACT.Exp).then_inc(S_["e_out"], 1)
                act.activation(E[:], E[:], ACT.Exp).then_inc(S_["e_out"], 1)
                act.activation(dc[:], dc[:], ACT.Exp).then_inc(S_["e_out"], 1)
                for g in range(3):
                    wait(act, it, "t_mm", g + 1)
                    cp(TM[:, g], ps[:, 3 + g, :].rearrange("p (h t) -> p h t", h=4)).then_inc(S_["t0"], 1)

                def x_evac(n):
                    g = order[n][1]
                    wait(act, it, "x_mm", n + 1)
                    cp(X[:, g], ps[:, g, :].rearrange("p (h t) -> p h t", h=4)).then_inc(S_["x_ev"], 1)

                for n in range(NL):
                    x_evac(n)
                wait(act, it, "wv_mm", 1)
                cp(W[:], ps[:, 0, :]).then_inc(S_["wv"], 1)

                def u_evac(c):
                    wait(act, it, "u_mm", c + 1)
                    cp(U[64 * c:64 * c + 64, :], ps[64 * c:64 * c + 64, 2, :]).then_inc(S_["u_ok"], 1)

                def o_evac(c):
                    wait_ahead(act, it, ("ost_mm", c + 1))
                    for par, b in ((0, 1), (1, 5)):
                        r = slice(64 * par, 64 * par + 64)
                        cp(oTr[r, :, bass.ds(it * P + 64 * c, 64)], ps[r, b, 256:512].rearrange("p (j t) -> p j t", j=4)
                           ).then_inc(S_["ost"], 1)

                u_evac(0)
                wait(act, it, "gu_mm", 1)
                cp(gU, ps[:, 7, :].rearrange("p (h t) -> p h t", h=4)).then_inc(S_["gu"], 1)
                o_evac(0)
                wait_ahead(act, it, ("go_mm", 1))
                cp(oTg[:, :, tcols(it)], ps[:, 6, :].rearrange("p (h t) -> p h t", h=4)).then_inc(S_["go"], 1)
                u_evac(1)
                o_evac(1)

        @block.gpsimd
        def _(pool):
            cp = nc.gpsimd.tensor_copy
            nc.gpsimd.memset(ST[:], 0.0).then_inc(sem("r_zero"), 1)
            nc.gpsimd.memset(S[:], 0.0).then_inc(sem("r_zero"), 1)
            with pool.Fori(0, NT) as it:
                wait(pool, it, "ouv_mm", 0)
                cp(BK[:, :, 0], BT[:, :, tcols(it)]).then_inc(S_["st_p"], 1)
                cp(BK[:, :, 1], KT[:, :, tcols(it)]).then_inc(S_["st_p"], 1)
                cp(QKV[:], conv[:, :, tcols(it)]).then_inc(S_["st_p"], 1)
                cp(bgS[:], bg[:, tcols(it)]).then_inc(S_["st_p"], 1)
                for n, (l, g) in enumerate(order):
                    if l == 0:
                        wait(pool, it, "tt0", g + 1)
                    else:
                        wait(pool, it, "x_mm", idx[l - 1, g] + 1)
                    nc.gpsimd.tensor_tensor(LM[:, g], LT[g], over4(const(m, f"lvl{LEVELS[l]}")), ALU.mult
                                            ).then_inc(S_["lm"], 1)

        @block.vector
        def _(dve):
            st = Steps(dve, sem("r_dve"))
            by4 = lambda b: ps[:, b, :].rearrange("p (h t) -> p h t", h=4)
            percol = lambda ap: ap.unsqueeze(2).to_broadcast([P, 4, P])
            KS = 10
            dve.wait_ge(sem("r_zero"), 2)
            with dve.Fori(0, NT) as it:
                st.n, st.base = 0, it * KS
                wait(dve, it, "turn", 2)
                dve.tensor_copy(bgt[:], ps[:, 5, 0:BG]).then_inc(S_["bgt_ok"], 1)
                wait(dve, it, "bgt_ok", 1)
                dve.tensor_tensor(gvt, by4(3), percol(bgt[:, 0:4]), ALU.mult).then_inc(S_["gv"], 1)
                wait(dve, it, "turn", 3)
                st.did(dve.tensor_tensor(E[:], by4(7), percol(bgt[:, 32:36]), ALU.subtract))
                dve.tensor_tensor(dc[:], by4(7)[:, :, P - 1], bgt[:, 32:36], ALU.subtract).then_inc(S_["e_in"], 1)
                st.settled()
                dve.tensor_scalar(E[:], E[:], 0.0, None, ALU.min).then_inc(S_["e_in"], 1)
                wait(dve, it, "e_out", 3)
                dve.tensor_tensor(gkd, by4(4), percol(dc[:]), ALU.mult).then_inc(S_["gkd_ok"], 1)
                dve.tensor_tensor(qE[:], QKV[:, 0:4], kE, ALU.mult).then_inc(S_["qe"], 1)
                dve.tensor_copy(eC[:], kE[:, :, P - 1]).then_inc(S_["ec"], 1)
                wait(dve, it, "qe", 1)
                wait(dve, it, "ec", 1)
                st.link(dve.scalar_tensor_tensor(out=kE, in0=kE, scalar=-1.0, in1=QKV[:, 4:8], op0=ALU.mult, op1=ALU.mult))
                dve.tensor_tensor(kE, kE, by4(6), ALU.mult).then_inc(S_["ke"], 1)
                wait(dve, it, "pairs", 1)
                mask = pair.unsqueeze(1).to_broadcast([P, 8, 2 * P])
                prv = lambda h0: PR[:, h0:h0 + 4].rearrange("p h (x k) t -> p (h x) (k t)", x=2)
                dve.tensor_tensor(prv(0), ps[:, 0:4, :].rearrange("p h (x c) -> p (h x) c", x=2), mask, ALU.mult
                                  ).then_inc(S_["pr"], 1)
                wait(dve, it, "pairs", 2)
                st.link(dve.scalar_tensor_tensor(out=LG, in0=by4(4), scalar=-1.0, in1=E[:], op0=ALU.mult, op1=ALU.mult))
                dve.tensor_tensor(LG, LG, by4(6), ALU.mult).then_inc(S_["lg"], 1)
                st.link(dve.tensor_tensor(E[:], E[:], over4(incl), ALU.mult))
                dve.tensor_tensor(E[:], E[:], by4(5), ALU.mult).then_inc(S_["intra"], 1)
                wait(dve, it, "pairs", 3)
                dve.tensor_tensor(prv(4), ps[:, 4:8, :].rearrange("p h (x c) -> p (h x) c", x=2), mask, ALU.mult
                                  ).then_inc(S_["pr"], 1)
                for g in range(3):
                    wait(dve, it, *(("pr", 1), ("pr", 2), ("lg", 1))[g])
                    st.link(dve.tensor_tensor(LM[:, g], LT[g], over4(const(m, "lvl1")), ALU.mult))
                    dve.tensor_tensor(TTm[:, g], LM[:, g], over4(ident), ALU.add).then_inc(S_["tt0"], 1)
                for n, (l, g) in enumerate(order):
                    wait(dve, it, "xt_mm", n + 1)
                    if l < last[g]:
                        dve.tensor_tensor(TM[:, g], TM[:, g], by4(3 + g), ALU.add)
                    dve.tensor_tensor(TTm[:, g], TTm[:, g], by4(g), ALU.add).then_inc(S_["upd"], 1)

                def w_add(c):
                    wait(dve, it, "as_mm", c + 1)
                    wait(dve, it, "wv", 1)
                    r = slice(64 * c, 64 * c + 64)
                    for par, b in ((0, 1), (1, 5)):
                        w = W[r].rearrange("p (j q v) -> p j q v", j=4, q=2)[:, :, par]
                        ins = dve.tensor_tensor(w, w, ps[r, b, 0:256].rearrange("p (j v) -> p j v", j=4), ALU.add)
                        if par:
                            ins.then_inc(S_["w_ok"], 1)
                        else:
                            ins.then_inc(sem("r_w_even"), 1)

                def state(c):
                    wait(dve, it, "s_mm", c + 1)
                    st.link(dve.tensor_tensor(ST[:, 1 - c], ST[:, c], ps[:, 3, 0:256].rearrange("p (j v) -> p j v", j=4), ALU.add))
                    ge = Gend[:, :, bass.ds(it * 2 + c, 1)].to_broadcast([P, 4, 64])
                    dve.tensor_tensor(ST[:, 1 - c], ST[:, 1 - c], ge, ALU.mult).then_inc(S_["s_ok"], 1)

                def o_add(c):
                    wait(dve, it, "ouv_mm", c + 1)
                    wait(dve, it, "ost", 2 * c + 2)
                    o = oTr[:, :, bass.ds(it * P + 64 * c, 64)]
                    dve.tensor_tensor(o, o, ps[:, 4, 0:256].rearrange("p (j t) -> p j t", j=4), ALU.add).then_inc(S_["o_ok"], 1)

                w_add(0)
                wait(dve, it, "gw_mm", 1)
                dve.tensor_tensor(gW, gvt, by4(6), ALU.add).then_inc(S_["gw"], 1)
                state(0)
                o_add(0)
                wait(dve, it, "gs_mm", 1)
                st.link(dve.tensor_tensor(S[:], S[:], percol(eC[:]), ALU.mult))
                dve.tensor_tensor(S[:], S[:], by4(7), ALU.add).then_inc(S_["gs"], 1)
                w_add(1)
                state(1)
                o_add(1)
                assert st.n == KS, st.n
            st.n, st.base = 0, 0
            dve.wait_ge(sem("wkv_mm"), 1)
            dve.tensor_copy(wkv, ps[0:64, 0, :].rearrange("p (j k) -> p j k", j=4)).then_inc(sem("wkv_ok"), 1)

        @block.tensor
        def _(pe):
            by4 = lambda b: ps[:, b, :].rearrange("p (h t) -> p h t", h=4)
            pe.wait_ge(sem("r_zero"), 2)
            with pe.Fori(0, NT) as it:
                wait(pe, it, "o_ok", 0)
                wait(pe, it, "go", 0)
                wait(pe, it, "gs", 0)
                wait(pe, it, "s_ok", 0)
                wait(pe, it, "st_a", 3)
                wait(pe, it, "st_p", 4)
                for n, src in enumerate((VS[:], BK[:, :, 1], BK[:, :, 0])):
                    for j in range(4):
                        mm = pe.transpose(ps[:, n, j * P:(j + 1) * P], src[:, j], ident)
                mm.then_inc(S_["turn"], 1)
                for n, j0 in ((3, 8), (4, 4)):
                    for j in range(4):
                        pe.transpose(ps[:, n, j * P:(j + 1) * P], QKV[:, j0 + j], ident)
                pe.transpose(ps[:, 5, 0:BG], bgS[:], ident[0:BG, 0:BG]).then_inc(S_["turn"], 1)
                for n in range(8):
                    mm = pe.matmul(ps[:, 6 + n // 4, (n % 4) * P:(n % 4 + 1) * P], selv[0:BG, n], bgS[:], start=True, stop=True)
                mm.then_inc(S_["turn"], 1)

                def pairs(h0, b0):
                    for h in range(h0, h0 + 4):
                        r, j = slice(64 * (h % 2), 64 * (h % 2) + 64), h // 2
                        ar = AR[r, j].rearrange("p k t -> p (k t)")
                        pe.matmul(ps[:, b0 + h - h0, 0:256], BK[r, j, 0], ar, start=True, stop=True)
                        mm = pe.matmul(ps[:, b0 + h - h0, 256:512], BK[r, j, 1], ar, start=True, stop=True)
                    mm.then_inc(S_["pairs"], 1)

                wait(pe, it, "tok", 3)
                wait(pe, it, "gv", 1)
                pairs(0, 0)
                wait(pe, it, "gkd_ok", 1)
                for h in range(4):
                    pe.matmul(by4(4)[:, h], QKV[:, 4 + h], QKV[:, 4 + h], start=True, stop=True)
                    mm = pe.matmul(by4(5)[:, h], QKV[:, 4 + h], QKV[:, h], start=True, stop=True)
                mm.then_inc(S_["pairs"], 1)
                wait(pe, it, "lg", 1)
                wait(pe, it, "intra", 1)
                wait(pe, it, "ke", 1)
                pairs(4, 4)
                for g in range(3):
                    wait(pe, it, "tt0", g + 1)
                    if g == 0:
                        wait(pe, it, "pr", 2)
                    for h in range(4):
                        mm = pe.transpose(by4(3 + g)[:, h], TTm[:, g, h], ident)
                    mm.then_inc(S_["t_mm"], 1)

                def x_mm(n):
                    l, g = order[n]
                    wait(pe, it, "lm", n + 1)
                    if l == 0:
                        wait(pe, it, "t0", g + 1)
                    else:
                        wait(pe, it, "upd", idx[l - 1, g] + 1)
                    for h in range(4):
                        mm = pe.matmul(by4(g)[:, h], LM[:, g, h], TM[:, g, h], start=True, stop=True)
                    mm.then_inc(S_["x_mm"], 1)

                def xt_mm(n):
                    l, g = order[n]
                    wait(pe, it, "x_ev", n + 1)
                    for h in range(4):
                        if l < last[g]:
                            pe.matmul(by4(3 + g)[:, h], TTm[:, g, h], X[:, g, h], start=True, stop=True)
                        mm = pe.matmul(by4(g)[:, h], X[:, g, h], TTm[:, g, h], start=True, stop=True)
                    mm.then_inc(S_["xt_mm"], 1)

                for l in range(5):
                    for g in range(3):
                        x_mm(idx[l, g])
                    for g in range(3):
                        xt_mm(idx[l, g])
                x_mm(idx[5, 2])
                wait(pe, it, "upd", idx[4, 2] + 1)
                for h in range(HR):
                    mm = pe.matmul(ps[:, 0, h * 64:(h + 1) * 64], PR[:, h, 2], Vt[:, h * 64:(h + 1) * 64], start=True, stop=True)
                mm.then_inc(S_["wv_mm"], 1)

                def a_state(c):
                    if c == 1:
                        wait_ahead(pe, it, ("s_ok", 1))
                    for par, b in ((0, 1), (1, 5)):
                        r = slice(64 * par, 64 * par + 64)
                        for j in range(4):
                            mm = pe.matmul(ps[64 * c:64 * c + 64, b, j * 64:(j + 1) * 64], AR[r, j, 0, 64 * c:64 * c + 64],
                                           ST[r, c, j], start=True, stop=True)
                    mm.then_inc(S_["as_mm"], 1)

                def chunk(c):
                    r = slice(64 * c, 64 * c + 64)
                    wait_ahead(pe, it, ("w_ok", c + 1))
                    for h in range(HR):
                        mm = pe.matmul(ps[r, 2, h * 64:(h + 1) * 64], TTm[r, h // 4, h % 4, 64 * c:64 * c + 64],
                                       W[r, h * 64:(h + 1) * 64], start=True, stop=True)
                    mm.then_inc(S_["u_mm"], 1)

                def chunk_state(c):
                    r = slice(64 * c, 64 * c + 64)
                    wait_ahead(pe, it, ("u_ok", c + 1))
                    for h in range(HR):
                        o = ps[64 * (h % 2):64 * (h % 2) + 64, 3, (h // 2) * 64:(h // 2 + 1) * 64]
                        hc = slice(h * 64, (h + 1) * 64)
                        pe.matmul(o, Bt[r, hc], U[r, hc], start=True, stop=False)
                        mm = pe.matmul(o, Kt[r, hc], Vt[r, hc], start=False, stop=True)
                    mm.then_inc(S_["s_mm"], 1)
                    for par, b in ((0, 1), (1, 5)):
                        q = slice(64 * par, 64 * par + 64)
                        for j in range(4):
                            mm = pe.matmul(ps[q, b, 256 + j * 64:256 + (j + 1) * 64], ST[q, c, j], AR[q, j, 1, 64 * c:64 * c + 64],
                                           start=True, stop=True)
                    mm.then_inc(S_["ost_mm"], 1)
                    if c == 1:
                        wait_ahead(pe, it, ("o_ok", 1))
                    for h in range(HR):
                        o = ps[64 * (h % 2):64 * (h % 2) + 64, 4, (h // 2) * 64:(h // 2 + 1) * 64]
                        hc, tc = slice(h * 64, (h + 1) * 64), slice(64 * c, 64 * c + 64)
                        pe.matmul(o, U[r, hc], PR[r, h, 1, tc], start=True, stop=False)
                        mm = pe.matmul(o, Vt[r, hc], PR[r, h, 3, tc], start=False, stop=True)
                    mm.then_inc(S_["ouv_mm"], 1)

                a_state(0)
                for h in range(4):
                    mm = pe.matmul(by4(6)[:, h], kE[:, h], S[:, h], start=True, stop=True)
                mm.then_inc(S_["gw_mm"], 1)
                xt_mm(idx[5, 2])
                wait(pe, it, "gw", 1)
                wait(pe, it, "upd", NL)
                for h in range(4):
                    mm = pe.matmul(by4(7)[:, h], TTm[:, 2, h], gW[:, h], start=True, stop=True)
                mm.then_inc(S_["gu_mm"], 1)
                chunk(0)
                chunk_state(0)
                wait(pe, it, "gu", 1)
                wait(pe, it, "ost", 2)
                for h in range(4):
                    pe.matmul(by4(6)[:, h], S[:, h], qE[:, h], start=True, stop=False)
                    mm = pe.matmul(by4(6)[:, h], gU[:, h], E[:, h], start=False, stop=True)
                mm.then_inc(S_["go_mm"], 1)
                for h in range(4):
                    mm = pe.matmul(by4(7)[:, h], gkd[:, h], gU[:, h], start=True, stop=True)
                mm.then_inc(S_["gs_mm"], 1)
                a_state(1)
                chunk(1)
                chunk_state(1)
            pe.wait_ge(S_["s_ok"], 2 * NT)
            pe.wait_ge(S_["upd"], NL * NT)
            pe.wait_ge(S_["wv"], NT)
            for j in range(4):
                mm = pe.transpose(ps[0:64, 0, j * P:(j + 1) * P], ST[:, 0, j], ident)
            mm.then_inc(sem("wkv_mm"), 1)

        @block.sync
        def _(sp):
            done = sem("saved")
            sp.wait_ge(sem("wkv_ok"), 1)
            sp.dma_start(a["p_wkv"][0, 0].rearrange("h v k -> v h k"), wkv.rearrange("v j (q k) -> v (j q) k", q=2)
                         ).then_inc(done, 16)
            sp.wait_ge(S_["gs"], NT)
            sp.dma_start(a["p_ssm"][0, 0].rearrange("h k v -> k h v"), S[:]).then_inc(done, 16)
            sp.wait_ge(done, m["saved"] + 32)
            m["saved"] += 32


def sample_recur(m):
    nc, a, sem, ps, tmp = (m[k] for k in ("nc", "a", "sem", "ps", "tmp"))
    oTr, oTg, ident, sum4 = m["oTr"], m["oTg"], const(m, "ident"), const(m, "sum4")
    SR, TR, rv, vh = tmp("SR", [P, 32, CR]), tmp("TR", [P, 32, CR]), tmp("rv", [P, 6, CR]), tmp("vh", [P, 32])
    TG = m["mix"][:, 0:8].rearrange("p a t -> p (a t)")[:, 0:32 * CG].rearrange("p (k v) -> p k v", k=32)
    SG, gqk, gv, gb = tmp("SG", [P, 32, CG]), tmp("gqk", [P, 2, 32]), tmp("gv", [P, CG]), tmp("gb", [P, 3])
    sa, oR, part, dl, oG = tmp("sa", [P, 32]), tmp("oR", [P, 32]), tmp("part", [P, CG]), tmp("dl", [P, CG]), tmp("oG", [P, CG])
    oRrow = tmp("oRrow", [NS, 512])
    rin, gin, o_back = sem("s_rin"), sem("s_gin"), sem("s_oback")
    new_rw, new_gd, o_ready, part_ready, sum_mm, saved = (sem(n) for n in (
        "s_new_rw", "s_new_gd", "s_o_ready", "s_part", "s_sum", "saved"))
    NB = NS * HG
    with nc.Block() as block:
        @block.sync
        def _(sp):
            for v in range(2):
                p = slice(64 * v, 64 * v + 64)
                sp.dma_start(SR[p], a["state_rwkv_wkv"][0].rearrange("b h v k -> (b h) v k")[:, 32 * v:32 * v + 32]).then_inc(rin, 16)
                sp.dma_start(rv[p], a["rows_rw"].rearrange("q p c -> p q c")).then_inc(rin, 16)
                sp.dma_start(vh[p], a["rows_rw"][3][:, 32 * v:32 * v + 32]).then_inc(rin, 16)
            for k in range(4):
                p = slice(NB * k, NB * k + NB)
                sp.dma_start(SG[p], a["state_gdn_ssm"][0].rearrange("b h k v -> (b h) k v")[:, 32 * k:32 * k + 32]).then_inc(gin, 16)
                sp.dma_start(gqk[p], a["rows_gd"][0:2, :, 32 * k:32 * k + 32].rearrange("q p c -> p q c")).then_inc(gin, 16)
                sp.dma_start(gv[p], a["rows_gd"][2]).then_inc(gin, 16)
                with nc.allow_non_contiguous_dma(reason="64 numbers"):
                    sp.dma_start(gb[p, 0:2], a["rows_bg"].rearrange("q p -> p q")).then_inc(gin, 16)
            sp.wait_ge(new_rw, 1)
            for v in range(2):
                p = slice(64 * v, 64 * v + 64)
                sp.dma_start(a["s_wkv"][0].rearrange("b h v k -> (b h) v k")[:, 32 * v:32 * v + 32], SR[p]).then_inc(saved, 16)
            sp.wait_ge(o_ready, 1)
            for v in range(2):
                sp.dma_start(a["o_rw"][:, 32 * v:32 * v + 32], oR[64 * v:64 * v + 64]).then_inc(o_back, 16)
            sp.wait_ge(o_back, 32)
            sp.dma_start(oRrow[:], a["o_rw"].rearrange("(b h) c -> b (h c)", b=NS)).then_inc(o_back, 16)
            sp.wait_ge(new_gd, 1)
            for k in range(4):
                p = slice(NB * k, NB * k + NB)
                sp.dma_start(a["s_ssm"][0].rearrange("b h k v -> (b h) k v")[:, 32 * k:32 * k + 32], SG[p]).then_inc(saved, 16)
            sp.wait_ge(saved, m["saved"] + 16 * 6)
            m["saved"] += 16 * 6

        @block.scalar
        def _(act):
            act.wait_ge(gin, 16 * 16)
            act.activation(gb[:, 2:3], gb[:, 1:2], ACT.Exp).then_inc(sem("s_decay"), 1)

        @block.tensor
        def _(pe):
            for n in range(2):
                pe.wait_ge(part_ready, n + 1)
                pe.matmul(ps[:, n, 0:CG], sum4, part[:], start=True, stop=True).then_inc(sum_mm, 1)
            pe.wait_ge(sem("s_oG"), 1)
            pe.transpose(ps[:, 2, 0:NB], oG[0:NB, :], ident[0:NB, 0:NB]).then_inc(sum_mm, 1)
            pe.wait_ge(o_back, 48)
            for j in range(4):
                mm = pe.transpose(ps[:, 3, j * NS:(j + 1) * NS], oRrow[:, j * P:(j + 1) * P], ident[0:NS, 0:NS])
            mm.then_inc(sum_mm, 1)

        @block.vector
        def _(dve):
            st = Steps(dve, sem("dve_step"), m["dve"])
            TT = lambda o, x, y, op: st.link(dve.tensor_tensor(o, x, y, op))
            keys = lambda n: rv[:, n].unsqueeze(1).to_broadcast([P, 32, CR])
            vals = lambda ap: ap.unsqueeze(2).to_broadcast([P, 32, CR])
            dve.wait_ge(rin, 16 * 6)
            TT(TR[:], SR[:], keys(4), ALU.mult)
            st.did(dve.tensor_reduce(sa[:], TR[:], AXX, ALU.add))
            TT(SR[:], SR[:], keys(1), ALU.mult)
            TT(TR[:], vals(sa[:]), keys(5), ALU.mult)
            TT(SR[:], SR[:], TR[:], ALU.subtract)
            TT(TR[:], vals(vh[:]), keys(2), ALU.mult)
            TT(SR[:], SR[:], TR[:], ALU.add)
            dve.sem_inc(new_rw, 1)
            TT(TR[:], SR[:], keys(0), ALU.mult)
            st.link(dve.tensor_reduce(oR[:], TR[:], AXX, ALU.add))
            dve.sem_inc(o_ready, 1)
            dve.wait_ge(sem("s_decay"), 1)
            gk = lambda n: gqk[:, n].unsqueeze(2).to_broadcast([P, 32, CG])
            gvv = lambda ap: ap.unsqueeze(1).to_broadcast([P, 32, CG])
            st.link(dve.tensor_scalar(SG[:], SG[:], gb[:, 2:3], None, ALU.mult))
            TT(TG, SG[:], gk(1), ALU.mult)
            dve.tensor_reduce(part[:], TG.rearrange("p k v -> p v k"), AXX, ALU.add).then_inc(part_ready, 1)
            dve.wait_ge(sum_mm, 1)
            TT(dl[:], gv[:], ps[:, 0, 0:CG], ALU.subtract)
            st.link(dve.tensor_scalar(dl[:], dl[:], gb[:, 0:1], None, ALU.mult))
            TT(TG, gk(1), gvv(dl[:]), ALU.mult)
            TT(SG[:], SG[:], TG, ALU.add)
            dve.sem_inc(new_gd, 1)
            TT(TG, SG[:], gk(0), ALU.mult)
            dve.tensor_reduce(part[:], TG.rearrange("p k v -> p v k"), AXX, ALU.add).then_inc(part_ready, 1)
            dve.wait_ge(sum_mm, 2)
            dve.tensor_copy(oG[:], ps[:, 1, 0:CG]).then_inc(sem("s_oG"), 1)
            dve.wait_ge(sum_mm, 4)
            st.did(dve.tensor_copy(oTg[:, :, NP:T], ps[:, 2, 0:NB].rearrange("p (b h) -> p h b", b=NS)))
            st.did(dve.tensor_copy(oTr[:, :, NP:T], ps[:, 3, 0:4 * NS].rearrange("p (j b) -> p j b", j=4)))
            st.settled()
            m["dve"] = st.n


def normalise(m):
    nc, a, sem, ps, tmp, par = (m[k] for k in ("nc", "a", "sem", "ps", "tmp", "par"))
    oTr, oTg, gg, Bv, z = m["oTr"], m["oTg"], m["gg"], m["scr"], m["Praw"][:, 26:30]
    mix = m["mix"]
    sqr, sqg, zs = mix[:, 0:4], mix[:, 4:8], mix[:, 8:12]
    blk64, ones, eps = const(m, "blk64"), const(m, "ones"), const(m, "eps")
    mm_, out = sem("n_mm"), sem("n_out")
    with nc.Block() as block:
        @block.tensor
        def _(pe):
            for n in range(12):
                if n >= 4:
                    pe.wait_ge(out, n - 3)
                kind, j = n // 4, n % 4
                if kind == 0:
                    pe.wait_ge(sem("n_sqg"), 1)
                if kind == 2:
                    pe.wait_ge(sem("n_sqr"), j + 1)
                w, x = ((ones, sqg), (blk64, oTr), (blk64, sqr))[kind]
                for h in range(2):
                    mm = pe.matmul(ps[:, 2 * (n % 4) + h, 0:TH], w, x[:, j, h * TH:(h + 1) * TH], start=True, stop=True)
                mm.then_inc(mm_, 1)

        @block.scalar
        def _(act):
            act.activation(zs, z, ACT.Silu).then_inc(sem("n_z"), 1)
            for n in (0, 1, 2, 3, 8, 9, 10, 11):
                act.wait_ge(mm_, n + 1)
                if n >= 8:
                    act.wait_ge(out, n)
                d, w, e = (sqg, CG, EPS_GD) if n < 4 else (sqr, CR, EPS_GN)
                act.activation(half(d[:, n % 4]), ps[:, 2 * (n % 4):2 * (n % 4) + 2, 0:TH], ACT.Sqrt, scale=1.0 / w,
                               bias=eps[:, e:e + 1]).then_inc(out, 1)

        @block.vector
        def _(dve):
            st = Steps(dve, sem("dve_step"), m["dve"])
            dve.tensor_tensor(sqg, oTg, oTg, ALU.mult).then_inc(sem("n_sqg"), 1)
            for j in range(4):
                dve.wait_ge(mm_, 5 + j)
                dve.wait_ge(out, 4 + j)
                dve.scalar_tensor_tensor(out=half(oTr[:, j]), in0=ps[:, 2 * j:2 * j + 2, 0:TH], scalar=-1.0 / CR,
                                         in1=half(oTr[:, j]), op0=ALU.mult, op1=ALU.add).then_inc(out, 1)
                dve.wait_ge(out, 5 + j)
                dve.tensor_tensor(sqr[:, j], oTr[:, j], oTr[:, j], ALU.mult).then_inc(sem("n_sqr"), 1)
            st.link(dve.reciprocal(sqg, sqg))
            st.link(dve.tensor_tensor(oTg, oTg, sqg, ALU.mult))
            dve.wait_ge(sem("n_z"), 1)
            st.did(dve.scalar_tensor_tensor(out=oTg, in0=oTg, scalar=param(m, "gdn_norm_w"), in1=zs, op0=ALU.mult, op1=ALU.mult))
            dve.wait_ge(out, 12)
            st.link(dve.reciprocal(sqr, sqr))
            st.link(dve.tensor_tensor(oTr, oTr, sqr, ALU.mult))
            for j in range(4):
                st.did(dve.tensor_scalar(oTr[:, j], oTr[:, j], param(m, "rwkv_ln_w", j), param(m, "rwkv_ln_b", j), ALU.mult, ALU.add))
            st.settled()
            st.link(dve.tensor_tensor(oTr, oTr, Bv[:], ALU.add))
            st.link(dve.tensor_tensor(oTr, oTr, gg, ALU.mult))
            m["dve"] = st.n


def merge(m):
    nc, a, sem, ps, tmp, par, xT = (m[k] for k in ("nc", "a", "sem", "ps", "tmp", "par", "xT"))
    oTr, oTg = m["oTr"], m["oTg"]
    merged = m["mix"][:, 0:KD]
    WG, WB, WO = tmp("WG", [P, 2, 2, KD, P]), tmp("WB", [P, 2, 2, 4, P]), tmp("WO", [P, 2, KD, P])
    ga, gb = tmp("gate_a", [P, T]), tmp("gate_b", [P, T])
    w_ready, wo_ready = [sem(f"weights{b}") for b in range(2)], [sem(f"weights{b}") for b in (2, 3)]
    base, base_o = [m["weights"][b] for b in range(2)], [m["weights"][b] for b in (2, 3)]
    mm_done, gate_out, ya_out, y_out, t_sum, o_mm, o_out = (sem("m_" + n) for n in (
        "mm", "gate", "ya", "y", "sum", "o_mm", "o_out"))

    with nc.Block() as block:
        @block.sync
        def _(sp):
            def load(b, col, first):
                for n, (src, c) in enumerate(((a["w_in"], GATE0), (a["w_in"], GATE0 + D))):
                    sp.dma_start(WG[:, b, n], src[0, :, bass.ds(col + c, P)].rearrange("(k p) c -> p k c", p=P)).then_inc(w_ready[b], 16)
                for n, src in enumerate((a["w_branch_a"], a["w_branch_b"])):
                    sp.dma_start(WB[:, b, n], src[0, :, bass.ds(col, P)].rearrange("(k p) c -> p k c", p=P)).then_inc(w_ready[b], 16)

            load(0, 0, True)
            load(1, P, True)
            for b in range(2):
                sp.dma_start(WO[:, b], a["w_out"][0, :, b * P:(b + 1) * P].rearrange("(k p) c -> p k c", p=P)).then_inc(wo_ready[b], 16)
            with sp.Fori(0, KD // 2 - 1) as it:
                for b in range(2):
                    sp.wait_ge(mm_done, it * 8 + (4 * b + 4))
                    load(b, it * (2 * P) + (2 + b) * P, False)
            with sp.Fori(0, KD // 2 - 1) as it:
                for b in range(2):
                    sp.wait_ge(o_mm, it * 2 + (b + 1))
                    sp.dma_start(WO[:, b], a["w_out"][0, :, bass.ds(it * (2 * P) + (2 + b) * P, P)]
                                 .rearrange("(k p) c -> p k c", p=P)).then_inc(wo_ready[b], 16)

        @block.tensor
        def _(pe):
            with pe.Fori(0, KD // 2) as it:
                for b in range(2):
                    pe.wait_ge(w_ready[b], it * 64 + (base[b] + 64))
                    for n in range(4):
                        pe.wait_ge((gate_out, gate_out, ya_out, y_out)[n], it * (4 if n < 2 else 2) + ((2 * b + n) if n < 2 else b))
                        kn, w, x = ((KD, WG[:, b, 0], xT), (KD, WG[:, b, 1], xT), (4, WB[:, b, 0], oTr), (4, WB[:, b, 1], oTg))[n]
                        for h in range(2):
                            for k in range(kn):
                                mm = pe.matmul(ps[:, 2 * n + h, 0:TH], w[:, k], x[:, k, h * TH:(h + 1) * TH],
                                               start=(k == 0), stop=(k == kn - 1))
                        mm.then_inc(mm_done, 1)
            pe.wait_ge(t_sum, KD)
            with pe.Fori(0, KD // 2) as it:
                for b in range(2):
                    pe.wait_ge(wo_ready[b], it * 16 + (base_o[b] + 16))
                    pe.wait_ge(o_out, it * 2 + b)
                    for h in range(2):
                        for k in range(KD):
                            mm = pe.matmul(ps[:, 2 * b + h, 0:TH], WO[:, b, k], merged[:, k, h * TH:(h + 1) * TH],
                                           start=(k == 0), stop=(k == KD - 1))
                    mm.then_inc(o_mm, 1)

        @block.scalar
        def _(act):
            with act.Fori(0, KD // 2) as it:
                for b in range(2):
                    for n, g in enumerate((ga, gb)):
                        act.wait_ge(mm_done, it * 8 + (4 * b + n + 1))
                        act.wait_ge(t_sum, it * 2 + b)
                        act.activation(half(g[:]), ps[:, 2 * n:2 * n + 2, 0:TH], ACT.Sigmoid).then_inc(gate_out, 1)

        @block.vector
        def _(dve):
            with dve.Fori(0, KD // 2) as it:
                for b in range(2):
                    dve.wait_ge(mm_done, it * 8 + (4 * b + 3))
                    dve.wait_ge(gate_out, it * 4 + (2 * b + 2))
                    dve.tensor_tensor(half(ga[:]), half(ga[:]), ps[:, 4:6, 0:TH], ALU.mult).then_inc(ya_out, 1)
                    dve.wait_ge(mm_done, it * 8 + (4 * b + 4))
                    dve.tensor_tensor(half(gb[:]), half(gb[:]), ps[:, 6:8, 0:TH], ALU.mult).then_inc(y_out, 1)
                    dve.wait_ge(ya_out, it * 2 + (b + 1))
                    dve.wait_ge(y_out, it * 2 + (b + 1))
                    dve.tensor_tensor(merged[:, bass.ds(it * 2 + b, 1)], ga[:].unsqueeze(1), gb[:].unsqueeze(1), ALU.add
                                      ).then_inc(t_sum, 1)
            with dve.Fori(0, KD // 2) as it:
                for b in range(2):
                    dve.wait_ge(o_mm, it * 2 + (b + 1))
                    xt = xT[:, bass.ds(it * 2 + b, 1)].rearrange("p o (h t) -> p (o h) t", h=2)
                    dve.scalar_tensor_tensor(out=xt, in0=xt, scalar=ALPHA, in1=ps[:, 2 * b:2 * b + 2, 0:TH],
                                             op0=ALU.mult, op1=ALU.add).then_inc(o_out, 1)
    m["weights"] = [w + n * KD // 2 for w, n in zip(m["weights"], (64, 64, 16, 16))]


def norm1(m):
    nc, sem, ps, tmp, xT = (m[k] for k in ("nc", "sem", "ps", "tmp", "xT"))
    ones, eps = const(m, "ones"), const(m, "eps")
    sq, rt = tmp("n1_sq", [P, KD, T]), tmp("n1_rt", [P, T])
    mm_, centred, squared, rooted = (sem("n1_" + n) for n in ("mm", "centred", "squared", "rooted"))
    hs = [slice(h * TH, (h + 1) * TH) for h in range(2)]
    with nc.Block() as block:
        @block.tensor
        def _(pe):
            for h in range(2):
                for k in range(KD):
                    mm = pe.matmul(ps[:, h, 0:TH], ones, xT[:, k, hs[h]], start=(k == 0), stop=(k == KD - 1))
                mm.then_inc(mm_, 1)
            for h in range(2):
                pe.wait_ge(squared, h + 1)
                for k in range(KD):
                    mm = pe.matmul(ps[:, 2 + h, 0:TH], ones, sq[:, k, hs[h]], start=(k == 0), stop=(k == KD - 1))
                mm.then_inc(mm_, 1)

        @block.scalar
        def _(act):
            for h in range(2):
                act.wait_ge(centred, h + 1)
                act.activation(sq[:, :, hs[h]], xT[:, :, hs[h]], ACT.Square).then_inc(squared, 1)
            for h in range(2):
                act.wait_ge(mm_, 3 + h)
                act.activation(rt[:, hs[h]], ps[:, 2 + h, 0:TH], ACT.Sqrt, scale=1.0 / D, bias=eps[:, EPS_LN:EPS_LN + 1]
                               ).then_inc(rooted, 1)

        @block.vector
        def _(dve):
            st = Steps(dve, sem("dve_step"), m["dve"])
            over = lambda ap: ap.unsqueeze(1).to_broadcast([P, KD, TH])
            for h in range(2):
                dve.wait_ge(mm_, h + 1)
                dve.scalar_tensor_tensor(out=xT[:, :, hs[h]], in0=over(ps[:, h, 0:TH]), scalar=-1.0 / D, in1=xT[:, :, hs[h]],
                                         op0=ALU.mult, op1=ALU.add).then_inc(centred, 1)
            for h in range(2):
                dve.wait_ge(rooted, h + 1)
                dve.wait_ge(squared, 2)
                st.link(dve.reciprocal(rt[:, hs[h]], rt[:, hs[h]]))
                st.link(dve.tensor_tensor(xT[:, :, hs[h]], xT[:, :, hs[h]], over(rt[:, hs[h]]), ALU.mult))
            for k in range(KD):
                st.did(dve.tensor_scalar(xT[:, k], xT[:, k], param(m, "ln1_g", k), param(m, "ln1_b", k), ALU.mult, ALU.add))
            st.settled()
            m["dve"] = st.n


HP = 16
NK = 128
TK = 16
PH = 8
TILES = [(n * P, P) for n in range(NT)] + [(NP, NS)]


def query(m):
    nc, a, sem, ps, tmp, xT = (m[k] for k in ("nc", "a", "sem", "ps", "tmp", "xT"))
    R = 4
    ring, qT = tmp("q_ring", [P, R, KD, P]), tmp("qT", [P, HP, T])
    keys, keysT = tmp("keys", [P, HP, P]), tmp("keysT", [P, HP, NK])
    m["scores"] = scores = tmp("scores", [P, NT + 1, HP, NK])
    w_in, k_in, k_mm, k_out = [sem(f"weights{b}") for b in range(R)], sem("q_kin"), sem("q_kmm"), sem("q_kout")
    q_mm, q_out, s_mm, s_out = (sem("q_" + n) for n in ("mm", "out", "smm", "sout"))
    base = m["weights"]

    with nc.Block() as block:
        @block.sync
        def _(sp):
            wq = a["peer_wq"]
            for b in range(R):
                sp.dma_start(ring[:, b], wq[0, :, b * P:(b + 1) * P].rearrange("(k p) c -> p k c", p=P)).then_inc(w_in[b], 16)
            sp.dma_start(keys[:], a["peer_subkeys"][0].rearrange("h q n c -> n (h q) c")).then_inc(k_in, 16)
            with sp.Fori(0, HP // R - 1) as it:
                for b in range(R):
                    sp.wait_ge(q_mm, it * R + (b + 1))
                    sp.dma_start(ring[:, b], wq[0, :, bass.ds(it * (R * P) + (R + b) * P, P)].rearrange("(k p) c -> p k c", p=P)
                                 ).then_inc(w_in[b], 16)

        @block.tensor
        def _(pe):
            with pe.Fori(0, HP // R) as it:
                for b in range(R):
                    pe.wait_ge(w_in[b], it * 16 + (base[b] + 16))
                    pe.wait_ge(q_out, it * R + (b + 1))
                    for h in range(2):
                        for k in range(KD):
                            mm = pe.matmul(ps[:, 2 * (b % 2) + h, 0:TH], ring[:, b, k], xT[:, k, h * TH:(h + 1) * TH],
                                           start=(k == 0), stop=(k == KD - 1))
                    mm.then_inc(q_mm, 1)
            pe.wait_ge(k_in, 16)
            for j in range(HP):
                mm = pe.transpose(ps[:, 4 + j // 4, (j % 4) * P:(j % 4 + 1) * P], keys[:, j], const(m, "ident"))
            mm.then_inc(k_mm, 1)
            pe.wait_ge(k_out, 1)
            pe.wait_ge(q_out, 2 + HP)
            for n, (t0, tn) in enumerate(TILES):
                if n >= 2:
                    pe.wait_ge(s_out, n - 1)
                for j in range(HP):
                    mm = pe.matmul(ps[0:tn, 4 * (n % 2) + j // 4, (j % 4) * P:(j % 4 + 1) * P], qT[:, j, t0:t0 + tn],
                                   keysT[:, j], start=True, stop=True)
                mm.then_inc(s_mm, 1)

        @block.scalar
        def _(act):
            act.sem_inc(q_out, 2)
            with act.Fori(0, HP // R) as it:
                for b in range(R):
                    act.wait_ge(q_mm, it * R + (b + 1))
                    act.activation(qT[:, bass.ds(it * R + b, 1), :].rearrange("p o (h t) -> p (o h) t", h=2),
                                   ps[:, 2 * (b % 2):2 * (b % 2) + 2, 0:TH], ACT.Copy).then_inc(q_out, 1)
            act.wait_ge(k_mm, 1)
            act.activation(keysT[:].rearrange("p (b j) n -> p b (j n)", b=4), ps[:, 4:8, :], ACT.Copy).then_inc(k_out, 1)
            for n, (t0, tn) in enumerate(TILES):
                act.wait_ge(s_mm, n + 1)
                act.activation(scores[0:tn, n].rearrange("p (b j) n -> p b (j n)", b=4),
                               ps[0:tn, 4 * (n % 2):4 * (n % 2) + 4, :], ACT.Copy).then_inc(s_out, 1)


def rows(m):
    nc, a, sem, ps, tmp, xT, x1row = (m[k] for k in ("nc", "a", "sem", "ps", "tmp", "xT", "x1row"))
    parts = tmp("parts", [P, 2, 3, D], BF16)
    rest = tmp("rest", [P, 2, D])
    r_mm, r_out, p_out, saved = (sem(n) for n in ("x1_mm", "x1_out", "x1_parts", "saved"))
    base = m["saved"]
    with nc.Block() as block:
        @block.tensor
        def _(pe):
            for n, (t0, tn) in enumerate(TILES):
                if n >= 2:
                    pe.wait_ge(r_out, n - 1)
                for k in range(KD):
                    mm = pe.transpose(ps[0:tn, 2 * (n % 2) + k // 4, (k % 4) * P:(k % 4 + 1) * P], xT[:, k, t0:t0 + tn],
                                      const(m, "ident"))
                mm.then_inc(r_mm, 1)

        @block.scalar
        def _(act):
            for n, (t0, tn) in enumerate(TILES):
                act.wait_ge(r_mm, n + 1)
                act.activation(x1row[0:tn, n].rearrange("p (b c) -> p b c", b=2), ps[0:tn, 2 * (n % 2):2 * (n % 2) + 2, :],
                               ACT.Copy).then_inc(r_out, 1)

        @block.gpsimd
        def _(pool):
            st = Steps(pool, sem("x1_pool"))
            for n, (t0, tn) in enumerate(TILES):
                pool.wait_ge(r_out, n + 1)
                if n >= 2:
                    pool.wait_ge(saved, base + 48 * (n - 1))
                src, left = x1row[0:tn, n], rest[0:tn, n % 2]
                for q in range(3):
                    st.link(nc.gpsimd.tensor_copy(parts[0:tn, n % 2, q], src))
                    if q < 2:
                        st.link(nc.gpsimd.tensor_tensor(left, src, parts[0:tn, n % 2, q], ALU.subtract))
                        src = left
                pool.sem_inc(p_out, 1)

        @block.sync
        def _(sp):
            for n, (t0, tn) in enumerate(TILES):
                sp.wait_ge(p_out, n + 1)
                for q in range(3):
                    sp.dma_start(a["x1_parts"][q, t0:t0 + tn, :], parts[0:tn, n % 2, q]).then_inc(saved, 16)
                sp.wait_ge(saved, base + 48 * (n + 1))
            m["saved"] += 48 * len(TILES)


def select(m):
    nc, sem, ps, tmp, scores, idxT, gateT = (m[k] for k in ("nc", "sem", "ps", "tmp", "scores", "idxT", "gateT"))
    LOWEST = -3.0e38
    top, topi, topf = tmp("top", [P, HP, TK]), tmp("topi", [P, HP, TK], U32), tmp("topf", [P, HP, TK])
    cand, one = tmp("cand", [P, PH, TK * TK]), tmp("one", [P, PH, TK, TK])
    best, besti, pos, posf = (tmp("best", [P, PH, TK]), tmp("besti", [P, PH, TK], U32), tmp("pos", [P, PH, TK], U32),
                              tmp("posf", [P, 2, PH, TK]))
    ids, gates, sums = tmp("ids", [P, 2, PH, TK]), tmp("gates", [P, PH, TK]), tmp("gsums", [P, PH])
    tops, exps, tiles, turned, taken = (sem("sel_" + n) for n in ("tops", "exps", "tiles", "turned", "taken"))
    with nc.Block() as block:
        @block.scalar
        def _(act):
            for n, (t0, tn) in enumerate(TILES):
                act.wait_ge(tops, n + 1)
                act.activation(gates[0:tn], gates[0:tn], ACT.Exp).then_inc(exps, 1)
                act.wait_ge(turned, n + 1)
                act.activation(idxT[:, t0:t0 + tn], ps[:, 0, 0:tn], ACT.Copy)
                act.activation(gateT[:, t0:t0 + tn], ps[:, 1, 0:tn], ACT.Copy).then_inc(taken, 1)

        @block.tensor
        def _(pe):
            for n, (t0, tn) in enumerate(TILES):
                pe.wait_ge(tiles, n + 1)
                if n >= 1:
                    pe.wait_ge(taken, n)
                pe.transpose(ps[:, 0, 0:tn], ids[0:tn, 0].rearrange("p h k -> p (h k)"), const(m, "ident")[0:tn, 0:tn])
                pe.transpose(ps[:, 1, 0:tn], gates[0:tn].rearrange("p h k -> p (h k)"), const(m, "ident")[0:tn, 0:tn]
                             ).then_inc(turned, 1)

        @block.vector
        def _(dve):
            st = Steps(dve, sem("dve_step"), m["dve"])

            def top16(values, indices, x):
                k = x.shape[1]
                for r in range(k):
                    st.did(dve.max(values[:, r, 0:8], x[:, r]))
                st.settled()
                for r in range(k):
                    st.did(dve.max_index(indices[:, r, 0:8], values[:, r, 0:8], x[:, r]))
                st.settled()
                for r in range(k):
                    st.did(dve.match_replace(x[:, r], values[:, r, 0:8], x[:, r], LOWEST))
                st.settled()
                for r in range(k):
                    st.did(dve.max(values[:, r, 8:16], x[:, r]))
                st.settled()
                for r in range(k):
                    st.did(dve.max_index(indices[:, r, 8:16], values[:, r, 8:16], x[:, r]))
                st.settled()

            for n, (t0, tn) in enumerate(TILES):
                p = slice(0, tn)
                top16(top[p], topi[p], scores[p, n])
                st.link(dve.tensor_copy(topf[p], topi[p]))
                halves = top[p].rearrange("p (h q) k -> p h q k", q=2)
                idx_ = topf[p].rearrange("p (h q) k -> p h q k", q=2)
                st.link(dve.tensor_tensor(cand[p].rearrange("p h (i j) -> p h i j", i=TK),
                                          halves[:, :, 0].unsqueeze(3).to_broadcast([tn, PH, TK, TK]),
                                          halves[:, :, 1].unsqueeze(2).to_broadcast([tn, PH, TK, TK]), ALU.add))
                top16(best[p], besti[p], cand[p])
                if n >= 1:
                    dve.wait_ge(turned, n)
                st.link(dve.tensor_tensor(gates[p], best[p], best[p, :, 0:1].to_broadcast([tn, PH, TK]), ALU.subtract))
                dve.sem_inc(tops, 1)
                st.link(dve.tensor_scalar(pos[p], besti[p], 4, None, ALU.logical_shift_right))
                st.link(dve.tensor_copy(posf[p, 0], pos[p]))
                st.link(dve.tensor_scalar(pos[p], besti[p], 15, None, ALU.bitwise_and))
                st.link(dve.tensor_copy(posf[p, 1], pos[p]))
                iota = const(m, "iota16")[p].unsqueeze(1).unsqueeze(1).to_broadcast([tn, PH, TK, TK])
                for q in range(2):
                    st.link(dve.tensor_tensor(one[p], posf[p, q].unsqueeze(3).to_broadcast([tn, PH, TK, TK]), iota, ALU.is_equal))
                    st.link(dve.tensor_tensor(one[p], one[p], idx_[:, :, q].unsqueeze(2).to_broadcast([tn, PH, TK, TK]), ALU.mult))
                    st.link(dve.tensor_reduce(ids[p, q], one[p], AXX, ALU.add))
                st.link(dve.scalar_tensor_tensor(out=ids[p, 0], in0=ids[p, 0], scalar=float(NK), in1=ids[p, 1],
                                                 op0=ALU.mult, op1=ALU.add))
                dve.wait_ge(exps, n + 1)
                st.link(dve.tensor_reduce(sums[p], gates[p], AXX, ALU.add))
                st.link(dve.reciprocal(sums[p], sums[p]))
                st.link(dve.tensor_tensor(gates[p], gates[p], sums[p].unsqueeze(2).to_broadcast([tn, PH, TK]), ALU.mult))
                dve.sem_inc(tiles, 1)
            m["dve"] = st.n


STEP, GROUP = 32, 16
RU, RV = 8, 16
BATCH = 4
UB = 2
LAG = 6


def experts(m):
    nc, a, sem, ps, tmp, idxT, gateT = (m[k] for k in ("nc", "a", "sem", "ps", "tmp", "idxT", "gateT"))
    U, V = tmp("U_rows", [P, RU, D]), tmp("V_rows", [P, RV, D])
    ixs, gs = tmp("ixs", [P, 2, GROUP], U32), tmp("gs", [P, 2, GROUP])
    pick = tmp("pick", [48, GROUP, P], BF16)
    pick1 = tmp("pick1", [48, GROUP])
    xp = tmp("xp", [48, 2, D], BF16)
    hp, hg, hz = tmp("hp", [P, STEP]), tmp("hg", [P, 2, BATCH]), tmp("hz", [P, 2, GROUP, GROUP])
    res = tmp("res", [GROUP, 2, D])
    u_in, v_in = [sem(f"e_u{k}") for k in range(RU // UB)], [sem(f"e_v{k}") for k in range(RV // BATCH)]
    xp_in = [sem(f"e_xp{g}") for g in range(2)]
    (pick_ok, zeroed, staged, xb_done, h_done, gelu_ok, hz_ok, mm_done, res_ok) = (sem("e_" + n) for n in (
        "pick", "zeroed", "staged", "xb", "h", "gelu", "hz", "mm", "res"))
    saved, base = sem("saved"), m["saved"]
    ITS = NP // STEP
    diag = lambda g, t, n: hz[:, g].rearrange("p t m -> p (t m)")[:, t * (GROUP + 1):(t + n - 1) * (GROUP + 1) + 1:GROUP + 1]

    with nc.Block() as block:
        @block.sync
        def _(sp):
            def load_x(it, g, tn=GROUP):
                for q in range(3):
                    src = a["x1_parts"][q, bass.ds(it * STEP + g * GROUP, tn), :] if tn == GROUP else a["x1_parts"][q, NP:T, :]
                    sp.dma_start(xp[q * GROUP:q * GROUP + tn, g], src).then_inc(xp_in[g], 16)

            def save(it, g, tn=GROUP):
                values = [it * 2 + (g + 1), it * 32 + (base + 16 * g)]
                if tn == GROUP and not isinstance(it, int):
                    values = [sp.to_reg(v) for v in values]
                sp.wait_ge(res_ok, values[0])
                sp.wait_ge(saved, values[1])
                dst = a["ff"][bass.ds(it * STEP + g * GROUP, tn), :] if tn == GROUP else a["ff"][NP:T, :]
                sp.dma_start(dst, res[0:tn, g]).then_inc(saved, 16)

            sp.wait_ge(zeroed, 2)
            load_x(0, 0)
            load_x(0, 1)
            with sp.Fori(0, ITS - 1) as it:
                for g in range(2):
                    sp.wait_ge(xb_done, it * STEP + GROUP * (g + 1))
                    load_x(it + 1, g)
                    save(it, g)
            sp.wait_ge(xb_done, ITS * STEP - GROUP)
            load_x(ITS, 0, NS)
            save(ITS - 1, 0)
            save(ITS - 1, 1)
            save(ITS, 0, NS)
            sp.wait_ge(saved, base + 16 * (2 * ITS + 1))
            m["saved"] += 16 * (2 * ITS + 1)

        @block.gpsimd
        def _(pool):
            def gather(it, tokens, ahead):
                for t in tokens:
                    g = t // GROUP
                    if t % GROUP == 0:
                        n = len(tokens) if len(tokens) < GROUP else GROUP
                        nc.gpsimd.tensor_copy(ixs[:, g, 0:n], idxT[:, bass.ds(it * STEP + t, n)]).then_inc(staged, 1)
                        nc.gpsimd.tensor_copy(gs[:, g, 0:n], gateT[:, bass.ds(it * STEP + t, n)]).then_inc(staged, 1)
                        pool.wait_ge(staged, it * 4 + 2 * (g + 1))
                    ku, kv = t % RU, t % RV
                    off = lambda: bass.IndirectOffsetOnAxis(ap=ixs[:, g, t % GROUP:t % GROUP + 1], axis=0)
                    ahead(h_done, it * STEP + (t + 1))
                    nc.gpsimd.indirect_dma_start(U[:, ku, :], None, a["peer_u"][0], off()).then_inc(u_in[ku // UB], 16)
                    ahead(mm_done, it * STEP + (t + 1))
                    nc.gpsimd.indirect_dma_start(V[:, kv, :], None, a["peer_v"][0], off()).then_inc(v_in[kv // BATCH], 16)

            def ahead(s, value):
                v = pool.to_reg(value)
                pool.wait_ge(sem("cst_in"), 16)
                pool.wait_ge(s, v)

            with pool.Fori(0, ITS) as it:
                gather(it, range(STEP), ahead)
            gather(ITS, range(NS), pool.wait_ge)

        @block.vector
        def _(dve):
            st = Steps(dve, sem("dve_step"), m["dve"])
            dve.sem_inc(h_done, RU)
            dve.memset(hz[:], 0.0).then_inc(zeroed, 1)
            dve.memset(xp[:], 0.0).then_inc(zeroed, 1)
            st.link(dve.tensor_tensor(pick1[:], const(m, "mod16")[0:48].to_broadcast([48, GROUP]), const(m, "iota16")[0:48],
                                      ALU.is_equal))
            m["dve"] = st.n
            dve.tensor_copy(pick[:], pick1[:].unsqueeze(2).to_broadcast([48, GROUP, P])).then_inc(pick_ok, 1)
            dve.wait_ge(zeroed, 2)

            def dots(it, n):
                def weigh(b):
                    dve.wait_ge(gelu_ok, it * (STEP // BATCH) + (b + 1))
                    g, t = b * BATCH // GROUP, b * BATCH % GROUP
                    dve.tensor_tensor(diag(g, t, BATCH), hg[:, b % 2], gs[:, g, t:t + BATCH], ALU.mult).then_inc(hz_ok, 1)

                for t in range(n):
                    k = t % RU
                    dve.wait_ge(xb_done, it * STEP + (t + 1))
                    if t % UB == 0:
                        dve.wait_ge(u_in[k // UB], it * (16 * UB * STEP // RU) + 16 * UB * (t // RU + 1))
                    u = U[:, k, :].rearrange("p (b c) -> p b c", b=2)
                    dve.tensor_tensor_reduce(u, u, ps[:, 2 * (t % 2):2 * (t % 2) + 2, :], 1.0, 0.0, ALU.mult, ALU.add,
                                             hp[:, t:t + 1]).then_inc(h_done, 1)
                    if t % BATCH == 0 and t:
                        weigh(t // BATCH - 1)
                weigh(n // BATCH - 1)

            with dve.Fori(0, ITS) as it:
                dots(it, STEP)
            dots(ITS, NS)

        @block.scalar
        def _(act):
            def gelus(it, n):
                def out(g, tn):
                    act.wait_ge(mm_done, it * STEP + (g * GROUP + tn + RV))
                    act.wait_ge(saved, it * 32 + (base + 16 * g))
                    act.activation(res[0:tn, g].rearrange("p (b c) -> p b c", b=2), ps[0:tn, 4 + 2 * g:6 + 2 * g, :], ACT.Copy
                                   ).then_inc(res_ok, 1)

                for b in range(n // BATCH):
                    act.wait_ge(h_done, it * STEP + (BATCH * b + BATCH + RU))
                    act.activation(hg[:, b % 2], hp[:, BATCH * b:BATCH * (b + 1)], ACT.Gelu).then_inc(gelu_ok, 1)
                    if b * BATCH == GROUP + BATCH:
                        out(0, GROUP)
                if n > GROUP:
                    out(1, GROUP)
                else:
                    out(0, n)

            with act.Fori(0, ITS) as it:
                gelus(it, STEP)
            gelus(ITS, NS)

        @block.tensor
        def _(pe):
            pe.sem_inc(mm_done, RV)
            pe.wait_ge(pick_ok, 1)

            def spread(it, t, n):
                g = t // GROUP
                if t % GROUP == 0:
                    pe.wait_ge(xp_in[g], it * 48 + 48)
                pe.wait_ge(h_done, it * STEP + (t + RU - 1))
                for h in range(2):
                    mm = pe.matmul(ps[:, 2 * (t % 2) + h, :], pick[:, t % GROUP, :], xp[:, g, h * 512:(h + 1) * 512],
                                   start=True, stop=True)
                mm.then_inc(xb_done, 1)

            def gather_v(it, t, n):
                g, tg = t // GROUP, t % GROUP
                if t % BATCH == 0:
                    pe.wait_ge(hz_ok, it * (STEP // BATCH) + (t // BATCH + 1))
                    pe.wait_ge(v_in[t % RV // BATCH], it * (16 * BATCH * STEP // RV) + 16 * BATCH * (t // RV + 1))
                if tg == 0:
                    pe.wait_ge(res_ok, it * 2)
                tn = min(n, GROUP)
                for h in range(2):
                    mm = pe.matmul(ps[0:tn, 4 + 2 * g + h, :], hz[:, g, tg, 0:tn], V[:, t % RV, h * 512:(h + 1) * 512],
                                   start=(tg == 0), stop=(tg == tn - 1))
                mm.then_inc(mm_done, 1)

            def tokens(it, n):
                for t in range(n + LAG):
                    if t < n:
                        spread(it, t, n)
                    if t >= LAG:
                        gather_v(it, t - LAG, n)

            with pe.Fori(0, ITS) as it:
                tokens(it, STEP)
            tokens(ITS, NS)


def norm2(m):
    nc, a, sem, tmp, x1row = (m[k] for k in ("nc", "a", "sem", "tmp", "x1row"))
    ff, g2, b2, sq = tmp("ff_in", [P, NT + 1, D]), tmp("n2_g", [P, D]), tmp("n2_b", [P, D]), tmp("n2_sq", [P, D])
    stat = tmp("stat", [P, NT + 1, 4])
    f_in, g_in, roots_in, roots, done = (sem("n2_" + n) for n in ("ff", "gb", "rin", "roots", "done"))
    saved, base = sem("saved"), m["saved"]
    with nc.Block() as block:
        @block.sync
        def _(sp):
            sp.dma_start(g2[:], a["ln2_g"].to_broadcast([P, D])).then_inc(g_in, 16)
            sp.dma_start(b2[:], a["ln2_b"].to_broadcast([P, D])).then_inc(g_in, 16)
            for n, (t0, tn) in enumerate(TILES):
                sp.dma_start(ff[0:tn, n], a["ff"][t0:t0 + tn, :]).then_inc(f_in, 16)
            for n, (t0, tn) in enumerate(TILES):
                dst = a["y_prompt"][0, t0:t0 + tn, :] if n < NT else a["y_sample"].rearrange("b o d -> (b o) d")
                sp.wait_ge(done, n + 1)
                sp.dma_start(dst, x1row[0:tn, n]).then_inc(saved, 16)
            sp.wait_ge(saved, base + 16 * len(TILES))

        @block.scalar
        def _(act):
            for n, (t0, tn) in enumerate(TILES):
                act.wait_ge(roots_in, n + 1)
                act.activation(stat[0:tn, n, 2:3], stat[0:tn, n, 1:2], ACT.Sqrt, scale=1.0 / D,
                               bias=const(m, "eps")[0:tn, EPS_LN:EPS_LN + 1]).then_inc(roots, 1)

        @block.vector
        def _(dve):
            st = Steps(dve, sem("dve_step"), m["dve"])
            dve.wait_ge(f_in, 16 * len(TILES))
            dve.wait_ge(g_in, 32)
            for n, (t0, tn) in enumerate(TILES):
                x, s = x1row[0:tn, n], stat[0:tn, n]
                st.link(dve.scalar_tensor_tensor(out=x, in0=x, scalar=ALPHA, in1=ff[0:tn, n], op0=ALU.mult, op1=ALU.add))
                st.link(dve.tensor_reduce(s[:, 0:1], x, AXX, ALU.add))
                st.link(dve.tensor_scalar(s[:, 0:1], s[:, 0:1], 1.0 / D, None, ALU.mult))
                st.link(dve.tensor_scalar(x, x, s[:, 0:1], None, ALU.subtract))
                st.link(dve.tensor_tensor_reduce(sq[0:tn], x, x, 1.0, 0.0, ALU.mult, ALU.add, s[:, 1:2]))
                dve.sem_inc(roots_in, 1)
                dve.wait_ge(roots, n + 1)
                st.link(dve.reciprocal(s[:, 3:4], s[:, 2:3]))
                st.link(dve.scalar_tensor_tensor(out=x, in0=x, scalar=s[:, 3:4], in1=g2[0:tn], op0=ALU.mult, op1=ALU.mult))
                dve.tensor_tensor(x, x, b2[0:tn], ALU.add).then_inc(done, 1)


_INS = ['x_prompt', 'x_sample', 'state_rwkv_shift', 'state_rwkv_wkv', 'state_gdn_conv', 'state_gdn_ssm', 'w_in', 'rwkv_mu',
        'rwkv_w0', 'rwkv_w2', 'rwkv_a0', 'rwkv_a2', 'rwkv_g2', 'rwkv_k_k', 'rwkv_k_a', 'rwkv_r_k', 'rwkv_ln_w', 'rwkv_ln_b',
        'gdn_conv_w', 'gdn_a_log', 'gdn_dt_bias', 'gdn_norm_w', 'w_branch_a', 'w_branch_b', 'w_out', 'ln1_g', 'ln1_b',
        'peer_wq', 'peer_subkeys', 'peer_u', 'peer_v', 'ln2_g', 'ln2_b']

_SHAPES = {"y_prompt": (1, NP, D), "y_sample": (NS, 1, D), "p_shift": (1, 1, RW_COLS), "p_wkv": (1, 1, HR, CR, CR),
           "p_conv": (1, 1, 3, GD_QKV), "p_ssm": (1, 1, HG, CG, CG), "s_shift": (1, NS, RW_COLS), "s_wkv": (1, NS, HR, CR, CR),
           "s_conv": (1, NS, 3, GD_QKV), "s_ssm": (1, NS, HG, CG, CG)}
_SCRATCH = {"rows_rw": (6, NS * HR, CR), "rows_gd": (3, NS * HG, CG), "rows_bg": (2, NS * HG), "o_rw": (NS * HR, CR),
            "ff": (T, D), "x1_parts": ((3, T, D), "bf16")}


def kernel(**inputs):
    import numpy as _np
    import concourse.bacc as _bacc
    from concourse import mybir as _mybir
    from concourse.bass_utils import run_bass_kernel_spmd as _run

    nc = _bacc.Bacc("TRN2", target_bir_lowering=False, num_devices=1)
    arrays, a = {}, {}
    for name in _INS + ["consts"]:
        x = _np.ascontiguousarray(CONSTS if name == "consts" else inputs[name])
        arrays[name + "_dram"] = x
        a[name] = nc.dram_tensor(name + "_dram", x.shape, _mybir.dt.from_np(x.dtype), kind="ExternalInput").ap()
    for name, shape in _SHAPES.items():
        a[name] = nc.dram_tensor(name + "_dram", shape, _mybir.dt.float32, kind="ExternalOutput").ap()
    for name, shape in _SCRATCH.items():
        dt = _mybir.dt.float32
        if isinstance(shape[-1], str):
            shape, dt = shape[0], _mybir.dt.bfloat16
        a[name] = nc.dram_tensor(name + "_dram", shape, dt, kind="Internal").ap()
    program(nc, a)
    r = _run(nc, [arrays], core_ids=[0])
    return tuple(r.results[0][name + "_dram"] for name in _SHAPES)
```

```python
from contextlib import ExitStack

import numpy as np

import concourse.bass as bass
from concourse import mybir

ALU = mybir.AluOpType
ACT = mybir.ActivationFunctionType
AXX = mybir.AxisListType.X
F32 = mybir.dt.float32
BF16 = mybir.dt.bfloat16
U32 = mybir.dt.uint32

P = 128
D = 1024
KD = D // P
NP = 512
NS = 8
T = NP + NS
TH = T // 2
NT = NP // P
HR, CR = 8, 64
HG, CG = 4, 128
RW_COLS = 1792
RT_ = RW_COLS // P
QT = 12
ZT = 4
PT = RT_ + QT + ZT
GD_QKV = 1536
BA0 = PT * P
GATE0 = BA0 + 8
ALPHA = 2.0 ** 0.25
DECAY = float(np.exp(-0.5))
TAIL = 11
BG = 36

_C = {}


def _consts():
    cols = []

    def put(name, a):
        _C[name] = (sum(c.shape[1] for c in cols), a.shape[1])
        cols.append(a.astype(np.float32))

    i = np.arange(P)
    s, t = i[:, None], i[None, :]
    put("ident", np.eye(P))
    put("ones", np.ones((P, P)))
    put("blk64", (s // 64 == t // 64) * 1.0)
    for m in (1, 2, 4, 8, 16, 32, 64):
        put(f"lvl{m}", ((s // (2 * m) == t // (2 * m)) & (s // m % 2 == 0) & (t // m % 2 == 1)) * 1.0)
    one = np.ones((P, P))
    put("pair", np.concatenate([((s // 64 == t // 64) & (s < t)) * 1.0, ((s // 64 == t // 64) & (s <= t)) * 1.0], 1))
    put("incl", (s <= t) * 1.0)
    sel = np.zeros((P, 8, P))
    for h in range(4):
        sel[h, h] = 1.0
        sel[32 + h, 4 + h] = 1.0
    put("sel", sel.reshape(P, -1))
    put("keep64", np.broadcast_to((np.arange(NP) % 64 != 0) * 1.0, (P, NP)))
    put("keep128", np.broadcast_to((np.arange(NP) % 128 != 0) * 1.0, (P, NP)))
    put("sum4", (s % 32 == t % 32) * 1.0)
    put("iota16", np.broadcast_to(np.arange(16.0), (P, 16)))
    put("mod16", (s % 16) * 1.0)
    put("eps", np.broadcast_to(np.array([1e-12, 1e-6, 64e-5, 1e-5]), (P, 4)))
    return np.concatenate(cols, 1)


CONSTS = _consts()
EPS_KK, EPS_GD, EPS_GN, EPS_LN = range(4)

_PAR = {}
_n = 0
for _name, _rows in (("rwkv_mu", RT_), ("rwkv_w0", 4), ("rwkv_a0", 4), ("rwkv_k_k", 4), ("rwkv_k_a", 4),
                     ("rwkv_r_k", 4), ("rwkv_ln_w", 4), ("rwkv_ln_b", 4), ("gdn_conv_w", 4 * QT), ("gdn_norm_w", 1),
                     ("ln1_g", KD), ("ln1_b", KD)):
    _PAR[_name] = (_n, _rows)
    _n += _rows
NPAR = _n


class Steps:

    def __init__(self, eng, sem, start=0):
        self.eng, self.sem, self.n, self.base = eng, sem, start, 0

    def did(self, ins):
        ins.then_inc(self.sem, 1)
        self.n += 1

    def settled(self):
        self.eng.wait_ge(self.sem, self.base + self.n)

    def link(self, ins):
        self.did(ins)
        self.settled()


def program(nc, a):
    ctx = ExitStack()
    with ctx:
        def sb(name, shape, dt=F32):
            return ctx.enter_context(nc.sbuf_tensor(name, shape, dt))

        sems = {}

        def sem(name):
            if name not in sems:
                sems[name] = ctx.enter_context(nc.semaphore(name))
            return sems[name]

        ps = ctx.enter_context(nc.psum_tensor("ps", [P, 8, 512], F32))
        cst = sb("cst", [P, CONSTS.shape[1]])
        par = sb("par", [P, NPAR])
        xT = sb("xT", [P, KD, T])
        m = dict(nc=nc, a=a, sem=sem, ps=ps, cst=cst, par=par, xT=xT, saved=0)

        def phase(*steps):
            with ExitStack() as local:
                m["tmp"] = lambda name, shape, dt=F32: local.enter_context(nc.sbuf_tensor(name, shape, dt))
                for step in steps:
                    step(m)

        with ExitStack() as mixing:
            for name, shape in (("Praw", [P, PT, T]), ("mix", [P, RT_, T]), ("conv", [P, QT, T]), ("kk", [P, 4, T]),
                                ("scr", [P, 4, T]), ("bg", [BG, T]), ("gdpar", [BG, 4]), ("omka", [P, 4]),
                                ("Gend", [P, 4, NP // 64])):
                m[name] = mixing.enter_context(nc.sbuf_tensor(name, shape, F32))
            phase(load_inputs, project, tokenwise)
            phase(sample_rows)
            phase(recur)
            phase(sample_recur)
            phase(normalise)
            phase(merge)
        for name, shape, dt in (("scores", [P, (NT + 1) * HP, NK], F32), ("idxT", [P, NP + P], U32), ("gateT", [P, NP + P], F32)):
            m[name] = sb(name, shape, dt)
        choose_buffers(m, sb)
        phase(norm1)
        phase(query)
        phase(first)
        phase(experts)
    return m


def const(m, name):
    c0, n = _C[name]
    return m["cst"][:, c0:c0 + n]


def ahead(m, eng, s, value):
    if isinstance(value, int):
        eng.wait_ge(s, value)
    else:
        value = eng.to_reg(value)
        eng.wait_ge(m["sem"]("cst_in"), 16)
        eng.wait_ge(s, value)


def param(m, name, j=0):
    c = _PAR[name][0] + j
    return m["par"][:, c:c + 1]


def load_inputs(m):
    nc, a, tmp, sem, ps, cst, par, xT = (m[k] for k in ("nc", "a", "tmp", "sem", "ps", "cst", "par", "xT"))
    mix, conv, gdpar = m["mix"], m["conv"], m["gdpar"]
    m["shT"] = shT = tmp("shT", [P, RT_, NS])
    m["cbT"] = cbT = tmp("cbT", [P, QT, NS * 3])
    m["ring"] = ring = tmp("ring", [P, 3, KD, P])
    m["wba"] = wba = tmp("wba", [P, KD, BG])
    m["w2a2"] = w2a2 = tmp("w2a2", [P, 512])
    m["g2"] = g2 = tmp("g2", [P, 512])
    xrow = mix[:].rearrange("p a t -> p (a t)")[:, 0:4 * D].rearrange("p (n d) -> p n d", n=4)
    flat = conv[:].rearrange("p a t -> p (a t)")
    xsrow, shrow, cbrow = flat[0:NS, 0:D], flat[0:NS, D:D + RW_COLS], flat[0:24, 2816:2816 + GD_QKV]
    prow = flat[0:NPAR, 4352:4352 + P]
    x_in, small_in, w_in = sem("x_in"), sem("small_in"), [sem(f"weights{b}") for b in range(3)]
    ba_zero, turned, xT_ready = sem("ba_zero"), sem("turned"), sem("xT_ready")
    ident = const(m, "ident")
    n_small = 0
    with nc.Block() as block:
        @block.sync
        def _(sp):
            sp.dma_start(cst[:], a["consts"]).then_inc(sem("cst_in"), 16)
            for n in range(NT):
                sp.dma_start(xrow[:, n, :], a["x_prompt"][0, n * P:(n + 1) * P, :]).then_inc(x_in, 16)
            for b in range(3):
                sp.dma_start(ring[:, b], a["w_in"][0, :, b * P:(b + 1) * P].rearrange("(k p) c -> p k c", p=P)
                             ).then_inc(w_in[b], 16)

        @block.scalar
        def _(act):
            nonlocal n_small
            act.dma_start(xsrow, a["x_sample"].rearrange("b o d -> (b o) d")).then_inc(small_in, 16)
            act.dma_start(shrow, a["state_rwkv_shift"][0]).then_inc(small_in, 16)
            act.dma_start(cbrow, a["state_gdn_conv"][0].rearrange("b j c -> (b j) c")).then_inc(small_in, 16)
            n_small = 3
            for name, (r0, n) in _PAR.items():
                src = a[name][0]
                if name in ("rwkv_r_k", "gdn_conv_w"):
                    src = src.rearrange("a b -> (a b)")
                act.dma_start(prow[r0:r0 + n, :], src.rearrange("(n c) -> n c", c=P)).then_inc(small_in, 16)
                n_small += 1
            act.dma_start(w2a2[0:64, :], a["rwkv_w2"][0]).then_inc(small_in, 16)
            act.dma_start(w2a2[64:128, :], a["rwkv_a2"][0]).then_inc(small_in, 16)
            act.dma_start(g2[:], a["rwkv_g2"][0]).then_inc(small_in, 16)
            act.dma_start(gdpar[32:36, 0:1], a["gdn_a_log"].rearrange("o h -> h o")).then_inc(small_in, 16)
            act.dma_start(gdpar[32:36, 1:2], a["gdn_dt_bias"].rearrange("o h -> h o")).then_inc(small_in, 16)
            act.wait_ge(ba_zero, 1)
            ba = a["w_in"][0, :, BA0:BA0 + 8].rearrange("(k p) c -> p k c", p=P)
            act.dma_start(wba[:, :, 0:4], ba[:, :, 0:4]).then_inc(small_in, 16)
            act.dma_start(wba[:, :, 32:36], ba[:, :, 4:8]).then_inc(small_in, 16)
            n_small += 7
            for n in range(NT):
                act.wait_ge(turned, n + 1)
                act.activation(xT[:, :, n * P:(n + 1) * P], ps[:, 2 * n:2 * n + 2, :].rearrange("p b (k t) -> p (b k) t", t=P),
                               ACT.Copy).then_inc(xT_ready, 1)

        @block.gpsimd
        def _(pool):
            nc.gpsimd.memset(wba[:], 0.0).then_inc(ba_zero, 1)

        @block.tensor
        def _(pe):
            pe.wait_ge(sem("cst_in"), 16)
            pe.wait_ge(x_in, 16 * NT)
            for n in range(NT):
                for k in range(KD):
                    mm = pe.transpose(ps[:, 2 * n + k // 4, (k % 4) * P:(k % 4 + 1) * P], xrow[:, n, k * P:(k + 1) * P], ident)
                mm.then_inc(turned, 1)
            pe.wait_ge(small_in, 16 * n_small)
            pe.wait_ge(xT_ready, 1)
            for k in range(KD):
                pe.transpose(ps[:, 0, k * NS:(k + 1) * NS], xsrow[:, k * P:(k + 1) * P], ident[0:NS, 0:NS])
            pe.transpose(ps[:, 0, 64:64 + NPAR], prow, ident[0:NPAR, 0:NPAR])
            for j in range(RT_):
                pe.transpose(ps[:, 0, 192 + j * NS:192 + (j + 1) * NS], shrow[:, j * P:(j + 1) * P], ident[0:NS, 0:NS])
            for j in range(QT):
                mm = pe.transpose(ps[:, 1, j * 24:(j + 1) * 24], cbrow[:, j * P:(j + 1) * P], ident[0:24, 0:24])
            mm.then_inc(turned, 1)

        @block.vector
        def _(dve):
            dve.wait_ge(turned, NT + 1)
            done = sem("small_ready")
            dve.tensor_copy(xT[:, :, NP:T], ps[:, 0, 0:64].rearrange("p (k t) -> p k t", t=NS)).then_inc(done, 1)
            dve.tensor_copy(par[:], ps[:, 0, 64:64 + NPAR]).then_inc(done, 1)
            dve.tensor_copy(shT[:], ps[:, 0, 192:192 + RT_ * NS].rearrange("p (k t) -> p k t", t=NS)).then_inc(done, 1)
            dve.tensor_copy(cbT[:], ps[:, 1, 0:24 * QT].rearrange("p (k t) -> p k t", t=24)).then_inc(done, 1)


def half(ap):
    return ap.rearrange("p (h t) -> p h t", h=2)


def project(m):
    nc, a, tmp, sem, ps, par, xT = (m[k] for k in ("nc", "a", "tmp", "sem", "ps", "par", "xT"))
    Praw, mix, conv, kk, scr, shT, cbT, ring, wba, gdpar = (
        m[k] for k in ("Praw", "mix", "conv", "kk", "scr", "shT", "cbT", "ring", "wba", "gdpar"))
    w_in = [sem(f"weights{b}") for b in range(3)]
    tile_done = sem("tile_done")
    tile_out = sem("tile_out")
    ba_done, ba_out, bg_zero, mixed, low_in, conv_ready, silu_ready = (sem(n) for n in (
        "ba_done", "ba_out", "bg_zero", "mixed", "low_in", "conv_ready", "silu_ready"))
    ITS, PER = PT // 6, 6
    m["weights"] = [16 * PT // 3] * 3 + [0]
    bg, omka = m["bg"], m["omka"]
    m["spx"] = tmp("spx", [BG, T])
    m["tail"] = tail = tmp("tail", [P, RT_ + QT, TAIL])
    m["lrk"] = lrk = tmp("lrk", [P, 2, T])
    m["sq"] = sq = Praw[:, 18:26]

    with nc.Block() as block:
        @block.sync
        def _(sp):
            with sp.Fori(0, ITS - 1) as it:
                for t in range(PER):
                    sp.wait_ge(tile_done, it * PER + (t + 1))
                    sp.dma_start(ring[:, t % 3], a["w_in"][0, :, bass.ds(it * (PER * P) + (t + 3) * P, P)]
                                 .rearrange("(k p) c -> p k c", p=P)).then_inc(w_in[t % 3], 16)
            for t in range(PER - 3):
                n = (ITS - 1) * PER + t
                sp.wait_ge(tile_done, n + 1)
                sp.dma_start(ring[:, t % 3], a["w_in"][0, :, (n + 3) * P:(n + 4) * P]
                             .rearrange("(k p) c -> p k c", p=P)).then_inc(w_in[t % 3], 16)

        @block.tensor
        def _(pe):
            with pe.Fori(0, ITS) as it:
                for t in range(PER):
                    pe.wait_ge(w_in[t % 3], it * 32 + 16 * (t // 3 + 1))
                    pe.wait_ge(tile_out, it * PER + (t + 1))
                    for h in range(2):
                        for k in range(KD):
                            mm = pe.matmul(ps[:, 2 * (t % 2) + h, 0:TH], ring[:, t % 3, k, :], xT[:, k, h * TH:(h + 1) * TH],
                                           start=(k == 0), stop=(k == KD - 1))
                    mm.then_inc(tile_done, 1)
            for h in range(2):
                for k in range(KD):
                    mm = pe.matmul(ps[0:BG, 4 + h, 0:TH], wba[:, k, :], xT[:, k, h * TH:(h + 1) * TH],
                                   start=(k == 0), stop=(k == KD - 1))
            mm.then_inc(ba_done, 1)

        @block.scalar
        def _(act):
            act.sem_inc(tile_out, 2)
            with act.Fori(0, ITS) as it:
                for t in range(PER):
                    act.wait_ge(tile_done, it * PER + (t + 1))
                    act.activation(Praw[:, bass.ds(it * PER + t, 1), :].rearrange("p o (h t) -> p (o h) t", h=2),
                                   ps[:, 2 * (t % 2):2 * (t % 2) + 2, 0:TH], ACT.Copy).then_inc(tile_out, 1)
            act.wait_ge(mixed, 1)
            act.activation(lrk[0:64, 0], mix[0:64, 12], ACT.Tanh).then_inc(low_in, 1)
            act.activation(lrk[64:128, 0], mix[64:128, 12], ACT.Copy).then_inc(low_in, 1)
            act.activation(lrk[:, 1], mix[:, 13], ACT.Sigmoid).then_inc(low_in, 1)
            act.wait_ge(ba_done, 1)
            act.wait_ge(bg_zero, 1)
            act.activation(half(bg[0:4, :]), ps[0:4, 4:6, 0:TH], ACT.Sigmoid).then_inc(ba_out, 1)
            act.activation(half(bg[32:36, :]), ps[32:36, 4:6, 0:TH], ACT.Identity, bias=gdpar[32:36, 1:2]).then_inc(ba_out, 1)
            act.wait_ge(conv_ready, 1)
            for n in range(3):
                act.activation(conv[:, 4 * n:4 * n + 4, :], conv[:, 4 * n:4 * n + 4, :], ACT.Silu).then_inc(silu_ready, 1)

        @block.gpsimd
        def _(pool):
            nc.gpsimd.memset(bg[:], 0.0).then_inc(bg_zero, 1)

        @block.vector
        def _(dve):
            st = Steps(dve, sem("dve_step"))
            dve.wait_ge(tile_out, 2 + RT_)
            st.did(dve.tensor_tensor(mix[:, :, 1:NP], Praw[:, 0:RT_, 0:NP - 1], Praw[:, 0:RT_, 1:NP], ALU.subtract))
            st.did(dve.tensor_scalar(mix[:, :, 0:1], Praw[:, 0:RT_, 0:1], -1.0, None, ALU.mult))
            st.did(dve.tensor_tensor(mix[:, :, NP:T], shT[:], Praw[:, 0:RT_, NP:T], ALU.subtract))
            c0 = _PAR["rwkv_k_a"][0]
            st.did(dve.tensor_scalar(omka[:], par[:, c0:c0 + 4], -1.0, 1.0, ALU.mult, ALU.add))
            st.settled()
            for j in range(RT_):
                st.did(dve.scalar_tensor_tensor(out=mix[:, j], in0=mix[:, j], scalar=param(m, "rwkv_mu", j), in1=Praw[:, j],
                                                op0=ALU.mult, op1=ALU.add))
            st.settled()
            dve.sem_inc(mixed, 1)
            for j in range(4):
                st.did(dve.tensor_scalar(kk[:, j], mix[:, 4 + j], param(m, "rwkv_k_k", j), None, ALU.mult))
            st.settled()
            st.did(dve.tensor_tensor(scr[:], kk[:], kk[:], ALU.mult))
            for j in range(QT):
                r = Praw[:, RT_ + j]
                dve.wait_ge(tile_out, 2 + RT_ + j + 1)
                st.link(dve.tensor_scalar(conv[:, j, :], r, param(m, "gdn_conv_w", 3 * QT + j), None, ALU.mult))
                for back in (1, 2, 3):
                    tap = 3 - back
                    w = param(m, "gdn_conv_w", tap * QT + j)
                    st.did(dve.scalar_tensor_tensor(out=conv[:, j, back:NP], in0=r[:, 0:NP - back], scalar=w,
                                                    in1=conv[:, j, back:NP], op0=ALU.mult, op1=ALU.add))
                    st.link(dve.scalar_tensor_tensor(out=conv[:, j, NP:T], in0=cbT[:, j, tap:24:3], scalar=w,
                                                     in1=conv[:, j, NP:T], op0=ALU.mult, op1=ALU.add))
            dve.sem_inc(conv_ready, 1)
            st.did(dve.tensor_copy(tail[:], Praw[:, 0:RT_ + QT, NP - 3:T]))
            st.settled()
            for n in range(2):
                dve.wait_ge(silu_ready, n + 1)
                st.did(dve.tensor_tensor(sq[:, 4 * n:4 * n + 4], conv[:, 4 * n:4 * n + 4], conv[:, 4 * n:4 * n + 4], ALU.mult))
            st.settled()
            m["dve"] = st.n


def tokenwise(m):
    nc, a, sem, ps, par = (m[k] for k in ("nc", "a", "sem", "ps", "par"))
    Praw, mix, conv, kk, scr, w2a2, g2, gdpar, bg, spx, tail, omka, lrk, sq = (m[k] for k in (
        "Praw", "mix", "conv", "kk", "scr", "w2a2", "g2", "gdpar", "bg", "spx", "tail", "omka", "lrk", "sq"))
    ones, blk64, ident, eps = (const(m, n) for n in ("ones", "blk64", "ident", "eps"))
    m["sw"], m["aa"], m["gg"] = sw, aa, gg = Praw[:, 0:4], Praw[:, 4:8], Praw[:, 8:12]
    m["G"], m["Gi"], m["Gp"] = G, Gi, Gp = Praw[:, 14:18], Praw[:, 18:22], Praw[:, 22:26]
    Gend = m["Gend"]
    tailrow = m["tmp"]("tailrow", [TAIL, RW_COLS + GD_QKV])
    norm_mm, root, low_mm, low_out, tail_mm, tail_out, spl_in, spl, cum_ready, exps, bon_in, bon_mm, bon_out, out = (
        sem(n) for n in ("norm_mm", "root", "low_mm", "low_out", "tail_mm", "tail_out", "spl_in", "spl", "cum_ready",
                         "exps", "bon_in", "bon_mm", "bon_out", "saved"))
    bank2 = lambda b: ps[:, b:b + 2, 0:TH]
    TAILS = ((0, 8), (8, 16), (16, 24), (24, 26))

    with nc.Block() as block:
        @block.sync
        def _(sp):
            sp.dma_start(a["s_conv"][0, :, 0:2, :], a["state_gdn_conv"][0, :, 1:3, :]).then_inc(out, 16)
            sp.wait_ge(tail_out, 4)
            sp.dma_start(a["p_shift"][0], tailrow[2:3, 0:RW_COLS]).then_inc(out, 16)
            sp.dma_start(a["s_shift"][0], tailrow[3:11, 0:RW_COLS]).then_inc(out, 16)
            sp.dma_start(a["p_conv"][0, 0], tailrow[0:3, RW_COLS:]).then_inc(out, 16)
            sp.dma_start(a["s_conv"][0, :, 2, :], tailrow[3:11, RW_COLS:]).then_inc(out, 16)
            sp.wait_ge(out, m["saved"] + 16 * 5)
            m["saved"] += 16 * 5

        @block.tensor
        def _(pe):
            for n in range(12):
                if n >= 2:
                    pe.wait_ge(root, n - 1)
                w, x = (blk64, scr[:, n]) if n < 4 else (ones, sq[:, n - 4])
                for h in range(2):
                    mm = pe.matmul(ps[:, 2 * (n % 2) + h, 0:TH], w, x[:, h * TH:(h + 1) * TH], start=True, stop=True)
                mm.then_inc(norm_mm, 1)
            for n in range(12):
                j, kind = n // 3, n % 3
                if n >= 2:
                    pe.wait_ge(low_out, n - 1)
                w = (w2a2[0:64], w2a2[64:128], g2[:])[kind]
                r = (lrk[0:64, 0], lrk[64:128, 0], lrk[:, 1])[kind]
                for h in range(2):
                    mm = pe.matmul(ps[:, 4 + 2 * (n % 2) + h, 0:TH], w[:, j * P:(j + 1) * P], r[:, h * TH:(h + 1) * TH],
                                   start=True, stop=True)
                mm.then_inc(low_mm, 1)
            pe.wait_ge(root, 12)
            for n, (j0, j1) in enumerate(TAILS):
                if n >= 2:
                    pe.wait_ge(tail_out, n - 1)
                for j in range(j0, j1):
                    mm = pe.transpose(ps[0:TAIL, 2 * (n % 2) + (j - j0) // 4, (j % 4) * P:(j % 4 + 1) * P], tail[:, j, :], ident)
                mm.then_inc(tail_mm, 1)
            pe.wait_ge(bon_in, 1)
            pe.wait_ge(low_out, 12)
            for n in range(4):
                if n >= 2:
                    pe.wait_ge(bon_out, n - 1)
                for h in range(2):
                    mm = pe.matmul(ps[:, 4 + 2 * (n % 2) + h, 0:TH], blk64, scr[:, n, h * TH:(h + 1) * TH], start=True, stop=True)
                mm.then_inc(bon_mm, 1)

        @block.scalar
        def _(act):
            for n in range(12):
                act.wait_ge(norm_mm, n + 1)
                d, e = (scr[:, n], EPS_KK) if n < 4 else (sq[:, n - 4], EPS_GD)
                act.activation(half(d), bank2(2 * (n % 2)), ACT.Sqrt, bias=eps[:, e:e + 1]).then_inc(root, 1)
            for n in range(12):
                j, kind = n // 3, n % 3
                act.wait_ge(low_mm, n + 1)
                dst = half((sw, aa, gg)[kind][:, j, :])
                if kind < 2:
                    ins = act.activation(dst, bank2(4 + 2 * (n % 2)), ACT.Sigmoid, bias=param(m, ("rwkv_w0", "rwkv_a0")[kind], j))
                else:
                    ins = act.activation(dst, bank2(4 + 2 * (n % 2)), ACT.Copy)
                ins.then_inc(low_out, 1)
            act.wait_ge(cum_ready, 1)
            act.activation(Gi[:, :, 0:NP], G[:, :, 0:NP], ACT.Exp, scale=DECAY).then_inc(exps, 1)
            act.wait_ge(exps, 1)
            act.activation(G[:, :, 0:NP], G[:, :, 0:NP], ACT.Exp, scale=-DECAY).then_inc(exps, 1)
            act.activation(Gp[:, :, 0:NP], Gp[:, :, 0:NP], ACT.Exp, scale=-DECAY).then_inc(exps, 1)
            act.activation(G[:, :, NP:T], sw[:, :, NP:T], ACT.Exp, scale=-DECAY).then_inc(exps, 1)
            act.wait_ge(spl_in, 1)
            act.activation(spx[32:36, :], spx[32:36, :], ACT.Exp, scale=-1.0).then_inc(spl, 1)
            act.activation(gdpar[32:36, 2:3], gdpar[32:36, 0:1], ACT.Exp).then_inc(spl, 1)
            act.wait_ge(spl, 2)
            act.activation(spx[32:36, :], spx[32:36, :], ACT.Ln, bias=1.0).then_inc(spl, 1)

        @block.vector
        def _(dve):
            st = Steps(dve, sem("dve_step"), m["dve"])
            st.link(dve.tensor_scalar(spx[32:36, :], bg[32:36, :], -1.0, None, ALU.mult))
            st.did(dve.tensor_tensor(spx[32:36, :], spx[32:36, :], bg[32:36, :], ALU.max))
            st.settled()
            st.link(dve.tensor_scalar(bg[32:36, :], bg[32:36, :], 0.0, None, ALU.max))
            dve.sem_inc(spl_in, 1)
            dve.wait_ge(root, 4)
            st.link(dve.reciprocal(scr[:], scr[:]))
            st.link(dve.tensor_tensor(kk[:], kk[:], scr[:], ALU.mult))
            dve.wait_ge(root, 12)
            st.link(dve.reciprocal(sq[:], sq[:]))
            st.did(dve.tensor_tensor(conv[:, 4:8], conv[:, 4:8], sq[:, 4:8], ALU.mult))
            st.did(dve.scalar_tensor_tensor(out=conv[:, 0:4], in0=conv[:, 0:4], scalar=CG ** -0.5, in1=sq[:, 0:4],
                                            op0=ALU.mult, op1=ALU.mult))
            st.settled()
            dve.wait_ge(low_out, 12)
            for j in range(4):
                st.did(dve.tensor_tensor_scan(G[:, j, 0:NP], const(m, "keep64"), sw[:, j, 0:NP], 0.0, ALU.mult, ALU.add))
            st.settled()
            dve.tensor_tensor(Gp[:, :, 0:NP], G[:, :, 0:NP], sw[:, :, 0:NP], ALU.subtract).then_inc(cum_ready, 1)
            for j in range(4):
                st.did(dve.tensor_scalar(scr[:, j], aa[:, j], param(m, "rwkv_k_a", j), omka[:, j:j + 1], ALU.mult, ALU.add))
            st.settled()
            k2 = mix[:, 4:8]
            st.did(dve.tensor_tensor(k2, k2, scr[:], ALU.mult))
            st.did(dve.tensor_tensor(aa, aa, kk[:], ALU.mult))
            st.settled()
            for j in range(4):
                st.did(dve.scalar_tensor_tensor(out=scr[:, j], in0=mix[:, j], scalar=param(m, "rwkv_r_k", j), in1=k2[:, j],
                                                op0=ALU.mult, op1=ALU.mult))
            st.settled()
            dve.sem_inc(bon_in, 1)
            for n, (j0, j1) in enumerate(TAILS):
                dve.wait_ge(tail_mm, n + 1)
                b = 2 * (n % 2)
                if n < 3:
                    ins = dve.tensor_copy(tailrow[:, j0 * P:j1 * P].rearrange("p (b c) -> p b c", b=2), ps[0:TAIL, b:b + 2, :])
                else:
                    ins = dve.tensor_copy(tailrow[:, j0 * P:j1 * P], ps[0:TAIL, b, 0:2 * P])
                ins.then_inc(tail_out, 1)
            dve.wait_ge(exps, 4)
            st.did(dve.scalar_tensor_tensor(out=Gp[:, :, 0:NP], in0=Gp[:, :, 0:NP], scalar=-1.0, in1=kk[:, :, 0:NP],
                                            op0=ALU.mult, op1=ALU.mult))
            st.did(dve.tensor_tensor(aa[:, :, 0:NP], aa[:, :, 0:NP], Gi[:, :, 0:NP], ALU.mult))
            st.did(dve.tensor_tensor(k2[:, :, 0:NP], k2[:, :, 0:NP], Gi[:, :, 0:NP], ALU.mult))
            st.did(dve.tensor_tensor(mix[:, 0:4, 0:NP], mix[:, 0:4, 0:NP], G[:, :, 0:NP], ALU.mult))
            st.did(dve.tensor_copy(Gend[:], G[:, :, 63:NP:64]))
            for n in range(4):
                dve.wait_ge(bon_mm, n + 1)
                dve.tensor_tensor(half(scr[:, n]), bank2(4 + 2 * (n % 2)), half(mix[:, 8 + n]), ALU.mult).then_inc(bon_out, 1)
            dve.wait_ge(spl, 3)
            st.link(dve.tensor_tensor(bg[32:36, :], bg[32:36, :], spx[32:36, :], ALU.add))
            st.link(dve.tensor_scalar(spx[32:36, :], bg[32:36, :], gdpar[32:36, 2:3], -1.0, ALU.mult, ALU.mult))
            st.did(dve.tensor_tensor_scan(bg[32:36, 0:NP], const(m, "keep128")[32:36], spx[32:36, 0:NP], 0.0, ALU.mult, ALU.add))
            st.did(dve.tensor_copy(bg[32:36, NP:T], spx[32:36, NP:T]))
            st.settled()
            m["dve"] = st.n


def sample_rows(m):
    nc, a, sem, ps, tmp = (m[k] for k in ("nc", "a", "sem", "ps", "tmp"))
    mix, conv, kk, bg, G, aa = (m[k] for k in ("mix", "conv", "kk", "bg", "G", "aa"))
    ident = const(m, "ident")
    RWROW, GDROW = 6 * 512, GD_QKV + BG
    srow = tmp("srow", [NS, RWROW + GDROW])
    tiles = [src[:, j, NP:T] for src in (mix[:, 0:4], G, mix[:, 4:8], mix[:, 8:12], kk, aa) for j in range(4)]
    tiles += [conv[:, j, NP:T] for j in range(QT)]
    rows_mm, rows_out, rows_saved = sem("rows_mm"), sem("rows_out"), sem("saved")
    rounds = [(c, min(c + 2 * 512, RWROW + GD_QKV)) for c in range(0, RWROW + GD_QKV, 2 * 512)]
    m["RWROW"] = RWROW

    with nc.Block() as block:
        @block.tensor
        def _(pe):
            for n, (c0, c1) in enumerate(rounds):
                if n >= 4:
                    pe.wait_ge(rows_out, n - 3)
                for c in range(c0, c1, P):
                    mm = pe.transpose(ps[0:NS, 2 * (n % 4) + (c - c0) // 512, (c - c0) % 512:(c - c0) % 512 + P],
                                      tiles[c // P], ident)
                mm.then_inc(rows_mm, 1)
            pe.wait_ge(rows_out, len(rounds))
            pe.transpose(ps[0:NS, 0, 0:BG], bg[:, NP:T], ident[0:BG, 0:BG]).then_inc(rows_mm, 1)

        @block.vector
        def _(dve):
            for n, (c0, c1) in enumerate(rounds):
                dve.wait_ge(rows_mm, n + 1)
                for h in range((c1 - c0) // 512):
                    ins = dve.tensor_copy(srow[:, c0 + 512 * h:c0 + 512 * (h + 1)], ps[0:NS, 2 * (n % 4) + h, :])
                ins.then_inc(rows_out, 1)
            dve.wait_ge(rows_mm, len(rounds) + 1)
            dve.tensor_copy(srow[:, RWROW + GD_QKV:], ps[0:NS, 0, 0:BG]).then_inc(rows_out, 1)

        @block.sync
        def _(sp):
            sp.wait_ge(rows_out, len(rounds) + 1)
            sp.dma_start(a["rows_rw"].rearrange("q (b h) c -> b q (h c)", b=NS),
                         srow[:, 0:RWROW].rearrange("b (q c) -> b q c", q=6)).then_inc(rows_saved, 16)
            sp.dma_start(a["rows_gd"].rearrange("q (b h) c -> b q (h c)", b=NS),
                         srow[:, RWROW:RWROW + GD_QKV].rearrange("b (q c) -> b q c", q=3)).then_inc(rows_saved, 16)
            for n, c in enumerate((0, 32)):
                sp.dma_start(a["rows_bg"][n].rearrange("(b h) -> b h", b=NS),
                             srow[:, RWROW + GD_QKV + c:RWROW + GD_QKV + c + HG]).then_inc(rows_saved, 16)
            sp.wait_ge(rows_saved, m["saved"] + 64)
            m["saved"] += 64


def recur(m):
    nc, a, sem, ps, tmp = (m[k] for k in ("nc", "a", "sem", "ps", "tmp"))
    Praw, mix, conv, kk, bg, Gend = (m[k] for k in ("Praw", "mix", "conv", "kk", "bg", "Gend"))
    ident, pair, incl, sel = (const(m, n) for n in ("ident", "pair", "incl", "sel"))
    selv = sel.rearrange("p (h c) -> p h c", c=P)
    over4 = lambda ap: ap.unsqueeze(1).to_broadcast([P, 4, ap.shape[1]])
    flat = lambda ap, n: ap.rearrange("p a t -> p (a t)")[:, 0:n]
    AT, BT, KT, RT, VT = m["Gp"], m["aa"], mix[:, 4:8], mix[:, 0:4], mix[:, 8:12]
    oTr, oTg = m["oTr"], m["oTg"] = m["Gp"], conv[:, 0:4]
    AR = flat(Praw[:, 12:14], 1024).rearrange("p (j k t) -> p j k t", j=4, k=2)
    BK = flat(mix[:, 12:14], 1024).rearrange("p (j k t) -> p j k t", j=4, k=2)
    TTm = flat(m["sw"], 1536).rearrange("p (g h t) -> p g h t", g=3, h=4)
    TM = flat(m["Gi"], 1536).rearrange("p (g h t) -> p g h t", g=3, h=4)
    X = flat(m["G"], 1536).rearrange("p (g h t) -> p g h t", g=3, h=4)
    LM = flat(kk[:], 1536).rearrange("p (g h t) -> p g h t", g=3, h=4)
    VS, QKV, bgS = tmp("VS", [P, 4, P]), tmp("QKV", [P, QT, P]), tmp("bgS", [BG, P])
    Vt, Kt, Bt = tmp("Vt", [P, 512]), tmp("Kt", [P, 512]), tmp("Bt", [P, 512])
    rest = lambda ap: ap.rearrange("p a t -> p (a t)")[:, 1536:2048].rearrange("p (h t) -> p h t", h=4)
    gvt, gkd, kE, LG = rest(m["sw"]), rest(m["Gi"]), rest(m["G"]), rest(kk[:])
    bgt, E, qE = tmp("bgt", [P, BG]), tmp("E", [P, 4, P]), tmp("qE", [P, 4, P])
    dc, eC = tmp("dc", [P, 4]), tmp("eC", [P, 4])
    PR = tmp("PR", [P, HR, 4, P])
    W, U, gW, gU = tmp("W", [P, 512]), VS[:].rearrange("p j t -> p (j t)"), QKV[:, 8:12], QKV[:, 0:4]
    ST, S = tmp("ST", [P, 2, 4, 64]), tmp("S", [P, 4, P])
    wkv = W[0:64].rearrange("p (j k) -> p j k", j=4)
    LT = [PR[:, 0:4, 0], PR[:, 4:8, 0], LG]
    LEVELS = (2, 4, 8, 16, 32, 64)
    order = [(l, g) for l in range(6) for g in range(3) if l < 5 or g == 2]
    idx = {lg: n for n, lg in enumerate(order)}
    last = {0: 4, 1: 4, 2: 5}
    NL = len(order)
    K = dict(st_a=3, st_p=4, turn=3, tok=3, e_in=2, e_out=3, gv=1, pairs=3, pr=2, lg=1, intra=1, tt0=3, t_mm=3, t0=3,
             lm=NL, x_mm=NL, x_ev=NL, xt_mm=NL, upd=NL, wv_mm=1, wv=1, as_mm=2, w_ok=2, u_mm=2, u_ok=2, s_mm=2, s_ok=2,
             ost_mm=2, ost=4, ouv_mm=2, o_ok=2, gw_mm=1, gw=1, gu_mm=1, gu=1, go_mm=1, go=1, gs_mm=1, gs=1,
             bgt_ok=1, gkd_ok=1, qe=1, ke=1, ec=1)
    S_ = {n: sem("r_" + n) for n in K}

    def wait(eng, it, name, n):
        eng.wait_ge(S_[name], it * K[name] + n)

    def wait_ahead(eng, it, signal):
        ahead(m, eng, S_[signal[0]], it * K[signal[0]] + signal[1])

    tcols = lambda it: bass.ds(it * P, P)

    with nc.Block() as block:
        @block.scalar
        def _(act):
            cp = lambda o, i: act.activation(o, i, ACT.Copy)
            with act.Fori(0, NT) as it:
                wait_ahead(act, it, ("ouv_mm", 0))
                cp(AR[:, :, 0], AT[:, :, tcols(it)]).then_inc(S_["st_a"], 1)
                cp(AR[:, :, 1], RT[:, :, tcols(it)]).then_inc(S_["st_a"], 1)
                cp(VS[:], VT[:, :, tcols(it)]).then_inc(S_["st_a"], 1)
                wait(act, it, "turn", 1)
                for n, o in enumerate((Vt, Kt, Bt)):
                    cp(o[:], ps[:, n, :]).then_inc(S_["tok"], 1)
                wait(act, it, "e_in", 2)
                act.activation(kE, ps[:, 7, :].rearrange("p (h t) -> p h t", h=4), ACT.Exp).then_inc(S_["e_out"], 1)
                act.activation(E[:], E[:], ACT.Exp).then_inc(S_["e_out"], 1)
                act.activation(dc[:], dc[:], ACT.Exp).then_inc(S_["e_out"], 1)
                for g in range(3):
                    wait(act, it, "t_mm", g + 1)
                    cp(TM[:, g], ps[:, 3 + g, :].rearrange("p (h t) -> p h t", h=4)).then_inc(S_["t0"], 1)

                def x_evac(n):
                    g = order[n][1]
                    wait(act, it, "x_mm", n + 1)
                    cp(X[:, g], ps[:, g, :].rearrange("p (h t) -> p h t", h=4)).then_inc(S_["x_ev"], 1)

                for n in range(NL):
                    x_evac(n)
                wait(act, it, "wv_mm", 1)
                cp(W[:], ps[:, 0, :]).then_inc(S_["wv"], 1)

                def u_evac(c):
                    wait(act, it, "u_mm", c + 1)
                    cp(U[64 * c:64 * c + 64, :], ps[64 * c:64 * c + 64, 2, :]).then_inc(S_["u_ok"], 1)

                def o_evac(c):
                    wait_ahead(act, it, ("ost_mm", c + 1))
                    for par, b in ((0, 1), (1, 5)):
                        r = slice(64 * par, 64 * par + 64)
                        cp(oTr[r, :, bass.ds(it * P + 64 * c, 64)], ps[r, b, 256:512].rearrange("p (j t) -> p j t", j=4)
                           ).then_inc(S_["ost"], 1)

                u_evac(0)
                wait(act, it, "gu_mm", 1)
                cp(gU, ps[:, 7, :].rearrange("p (h t) -> p h t", h=4)).then_inc(S_["gu"], 1)
                o_evac(0)
                wait_ahead(act, it, ("go_mm", 1))
                cp(oTg[:, :, tcols(it)], ps[:, 6, :].rearrange("p (h t) -> p h t", h=4)).then_inc(S_["go"], 1)
                u_evac(1)
                o_evac(1)

        @block.gpsimd
        def _(pool):
            cp = nc.gpsimd.tensor_copy
            nc.gpsimd.memset(ST[:], 0.0).then_inc(sem("r_zero"), 1)
            nc.gpsimd.memset(S[:], 0.0).then_inc(sem("r_zero"), 1)
            with pool.Fori(0, NT) as it:
                wait(pool, it, "ouv_mm", 0)
                cp(BK[:, :, 0], BT[:, :, tcols(it)]).then_inc(S_["st_p"], 1)
                cp(BK[:, :, 1], KT[:, :, tcols(it)]).then_inc(S_["st_p"], 1)
                cp(QKV[:], conv[:, :, tcols(it)]).then_inc(S_["st_p"], 1)
                cp(bgS[:], bg[:, tcols(it)]).then_inc(S_["st_p"], 1)
                for n, (l, g) in enumerate(order):
                    if l == 0:
                        wait(pool, it, "tt0", g + 1)
                    else:
                        wait(pool, it, "x_mm", idx[l - 1, g] + 1)
                    nc.gpsimd.tensor_tensor(LM[:, g], LT[g], over4(const(m, f"lvl{LEVELS[l]}")), ALU.mult
                                            ).then_inc(S_["lm"], 1)

        @block.vector
        def _(dve):
            st = Steps(dve, sem("r_dve"))
            by4 = lambda b: ps[:, b, :].rearrange("p (h t) -> p h t", h=4)
            percol = lambda ap: ap.unsqueeze(2).to_broadcast([P, 4, P])
            KS = 10
            dve.wait_ge(sem("r_zero"), 2)
            with dve.Fori(0, NT) as it:
                st.n, st.base = 0, it * KS
                wait(dve, it, "turn", 2)
                dve.tensor_copy(bgt[:], ps[:, 5, 0:BG]).then_inc(S_["bgt_ok"], 1)
                wait(dve, it, "bgt_ok", 1)
                dve.tensor_tensor(gvt, by4(3), percol(bgt[:, 0:4]), ALU.mult).then_inc(S_["gv"], 1)
                wait(dve, it, "turn", 3)
                st.did(dve.tensor_tensor(E[:], by4(7), percol(bgt[:, 32:36]), ALU.subtract))
                dve.tensor_tensor(dc[:], by4(7)[:, :, P - 1], bgt[:, 32:36], ALU.subtract).then_inc(S_["e_in"], 1)
                st.settled()
                dve.tensor_scalar(E[:], E[:], 0.0, None, ALU.min).then_inc(S_["e_in"], 1)
                wait(dve, it, "e_out", 3)
                dve.tensor_tensor(gkd, by4(4), percol(dc[:]), ALU.mult).then_inc(S_["gkd_ok"], 1)
                dve.tensor_tensor(qE[:], QKV[:, 0:4], kE, ALU.mult).then_inc(S_["qe"], 1)
                dve.tensor_copy(eC[:], kE[:, :, P - 1]).then_inc(S_["ec"], 1)
                wait(dve, it, "qe", 1)
                wait(dve, it, "ec", 1)
                st.link(dve.scalar_tensor_tensor(out=kE, in0=kE, scalar=-1.0, in1=QKV[:, 4:8], op0=ALU.mult, op1=ALU.mult))
                dve.tensor_tensor(kE, kE, by4(6), ALU.mult).then_inc(S_["ke"], 1)
                wait(dve, it, "pairs", 1)
                mask = pair.unsqueeze(1).to_broadcast([P, 8, 2 * P])
                prv = lambda h0: PR[:, h0:h0 + 4].rearrange("p h (x k) t -> p (h x) (k t)", x=2)
                dve.tensor_tensor(prv(0), ps[:, 0:4, :].rearrange("p h (x c) -> p (h x) c", x=2), mask, ALU.mult
                                  ).then_inc(S_["pr"], 1)
                wait(dve, it, "pairs", 2)
                st.link(dve.scalar_tensor_tensor(out=LG, in0=by4(4), scalar=-1.0, in1=E[:], op0=ALU.mult, op1=ALU.mult))
                dve.tensor_tensor(LG, LG, by4(6), ALU.mult).then_inc(S_["lg"], 1)
                st.link(dve.tensor_tensor(E[:], E[:], over4(incl), ALU.mult))
                dve.tensor_tensor(E[:], E[:], by4(5), ALU.mult).then_inc(S_["intra"], 1)
                wait(dve, it, "pairs", 3)
                dve.tensor_tensor(prv(4), ps[:, 4:8, :].rearrange("p h (x c) -> p (h x) c", x=2), mask, ALU.mult
                                  ).then_inc(S_["pr"], 1)
                for g in range(3):
                    wait(dve, it, *(("pr", 1), ("pr", 2), ("lg", 1))[g])
                    st.link(dve.tensor_tensor(LM[:, g], LT[g], over4(const(m, "lvl1")), ALU.mult))
                    dve.tensor_tensor(TTm[:, g], LM[:, g], over4(ident), ALU.add).then_inc(S_["tt0"], 1)
                for n, (l, g) in enumerate(order):
                    wait(dve, it, "xt_mm", n + 1)
                    if l < last[g]:
                        dve.tensor_tensor(TM[:, g], TM[:, g], by4(3 + g), ALU.add)
                    dve.tensor_tensor(TTm[:, g], TTm[:, g], by4(g), ALU.add).then_inc(S_["upd"], 1)

                def w_add(c):
                    wait(dve, it, "as_mm", c + 1)
                    wait(dve, it, "wv", 1)
                    r = slice(64 * c, 64 * c + 64)
                    for par, b in ((0, 1), (1, 5)):
                        w = W[r].rearrange("p (j q v) -> p j q v", j=4, q=2)[:, :, par]
                        ins = dve.tensor_tensor(w, w, ps[r, b, 0:256].rearrange("p (j v) -> p j v", j=4), ALU.add)
                        if par:
                            ins.then_inc(S_["w_ok"], 1)
                        else:
                            ins.then_inc(sem("r_w_even"), 1)

                def state(c):
                    wait(dve, it, "s_mm", c + 1)
                    st.link(dve.tensor_tensor(ST[:, 1 - c], ST[:, c], ps[:, 3, 0:256].rearrange("p (j v) -> p j v", j=4), ALU.add))
                    ge = Gend[:, :, bass.ds(it * 2 + c, 1)].to_broadcast([P, 4, 64])
                    dve.tensor_tensor(ST[:, 1 - c], ST[:, 1 - c], ge, ALU.mult).then_inc(S_["s_ok"], 1)

                def o_add(c):
                    wait(dve, it, "ouv_mm", c + 1)
                    wait(dve, it, "ost", 2 * c + 2)
                    o = oTr[:, :, bass.ds(it * P + 64 * c, 64)]
                    dve.tensor_tensor(o, o, ps[:, 4, 0:256].rearrange("p (j t) -> p j t", j=4), ALU.add).then_inc(S_["o_ok"], 1)

                w_add(0)
                wait(dve, it, "gw_mm", 1)
                dve.tensor_tensor(gW, gvt, by4(6), ALU.add).then_inc(S_["gw"], 1)
                state(0)
                o_add(0)
                wait(dve, it, "gs_mm", 1)
                st.link(dve.tensor_tensor(S[:], S[:], percol(eC[:]), ALU.mult))
                dve.tensor_tensor(S[:], S[:], by4(7), ALU.add).then_inc(S_["gs"], 1)
                w_add(1)
                state(1)
                o_add(1)
                assert st.n == KS, st.n
            st.n, st.base = 0, 0
            dve.wait_ge(sem("wkv_mm"), 1)
            dve.tensor_copy(wkv, ps[0:64, 0, :].rearrange("p (j k) -> p j k", j=4)).then_inc(sem("wkv_ok"), 1)

        @block.tensor
        def _(pe):
            by4 = lambda b: ps[:, b, :].rearrange("p (h t) -> p h t", h=4)
            pe.wait_ge(sem("r_zero"), 2)
            with pe.Fori(0, NT) as it:
                wait(pe, it, "o_ok", 0)
                wait(pe, it, "go", 0)
                wait(pe, it, "gs", 0)
                wait(pe, it, "s_ok", 0)
                wait(pe, it, "st_a", 3)
                wait(pe, it, "st_p", 4)
                for n, src in enumerate((VS[:], BK[:, :, 1], BK[:, :, 0])):
                    for j in range(4):
                        mm = pe.transpose(ps[:, n, j * P:(j + 1) * P], src[:, j], ident)
                mm.then_inc(S_["turn"], 1)
                for n, j0 in ((3, 8), (4, 4)):
                    for j in range(4):
                        pe.transpose(ps[:, n, j * P:(j + 1) * P], QKV[:, j0 + j], ident)
                pe.transpose(ps[:, 5, 0:BG], bgS[:], ident[0:BG, 0:BG]).then_inc(S_["turn"], 1)
                for n in range(8):
                    mm = pe.matmul(ps[:, 6 + n // 4, (n % 4) * P:(n % 4 + 1) * P], selv[0:BG, n], bgS[:], start=True, stop=True)
                mm.then_inc(S_["turn"], 1)

                def pairs(h0, b0):
                    for h in range(h0, h0 + 4):
                        r, j = slice(64 * (h % 2), 64 * (h % 2) + 64), h // 2
                        ar = AR[r, j].rearrange("p k t -> p (k t)")
                        pe.matmul(ps[:, b0 + h - h0, 0:256], BK[r, j, 0], ar, start=True, stop=True)
                        mm = pe.matmul(ps[:, b0 + h - h0, 256:512], BK[r, j, 1], ar, start=True, stop=True)
                    mm.then_inc(S_["pairs"], 1)

                wait(pe, it, "tok", 3)
                wait(pe, it, "gv", 1)
                pairs(0, 0)
                wait(pe, it, "gkd_ok", 1)
                for h in range(4):
                    pe.matmul(by4(4)[:, h], QKV[:, 4 + h], QKV[:, 4 + h], start=True, stop=True)
                    mm = pe.matmul(by4(5)[:, h], QKV[:, 4 + h], QKV[:, h], start=True, stop=True)
                mm.then_inc(S_["pairs"], 1)
                wait(pe, it, "lg", 1)
                wait(pe, it, "intra", 1)
                wait(pe, it, "ke", 1)
                pairs(4, 4)
                for g in range(3):
                    wait(pe, it, "tt0", g + 1)
                    if g == 0:
                        wait(pe, it, "pr", 2)
                    for h in range(4):
                        mm = pe.transpose(by4(3 + g)[:, h], TTm[:, g, h], ident)
                    mm.then_inc(S_["t_mm"], 1)

                def x_mm(n):
                    l, g = order[n]
                    wait(pe, it, "lm", n + 1)
                    if l == 0:
                        wait(pe, it, "t0", g + 1)
                    else:
                        wait(pe, it, "upd", idx[l - 1, g] + 1)
                    for h in range(4):
                        mm = pe.matmul(by4(g)[:, h], LM[:, g, h], TM[:, g, h], start=True, stop=True)
                    mm.then_inc(S_["x_mm"], 1)

                def xt_mm(n):
                    l, g = order[n]
                    wait(pe, it, "x_ev", n + 1)
                    for h in range(4):
                        if l < last[g]:
                            pe.matmul(by4(3 + g)[:, h], TTm[:, g, h], X[:, g, h], start=True, stop=True)
                        mm = pe.matmul(by4(g)[:, h], X[:, g, h], TTm[:, g, h], start=True, stop=True)
                    mm.then_inc(S_["xt_mm"], 1)

                for l in range(5):
                    for g in range(3):
                        x_mm(idx[l, g])
                    for g in range(3):
                        xt_mm(idx[l, g])
                x_mm(idx[5, 2])
                wait(pe, it, "upd", idx[4, 2] + 1)
                for h in range(HR):
                    mm = pe.matmul(ps[:, 0, h * 64:(h + 1) * 64], PR[:, h, 2], Vt[:, h * 64:(h + 1) * 64], start=True, stop=True)
                mm.then_inc(S_["wv_mm"], 1)

                def a_state(c):
                    if c == 1:
                        wait_ahead(pe, it, ("s_ok", 1))
                    for par, b in ((0, 1), (1, 5)):
                        r = slice(64 * par, 64 * par + 64)
                        for j in range(4):
                            mm = pe.matmul(ps[64 * c:64 * c + 64, b, j * 64:(j + 1) * 64], AR[r, j, 0, 64 * c:64 * c + 64],
                                           ST[r, c, j], start=True, stop=True)
                    mm.then_inc(S_["as_mm"], 1)

                def chunk(c):
                    r = slice(64 * c, 64 * c + 64)
                    wait_ahead(pe, it, ("w_ok", c + 1))
                    for h in range(HR):
                        mm = pe.matmul(ps[r, 2, h * 64:(h + 1) * 64], TTm[r, h // 4, h % 4, 64 * c:64 * c + 64],
                                       W[r, h * 64:(h + 1) * 64], start=True, stop=True)
                    mm.then_inc(S_["u_mm"], 1)

                def chunk_state(c):
                    r = slice(64 * c, 64 * c + 64)
                    wait_ahead(pe, it, ("u_ok", c + 1))
                    for h in range(HR):
                        o = ps[64 * (h % 2):64 * (h % 2) + 64, 3, (h // 2) * 64:(h // 2 + 1) * 64]
                        hc = slice(h * 64, (h + 1) * 64)
                        pe.matmul(o, Bt[r, hc], U[r, hc], start=True, stop=False)
                        mm = pe.matmul(o, Kt[r, hc], Vt[r, hc], start=False, stop=True)
                    mm.then_inc(S_["s_mm"], 1)
                    for par, b in ((0, 1), (1, 5)):
                        q = slice(64 * par, 64 * par + 64)
                        for j in range(4):
                            mm = pe.matmul(ps[q, b, 256 + j * 64:256 + (j + 1) * 64], ST[q, c, j], AR[q, j, 1, 64 * c:64 * c + 64],
                                           start=True, stop=True)
                    mm.then_inc(S_["ost_mm"], 1)
                    if c == 1:
                        wait_ahead(pe, it, ("o_ok", 1))
                    for h in range(HR):
                        o = ps[64 * (h % 2):64 * (h % 2) + 64, 4, (h // 2) * 64:(h // 2 + 1) * 64]
                        hc, tc = slice(h * 64, (h + 1) * 64), slice(64 * c, 64 * c + 64)
                        pe.matmul(o, U[r, hc], PR[r, h, 1, tc], start=True, stop=False)
                        mm = pe.matmul(o, Vt[r, hc], PR[r, h, 3, tc], start=False, stop=True)
                    mm.then_inc(S_["ouv_mm"], 1)

                a_state(0)
                for h in range(4):
                    mm = pe.matmul(by4(6)[:, h], kE[:, h], S[:, h], start=True, stop=True)
                mm.then_inc(S_["gw_mm"], 1)
                xt_mm(idx[5, 2])
                wait(pe, it, "gw", 1)
                wait(pe, it, "upd", NL)
                for h in range(4):
                    mm = pe.matmul(by4(7)[:, h], TTm[:, 2, h], gW[:, h], start=True, stop=True)
                mm.then_inc(S_["gu_mm"], 1)
                chunk(0)
                chunk_state(0)
                wait(pe, it, "gu", 1)
                wait(pe, it, "ost", 2)
                for h in range(4):
                    pe.matmul(by4(6)[:, h], S[:, h], qE[:, h], start=True, stop=False)
                    mm = pe.matmul(by4(6)[:, h], gU[:, h], E[:, h], start=False, stop=True)
                mm.then_inc(S_["go_mm"], 1)
                for h in range(4):
                    mm = pe.matmul(by4(7)[:, h], gkd[:, h], gU[:, h], start=True, stop=True)
                mm.then_inc(S_["gs_mm"], 1)
                a_state(1)
                chunk(1)
                chunk_state(1)
            pe.wait_ge(S_["s_ok"], 2 * NT)
            pe.wait_ge(S_["upd"], NL * NT)
            pe.wait_ge(S_["wv"], NT)
            for j in range(4):
                mm = pe.transpose(ps[0:64, 0, j * P:(j + 1) * P], ST[:, 0, j], ident)
            mm.then_inc(sem("wkv_mm"), 1)

        @block.sync
        def _(sp):
            done = sem("saved")
            sp.wait_ge(sem("wkv_ok"), 1)
            sp.dma_start(a["p_wkv"][0, 0].rearrange("h v k -> v h k"), wkv.rearrange("v j (q k) -> v (j q) k", q=2)
                         ).then_inc(done, 16)
            sp.wait_ge(S_["gs"], NT)
            sp.dma_start(a["p_ssm"][0, 0].rearrange("h k v -> k h v"), S[:]).then_inc(done, 16)
            sp.wait_ge(done, m["saved"] + 32)
            m["saved"] += 32


def sample_recur(m):
    nc, a, sem, ps, tmp = (m[k] for k in ("nc", "a", "sem", "ps", "tmp"))
    oTr, oTg, ident, sum4 = m["oTr"], m["oTg"], const(m, "ident"), const(m, "sum4")
    SR, TR, rv, vh = tmp("SR", [P, 32, CR]), tmp("TR", [P, 32, CR]), tmp("rv", [P, 6, CR]), tmp("vh", [P, 32])
    TG = m["mix"][:, 0:8].rearrange("p a t -> p (a t)")[:, 0:32 * CG].rearrange("p (k v) -> p k v", k=32)
    SG, gqk, gv, gb = tmp("SG", [P, 32, CG]), tmp("gqk", [P, 2, 32]), tmp("gv", [P, CG]), tmp("gb", [P, 3])
    sa, oR, part, dl, oG = tmp("sa", [P, 32]), tmp("oR", [P, 32]), tmp("part", [P, CG]), tmp("dl", [P, CG]), tmp("oG", [P, CG])
    oRrow = tmp("oRrow", [NS, 512])
    rin, gin, o_back = sem("s_rin"), sem("s_gin"), sem("s_oback")
    new_rw, new_gd, o_ready, part_ready, sum_mm, saved = (sem(n) for n in (
        "s_new_rw", "s_new_gd", "s_o_ready", "s_part", "s_sum", "saved"))
    NB = NS * HG
    with nc.Block() as block:
        @block.sync
        def _(sp):
            for v in range(2):
                p = slice(64 * v, 64 * v + 64)
                sp.dma_start(SR[p], a["state_rwkv_wkv"][0].rearrange("b h v k -> (b h) v k")[:, 32 * v:32 * v + 32]).then_inc(rin, 16)
                sp.dma_start(rv[p], a["rows_rw"].rearrange("q p c -> p q c")).then_inc(rin, 16)
                sp.dma_start(vh[p], a["rows_rw"][3][:, 32 * v:32 * v + 32]).then_inc(rin, 16)
            for k in range(4):
                p = slice(NB * k, NB * k + NB)
                sp.dma_start(SG[p], a["state_gdn_ssm"][0].rearrange("b h k v -> (b h) k v")[:, 32 * k:32 * k + 32]).then_inc(gin, 16)
                sp.dma_start(gqk[p], a["rows_gd"][0:2, :, 32 * k:32 * k + 32].rearrange("q p c -> p q c")).then_inc(gin, 16)
                sp.dma_start(gv[p], a["rows_gd"][2]).then_inc(gin, 16)
                with nc.allow_non_contiguous_dma(reason="64 numbers"):
                    sp.dma_start(gb[p, 0:2], a["rows_bg"].rearrange("q p -> p q")).then_inc(gin, 16)
            sp.wait_ge(new_rw, 1)
            for v in range(2):
                p = slice(64 * v, 64 * v + 64)
                sp.dma_start(a["s_wkv"][0].rearrange("b h v k -> (b h) v k")[:, 32 * v:32 * v + 32], SR[p]).then_inc(saved, 16)
            sp.wait_ge(o_ready, 1)
            for v in range(2):
                sp.dma_start(a["o_rw"][:, 32 * v:32 * v + 32], oR[64 * v:64 * v + 64]).then_inc(o_back, 16)
            sp.wait_ge(o_back, 32)
            sp.dma_start(oRrow[:], a["o_rw"].rearrange("(b h) c -> b (h c)", b=NS)).then_inc(o_back, 16)
            sp.wait_ge(new_gd, 1)
            for k in range(4):
                p = slice(NB * k, NB * k + NB)
                sp.dma_start(a["s_ssm"][0].rearrange("b h k v -> (b h) k v")[:, 32 * k:32 * k + 32], SG[p]).then_inc(saved, 16)
            sp.wait_ge(saved, m["saved"] + 16 * 6)
            m["saved"] += 16 * 6

        @block.scalar
        def _(act):
            act.wait_ge(gin, 16 * 16)
            act.activation(gb[:, 2:3], gb[:, 1:2], ACT.Exp).then_inc(sem("s_decay"), 1)

        @block.tensor
        def _(pe):
            for n in range(2):
                pe.wait_ge(part_ready, n + 1)
                pe.matmul(ps[:, n, 0:CG], sum4, part[:], start=True, stop=True).then_inc(sum_mm, 1)
            pe.wait_ge(sem("s_oG"), 1)
            pe.transpose(ps[:, 2, 0:NB], oG[0:NB, :], ident[0:NB, 0:NB]).then_inc(sum_mm, 1)
            pe.wait_ge(o_back, 48)
            for j in range(4):
                mm = pe.transpose(ps[:, 3, j * NS:(j + 1) * NS], oRrow[:, j * P:(j + 1) * P], ident[0:NS, 0:NS])
            mm.then_inc(sum_mm, 1)

        @block.vector
        def _(dve):
            st = Steps(dve, sem("dve_step"), m["dve"])
            TT = lambda o, x, y, op: st.link(dve.tensor_tensor(o, x, y, op))
            keys = lambda n: rv[:, n].unsqueeze(1).to_broadcast([P, 32, CR])
            vals = lambda ap: ap.unsqueeze(2).to_broadcast([P, 32, CR])
            dve.wait_ge(rin, 16 * 6)
            TT(TR[:], SR[:], keys(4), ALU.mult)
            st.did(dve.tensor_reduce(sa[:], TR[:], AXX, ALU.add))
            TT(SR[:], SR[:], keys(1), ALU.mult)
            TT(TR[:], vals(sa[:]), keys(5), ALU.mult)
            TT(SR[:], SR[:], TR[:], ALU.subtract)
            TT(TR[:], vals(vh[:]), keys(2), ALU.mult)
            TT(SR[:], SR[:], TR[:], ALU.add)
            dve.sem_inc(new_rw, 1)
            TT(TR[:], SR[:], keys(0), ALU.mult)
            st.link(dve.tensor_reduce(oR[:], TR[:], AXX, ALU.add))
            dve.sem_inc(o_ready, 1)
            dve.wait_ge(sem("s_decay"), 1)
            gk = lambda n: gqk[:, n].unsqueeze(2).to_broadcast([P, 32, CG])
            gvv = lambda ap: ap.unsqueeze(1).to_broadcast([P, 32, CG])
            st.link(dve.tensor_scalar(SG[:], SG[:], gb[:, 2:3], None, ALU.mult))
            TT(TG, SG[:], gk(1), ALU.mult)
            dve.tensor_reduce(part[:], TG.rearrange("p k v -> p v k"), AXX, ALU.add).then_inc(part_ready, 1)
            dve.wait_ge(sum_mm, 1)
            TT(dl[:], gv[:], ps[:, 0, 0:CG], ALU.subtract)
            st.link(dve.tensor_scalar(dl[:], dl[:], gb[:, 0:1], None, ALU.mult))
            TT(TG, gk(1), gvv(dl[:]), ALU.mult)
            TT(SG[:], SG[:], TG, ALU.add)
            dve.sem_inc(new_gd, 1)
            TT(TG, SG[:], gk(0), ALU.mult)
            dve.tensor_reduce(part[:], TG.rearrange("p k v -> p v k"), AXX, ALU.add).then_inc(part_ready, 1)
            dve.wait_ge(sum_mm, 2)
            dve.tensor_copy(oG[:], ps[:, 1, 0:CG]).then_inc(sem("s_oG"), 1)
            dve.wait_ge(sum_mm, 4)
            st.did(dve.tensor_copy(oTg[:, :, NP:T], ps[:, 2, 0:NB].rearrange("p (b h) -> p h b", b=NS)))
            st.did(dve.tensor_copy(oTr[:, :, NP:T], ps[:, 3, 0:4 * NS].rearrange("p (j b) -> p j b", j=4)))
            st.settled()
            m["dve"] = st.n


def normalise(m):
    nc, a, sem, ps, tmp, par = (m[k] for k in ("nc", "a", "sem", "ps", "tmp", "par"))
    oTr, oTg, gg, Bv, z = m["oTr"], m["oTg"], m["gg"], m["scr"], m["Praw"][:, 26:30]
    mix = m["mix"]
    sqr, sqg, zs = mix[:, 0:4], mix[:, 4:8], mix[:, 8:12]
    blk64, ones, eps = const(m, "blk64"), const(m, "ones"), const(m, "eps")
    mm_, out = sem("n_mm"), sem("n_out")
    with nc.Block() as block:
        @block.tensor
        def _(pe):
            for n in range(12):
                if n >= 4:
                    pe.wait_ge(out, n - 3)
                kind, j = n // 4, n % 4
                if kind == 0:
                    pe.wait_ge(sem("n_sqg"), 1)
                if kind == 2:
                    pe.wait_ge(sem("n_sqr"), j + 1)
                w, x = ((ones, sqg), (blk64, oTr), (blk64, sqr))[kind]
                for h in range(2):
                    mm = pe.matmul(ps[:, 2 * (n % 4) + h, 0:TH], w, x[:, j, h * TH:(h + 1) * TH], start=True, stop=True)
                mm.then_inc(mm_, 1)

        @block.scalar
        def _(act):
            act.activation(zs, z, ACT.Silu).then_inc(sem("n_z"), 1)
            for n in (0, 1, 2, 3, 8, 9, 10, 11):
                act.wait_ge(mm_, n + 1)
                if n >= 8:
                    act.wait_ge(out, n)
                d, w, e = (sqg, CG, EPS_GD) if n < 4 else (sqr, CR, EPS_GN)
                act.activation(half(d[:, n % 4]), ps[:, 2 * (n % 4):2 * (n % 4) + 2, 0:TH], ACT.Sqrt, scale=1.0 / w,
                               bias=eps[:, e:e + 1]).then_inc(out, 1)

        @block.vector
        def _(dve):
            st = Steps(dve, sem("dve_step"), m["dve"])
            dve.tensor_tensor(sqg, oTg, oTg, ALU.mult).then_inc(sem("n_sqg"), 1)
            for j in range(4):
                dve.wait_ge(mm_, 5 + j)
                dve.wait_ge(out, 4 + j)
                dve.scalar_tensor_tensor(out=half(oTr[:, j]), in0=ps[:, 2 * j:2 * j + 2, 0:TH], scalar=-1.0 / CR,
                                         in1=half(oTr[:, j]), op0=ALU.mult, op1=ALU.add).then_inc(out, 1)
                dve.wait_ge(out, 5 + j)
                dve.tensor_tensor(sqr[:, j], oTr[:, j], oTr[:, j], ALU.mult).then_inc(sem("n_sqr"), 1)
            st.link(dve.reciprocal(sqg, sqg))
            st.link(dve.tensor_tensor(oTg, oTg, sqg, ALU.mult))
            dve.wait_ge(sem("n_z"), 1)
            st.did(dve.scalar_tensor_tensor(out=oTg, in0=oTg, scalar=param(m, "gdn_norm_w"), in1=zs, op0=ALU.mult, op1=ALU.mult))
            dve.wait_ge(out, 12)
            st.link(dve.reciprocal(sqr, sqr))
            st.link(dve.tensor_tensor(oTr, oTr, sqr, ALU.mult))
            for j in range(4):
                st.did(dve.tensor_scalar(oTr[:, j], oTr[:, j], param(m, "rwkv_ln_w", j), param(m, "rwkv_ln_b", j), ALU.mult, ALU.add))
            st.settled()
            st.link(dve.tensor_tensor(oTr, oTr, Bv[:], ALU.add))
            st.link(dve.tensor_tensor(oTr, oTr, gg, ALU.mult))
            m["dve"] = st.n


def merge(m):
    nc, a, sem, ps, tmp, par, xT = (m[k] for k in ("nc", "a", "sem", "ps", "tmp", "par", "xT"))
    oTr, oTg = m["oTr"], m["oTg"]
    merged = m["mix"][:, 0:KD]
    WG, WB, WO = tmp("WG", [P, 2, 2, KD, P]), tmp("WB", [P, 2, 2, 4, P]), tmp("WO", [P, 2, KD, P])
    ga, gb = tmp("gate_a", [P, T]), tmp("gate_b", [P, T])
    w_ready, wo_ready = [sem(f"weights{b}") for b in range(2)], [sem(f"weights{b}") for b in (2, 3)]
    base, base_o = [m["weights"][b] for b in range(2)], [m["weights"][b] for b in (2, 3)]
    mm_done, gate_out, ya_out, y_out, t_sum, o_mm, o_out = (sem("m_" + n) for n in (
        "mm", "gate", "ya", "y", "sum", "o_mm", "o_out"))

    with nc.Block() as block:
        @block.sync
        def _(sp):
            def load(b, col, first):
                for n, (src, c) in enumerate(((a["w_in"], GATE0), (a["w_in"], GATE0 + D))):
                    sp.dma_start(WG[:, b, n], src[0, :, bass.ds(col + c, P)].rearrange("(k p) c -> p k c", p=P)).then_inc(w_ready[b], 16)
                for n, src in enumerate((a["w_branch_a"], a["w_branch_b"])):
                    sp.dma_start(WB[:, b, n], src[0, :, bass.ds(col, P)].rearrange("(k p) c -> p k c", p=P)).then_inc(w_ready[b], 16)

            load(0, 0, True)
            load(1, P, True)
            for b in range(2):
                sp.dma_start(WO[:, b], a["w_out"][0, :, b * P:(b + 1) * P].rearrange("(k p) c -> p k c", p=P)).then_inc(wo_ready[b], 16)
            with sp.Fori(0, KD // 2 - 1) as it:
                for b in range(2):
                    sp.wait_ge(mm_done, it * 8 + (4 * b + 4))
                    load(b, it * (2 * P) + (2 + b) * P, False)
            with sp.Fori(0, KD // 2 - 1) as it:
                for b in range(2):
                    sp.wait_ge(o_mm, it * 2 + (b + 1))
                    sp.dma_start(WO[:, b], a["w_out"][0, :, bass.ds(it * (2 * P) + (2 + b) * P, P)]
                                 .rearrange("(k p) c -> p k c", p=P)).then_inc(wo_ready[b], 16)

        @block.tensor
        def _(pe):
            with pe.Fori(0, KD // 2) as it:
                for b in range(2):
                    pe.wait_ge(w_ready[b], it * 64 + (base[b] + 64))
                    for n in range(4):
                        pe.wait_ge((gate_out, gate_out, ya_out, y_out)[n], it * (4 if n < 2 else 2) + ((2 * b + n) if n < 2 else b))
                        kn, w, x = ((KD, WG[:, b, 0], xT), (KD, WG[:, b, 1], xT), (4, WB[:, b, 0], oTr), (4, WB[:, b, 1], oTg))[n]
                        for h in range(2):
                            for k in range(kn):
                                mm = pe.matmul(ps[:, 2 * n + h, 0:TH], w[:, k], x[:, k, h * TH:(h + 1) * TH],
                                               start=(k == 0), stop=(k == kn - 1))
                        mm.then_inc(mm_done, 1)
            pe.wait_ge(t_sum, KD)
            with pe.Fori(0, KD // 2) as it:
                for b in range(2):
                    pe.wait_ge(wo_ready[b], it * 16 + (base_o[b] + 16))
                    pe.wait_ge(o_out, it * 2 + b)
                    for h in range(2):
                        for k in range(KD):
                            mm = pe.matmul(ps[:, 2 * b + h, 0:TH], WO[:, b, k], merged[:, k, h * TH:(h + 1) * TH],
                                           start=(k == 0), stop=(k == KD - 1))
                    mm.then_inc(o_mm, 1)

        @block.scalar
        def _(act):
            with act.Fori(0, KD // 2) as it:
                for b in range(2):
                    for n, g in enumerate((ga, gb)):
                        act.wait_ge(mm_done, it * 8 + (4 * b + n + 1))
                        act.wait_ge(t_sum, it * 2 + b)
                        act.activation(half(g[:]), ps[:, 2 * n:2 * n + 2, 0:TH], ACT.Sigmoid).then_inc(gate_out, 1)

        @block.vector
        def _(dve):
            with dve.Fori(0, KD // 2) as it:
                for b in range(2):
                    dve.wait_ge(mm_done, it * 8 + (4 * b + 3))
                    dve.wait_ge(gate_out, it * 4 + (2 * b + 2))
                    dve.tensor_tensor(half(ga[:]), half(ga[:]), ps[:, 4:6, 0:TH], ALU.mult).then_inc(ya_out, 1)
                    dve.wait_ge(mm_done, it * 8 + (4 * b + 4))
                    dve.tensor_tensor(half(gb[:]), half(gb[:]), ps[:, 6:8, 0:TH], ALU.mult).then_inc(y_out, 1)
                    dve.wait_ge(ya_out, it * 2 + (b + 1))
                    dve.wait_ge(y_out, it * 2 + (b + 1))
                    dve.tensor_tensor(merged[:, bass.ds(it * 2 + b, 1)], ga[:].unsqueeze(1), gb[:].unsqueeze(1), ALU.add
                                      ).then_inc(t_sum, 1)
            with dve.Fori(0, KD // 2) as it:
                for b in range(2):
                    dve.wait_ge(o_mm, it * 2 + (b + 1))
                    xt = xT[:, bass.ds(it * 2 + b, 1)].rearrange("p o (h t) -> p (o h) t", h=2)
                    dve.scalar_tensor_tensor(out=xt, in0=xt, scalar=ALPHA, in1=ps[:, 2 * b:2 * b + 2, 0:TH],
                                             op0=ALU.mult, op1=ALU.add).then_inc(o_out, 1)
    m["weights"] = [w + n * KD // 2 for w, n in zip(m["weights"], (64, 64, 16, 16))]


def norm1(m):
    nc, sem, ps, tmp, xT = (m[k] for k in ("nc", "sem", "ps", "tmp", "xT"))
    ones, eps = const(m, "ones"), const(m, "eps")
    sq, rt = tmp("n1_sq", [P, KD, T]), tmp("n1_rt", [P, T])
    mm_, centred, squared, rooted = (sem("n1_" + n) for n in ("mm", "centred", "squared", "rooted"))
    hs = [slice(h * TH, (h + 1) * TH) for h in range(2)]
    with nc.Block() as block:
        @block.tensor
        def _(pe):
            for h in range(2):
                for k in range(KD):
                    mm = pe.matmul(ps[:, h, 0:TH], ones, xT[:, k, hs[h]], start=(k == 0), stop=(k == KD - 1))
                mm.then_inc(mm_, 1)
            for h in range(2):
                pe.wait_ge(squared, h + 1)
                for k in range(KD):
                    mm = pe.matmul(ps[:, 2 + h, 0:TH], ones, sq[:, k, hs[h]], start=(k == 0), stop=(k == KD - 1))
                mm.then_inc(mm_, 1)

        @block.scalar
        def _(act):
            for h in range(2):
                act.wait_ge(centred, h + 1)
                act.activation(sq[:, :, hs[h]], xT[:, :, hs[h]], ACT.Square).then_inc(squared, 1)
            for h in range(2):
                act.wait_ge(mm_, 3 + h)
                act.activation(rt[:, hs[h]], ps[:, 2 + h, 0:TH], ACT.Sqrt, scale=1.0 / D, bias=eps[:, EPS_LN:EPS_LN + 1]
                               ).then_inc(rooted, 1)

        @block.vector
        def _(dve):
            st = Steps(dve, sem("dve_step"), m["dve"])
            over = lambda ap: ap.unsqueeze(1).to_broadcast([P, KD, TH])
            for h in range(2):
                dve.wait_ge(mm_, h + 1)
                dve.scalar_tensor_tensor(out=xT[:, :, hs[h]], in0=over(ps[:, h, 0:TH]), scalar=-1.0 / D, in1=xT[:, :, hs[h]],
                                         op0=ALU.mult, op1=ALU.add).then_inc(centred, 1)
            for h in range(2):
                dve.wait_ge(rooted, h + 1)
                dve.wait_ge(squared, 2)
                st.link(dve.reciprocal(rt[:, hs[h]], rt[:, hs[h]]))
                st.link(dve.tensor_tensor(xT[:, :, hs[h]], xT[:, :, hs[h]], over(rt[:, hs[h]]), ALU.mult))
            for k in range(KD):
                st.did(dve.tensor_scalar(xT[:, k], xT[:, k], param(m, "ln1_g", k), param(m, "ln1_b", k), ALU.mult, ALU.add))
            st.settled()
            m["dve"] = st.n


HP = 16
NK = 128
TK = 16
PH = 8
TILES = [(n * P, P) for n in range(NT)] + [(NP, NS)]


def query(m):
    nc, a, sem, ps, tmp, xT = (m[k] for k in ("nc", "a", "sem", "ps", "tmp", "xT"))
    R = 4
    ring, qT = tmp("q_ring", [P, R, KD, P]), tmp("qT", [P, HP, T])
    keys, keysT = tmp("keys", [P, HP, P]), tmp("keysT", [P, HP, NK])
    scores = m["scores"]
    w_in, k_in, k_mm, k_out = [sem(f"weights{b}") for b in range(R)], sem("q_kin"), sem("q_kmm"), sem("q_kout")
    q_mm, q_out, s_mm, s_out = (sem("q_" + n) for n in ("mm", "out", "smm", "sout"))
    base = m["weights"]

    with nc.Block() as block:
        @block.sync
        def _(sp):
            wq = a["peer_wq"]
            for b in range(R):
                sp.dma_start(ring[:, b], wq[0, :, b * P:(b + 1) * P].rearrange("(k p) c -> p k c", p=P)).then_inc(w_in[b], 16)
            sp.dma_start(keys[:], a["peer_subkeys"][0].rearrange("h q n c -> n (h q) c")).then_inc(k_in, 16)
            with sp.Fori(0, HP // R - 1) as it:
                for b in range(R):
                    sp.wait_ge(q_mm, it * R + (b + 1))
                    sp.dma_start(ring[:, b], wq[0, :, bass.ds(it * (R * P) + (R + b) * P, P)].rearrange("(k p) c -> p k c", p=P)
                                 ).then_inc(w_in[b], 16)

        @block.tensor
        def _(pe):
            with pe.Fori(0, HP // R) as it:
                for b in range(R):
                    pe.wait_ge(w_in[b], it * 16 + (base[b] + 16))
                    pe.wait_ge(q_out, it * R + (b + 1))
                    for h in range(2):
                        for k in range(KD):
                            mm = pe.matmul(ps[:, 2 * (b % 2) + h, 0:TH], ring[:, b, k], xT[:, k, h * TH:(h + 1) * TH],
                                           start=(k == 0), stop=(k == KD - 1))
                    mm.then_inc(q_mm, 1)
            pe.wait_ge(k_in, 16)
            for j in range(HP):
                mm = pe.transpose(ps[:, 4 + j // 4, (j % 4) * P:(j % 4 + 1) * P], keys[:, j], const(m, "ident"))
            mm.then_inc(k_mm, 1)
            pe.wait_ge(k_out, 1)
            pe.wait_ge(q_out, 2 + HP)
            for n, (t0, tn) in enumerate(TILES):
                if n >= 2:
                    pe.wait_ge(s_out, n - 1)
                for j in range(HP):
                    mm = pe.matmul(ps[0:tn, 4 * (n % 2) + j // 4, (j % 4) * P:(j % 4 + 1) * P], qT[:, j, t0:t0 + tn],
                                   keysT[:, j], start=True, stop=True)
                mm.then_inc(s_mm, 1)

        @block.gpsimd
        def _(pool):
            nc.gpsimd.memset(scores[:, NT * HP:], 0.0).then_inc(sem("q_zero"), 1)

        @block.scalar
        def _(act):
            act.sem_inc(q_out, 2)
            act.wait_ge(sem("q_zero"), 1)
            with act.Fori(0, HP // R) as it:
                for b in range(R):
                    act.wait_ge(q_mm, it * R + (b + 1))
                    act.activation(qT[:, bass.ds(it * R + b, 1), :].rearrange("p o (h t) -> p (o h) t", h=2),
                                   ps[:, 2 * (b % 2):2 * (b % 2) + 2, 0:TH], ACT.Copy).then_inc(q_out, 1)
            act.wait_ge(k_mm, 1)
            act.activation(keysT[:].rearrange("p (b j) n -> p b (j n)", b=4), ps[:, 4:8, :], ACT.Copy).then_inc(k_out, 1)
            for n, (t0, tn) in enumerate(TILES):
                act.wait_ge(s_mm, n + 1)
                act.activation(scores[0:tn, n * HP:(n + 1) * HP].rearrange("p (b j) n -> p b (j n)", b=4),
                               ps[0:tn, 4 * (n % 2):4 * (n % 2) + 4, :], ACT.Copy).then_inc(s_out, 1)


def first(m):
    nc, a, sem, ps, tmp, xT, scores = (m[k] for k in ("nc", "a", "sem", "ps", "tmp", "xT", "scores"))
    x1row = tmp("x1row", [P, 2, D])
    parts, left2 = tmp("parts", [P, 2, 3, D], BF16), tmp("left", [P, 2, D])
    r_mm, r_out, p_out, saved = (sem(n) for n in ("x1_mm", "x1_out", "x1_parts", "saved"))
    sel_done, turned, taken, tops, exps = (sem("sel_" + n) for n in ("done", "turned", "taken", "tops", "exps"))
    base = m["saved"]
    with nc.Block() as block:
        @block.tensor
        def _(pe):
            for n, (t0, tn) in enumerate(TILES):
                if n >= 2:
                    pe.wait_ge(r_out, n - 1)
                for k in range(KD):
                    mm = pe.transpose(ps[0:tn, 2 * (n % 2) + k // 4, (k % 4) * P:(k % 4 + 1) * P], xT[:, k, t0:t0 + tn],
                                      const(m, "ident"))
                mm.then_inc(r_mm, 1)
            pe.wait_ge(sel_done, 2)
            turn_chosen(m, pe, 4)

        @block.scalar
        def _(act):
            for n, (t0, tn) in enumerate(TILES):
                act.wait_ge(r_mm, n + 1)
                if n >= 2:
                    act.wait_ge(saved, base + 64 * (n - 1))
                act.activation(x1row[0:tn, n % 2].rearrange("p (b c) -> p b c", b=2), ps[0:tn, 2 * (n % 2):2 * (n % 2) + 2, :],
                               ACT.Copy).then_inc(r_out, 1)
                if n < 2:
                    choose_exp(m, act, n)
            act.wait_ge(turned, 1)
            act.activation(m["idxT"][:, 0:P], ps[:, 4, 0:P], ACT.Copy).then_inc(taken, 1)
            act.activation(m["gateT"][:, 0:P], ps[:, 5, 0:P], ACT.Copy).then_inc(taken, 1)

        @block.gpsimd
        def _(pool):
            st = Steps(pool, sem("x1_pool"))
            for n, (t0, tn) in enumerate(TILES):
                pool.wait_ge(r_out, n + 1)
                src, left = x1row[0:tn, n % 2], left2[0:tn, n % 2]
                for q in range(3):
                    st.link(nc.gpsimd.tensor_copy(parts[0:tn, n % 2, q], src))
                    if q < 2:
                        st.link(nc.gpsimd.tensor_tensor(left, src, parts[0:tn, n % 2, q], ALU.subtract))
                        src = left
                pool.sem_inc(p_out, 1)

        @block.sync
        def _(sp):
            for n, (t0, tn) in enumerate(TILES):
                sp.wait_ge(p_out, n + 1)
                sp.dma_start(a["x1_rows"][t0:t0 + tn, :], x1row[0:tn, n % 2]).then_inc(saved, 16)
                for q in range(3):
                    sp.dma_start(a["x1_parts"][q, t0:t0 + tn, :], parts[0:tn, n % 2, q]).then_inc(saved, 16)
                sp.wait_ge(saved, base + 64 * (n + 1))
            m["saved"] = base + 64 * len(TILES)

        @block.vector
        def _(dve):
            st = Steps(dve, sem("dve_step"), m["dve"])
            for n in range(2):
                for k in range(32):
                    choose(m, dve, st, k // 4, k % 4, n, 8 * n, 4 * n)
            m["dve"] = st.n


CH = 4
LOWEST = -3.0e38


def choose_buffers(m, sb):
    for name, shape, dt in (("work", [P, 2 * CH, NK], F32), ("top", [P, 2 * CH, TK], F32), ("topi", [P, 2 * CH, TK], U32),
                            ("topf", [P, 2 * CH, TK], F32), ("cand", [P, CH, TK * TK], F32), ("one", [P, CH, TK, TK], F32),
                            ("best", [P, CH, TK], F32), ("besti", [P, CH, TK], U32), ("pos", [P, 2, CH, TK], U32),
                            ("posf", [P, 2, CH, TK], F32), ("pair_ids", [P, 2, CH, TK], F32), ("ex", [P, CH, TK], F32),
                            ("exsum", [P, CH], F32), ("ids", [P, PH, TK], F32), ("gates", [P, PH, TK], F32)):
        m["c_" + name] = sb("c_" + name, shape, dt)


def choose(m, dve, st, stage, part, n, row, head):
    sem = m["sem"]
    (work, top, topi, topf, cand, one, best, besti, pos, posf, pair_ids, ex, exsum, ids, gates) = (m["c_" + k][:] for k in (
        "work", "top", "topi", "topf", "cand", "one", "best", "besti", "pos", "posf", "pair_ids", "ex", "exsum", "ids", "gates"))
    full = [P, CH, TK, TK]
    iota = const(m, "iota16").unsqueeze(1).unsqueeze(1).to_broadcast(full)
    keys = topf.rearrange("p (h q) k -> p h q k", q=2)
    pair = (2 * part, 2 * part + 1)
    r = part

    def settled():
        ahead(m, dve, st.sem, st.base + st.n)

    def link(ins):
        st.did(ins)
        settled()

    if stage == 0:
        if part == 0:
            link(dve.tensor_copy(work, m["scores"][:, bass.ds(row, 2 * CH)]))
        for k in pair:
            st.did(dve.max(top[:, k, 0:8], work[:, k]))
        settled()
    elif stage == 1:
        for k in pair:
            st.did(dve.max_index(topi[:, k, 0:8], top[:, k, 0:8], work[:, k]))
        settled()
    elif stage == 2:
        for k in pair:
            st.did(dve.match_replace(work[:, k], top[:, k, 0:8], work[:, k], LOWEST))
        settled()
    elif stage == 3:
        for k in pair:
            st.did(dve.max(top[:, k, 8:16], work[:, k]))
        settled()
    elif stage == 4:
        for k in pair:
            st.did(dve.max_index(topi[:, k, 8:16], top[:, k, 8:16], work[:, k]))
        h = slice(part, part + 1)
        v = top[:, 2 * part:2 * part + 2].rearrange("p (h q) k -> p h q k", q=2)
        st.did(dve.tensor_tensor(cand[:, h].rearrange("p h (i j) -> p h i j", i=TK),
                                 v[:, :, 0].unsqueeze(3).to_broadcast([P, 1, TK, TK]),
                                 v[:, :, 1].unsqueeze(2).to_broadcast([P, 1, TK, TK]), ALU.add))
        settled()
        if part == 3:
            link(dve.tensor_copy(topf, topi))
    elif stage == 5:
        link(dve.max(best[:, r, 0:8], cand[:, r]))
        link(dve.max_index(besti[:, r, 0:8], best[:, r, 0:8], cand[:, r]))
        link(dve.match_replace(cand[:, r], best[:, r, 0:8], cand[:, r], LOWEST))
    elif stage == 6:
        link(dve.max(best[:, r, 8:16], cand[:, r]))
        link(dve.max_index(besti[:, r, 8:16], best[:, r, 8:16], cand[:, r]))
        if part == 3:
            dve.tensor_tensor(ex, best, best[:, :, 0:1].to_broadcast([P, CH, TK]), ALU.subtract).then_inc(sem("sel_tops"), 1)
            st.did(dve.tensor_scalar(pos[:, 0], besti, 4, None, ALU.logical_shift_right))
            st.did(dve.tensor_scalar(pos[:, 1], besti, 15, None, ALU.bitwise_and))
            settled()
            link(dve.tensor_copy(posf, pos))
    elif stage == 7:
        q = part // 2
        if part % 2 == 0:
            link(dve.tensor_tensor(one, posf[:, q].unsqueeze(3).to_broadcast(full), iota, ALU.is_equal))
            link(dve.tensor_tensor(one, one, keys[:, :, q].unsqueeze(2).to_broadcast(full), ALU.mult))
        else:
            link(dve.tensor_reduce(pair_ids[:, q], one, AXX, ALU.add))
        if part == 3:
            st.did(dve.scalar_tensor_tensor(out=ids[:, bass.ds(head, CH)], in0=pair_ids[:, 0], scalar=float(NK),
                                            in1=pair_ids[:, 1], op0=ALU.mult, op1=ALU.add))
            ahead(m, dve, sem("sel_exps"), n + 1)
            link(dve.tensor_reduce(exsum, ex, AXX, ALU.add))
            link(dve.reciprocal(exsum, exsum))
            link(dve.tensor_tensor(gates[:, bass.ds(head, CH)], ex, exsum.unsqueeze(2).to_broadcast([P, CH, TK]), ALU.mult))
            dve.sem_inc(sem("sel_done"), 1)


def choose_exp(m, act, n):
    act.wait_ge(m["sem"]("sel_tops"), n + 1)
    act.activation(m["c_ex"][:], m["c_ex"][:], ACT.Exp).then_inc(m["sem"]("sel_exps"), 1)


def turn_chosen(m, pe, bank):
    for q, name in enumerate(("c_ids", "c_gates")):
        mm = pe.transpose(m["ps"][:, bank + q, 0:P], m[name][:].rearrange("p h k -> p (h k)"), const(m, "ident"))
    mm.then_inc(m["sem"]("sel_turned"), 1)


STEP, GROUP = 32, 16
RU, RV = 8, 16
BATCH = 4
UB = 2
LEAD = 8


def experts(m):
    assert LEAD == RU == NS and LEAD % BATCH == 0
    nc, a, sem, ps, tmp, idxT, gateT = (m[k] for k in ("nc", "a", "sem", "ps", "tmp", "idxT", "gateT"))
    U, V = tmp("U_rows", [P, RU, D]), tmp("V_rows", [P, RV, D])
    ixs, gs = tmp("ixs", [P, 2, GROUP], U32), tmp("gs", [P, 2, GROUP])
    pick = tmp("pick", [48, GROUP, P], BF16)
    pick1 = tmp("pick1", [48, GROUP])
    xp = tmp("xp", [48, 2, D], BF16)
    hp, hg, hz = tmp("hp", [P, STEP]), tmp("hg", [P, 2, BATCH]), tmp("hz", [P, 2, GROUP, GROUP])
    free = m["xT"][0:GROUP].rearrange("p k t -> p (k t)")
    y, g2, b2 = free[:, 0:2 * D].rearrange("p (g d) -> p g d", g=2), free[:, 2 * D:3 * D], free[:, 3 * D:4 * D]
    scrap = m["c_work"][0:GROUP].rearrange("p h n -> p (h n)")
    stat = tmp("stat", [GROUP, 4])
    u_in, v_in = [sem(f"e_u{k}") for k in range(RU // UB)], [sem(f"e_v{k}") for k in range(RV // BATCH)]
    xp_in, x_in = [sem(f"e_xp{g}") for g in range(2)], [sem(f"e_x{g}") for g in range(2)]
    (pick_ok, zeroed, staged, xb_done, h_done, gelu_ok, hz_ok, mm_done, ff_used, y_ok, var_ok, root_ok, gb_in) = (
        sem("e_" + n) for n in ("pick", "zeroed", "staged", "xb", "h", "gelu", "hz", "mm", "ff_used", "y", "var", "root", "gb"))
    sel_done, turned, taken = (sem("sel_" + n) for n in ("done", "turned", "taken"))
    saved, base = sem("saved"), m["saved"]
    ITS, PT_ = NP // STEP, P // STEP
    diag = lambda g, t, n: hz[:, g].rearrange("p t m -> p (t m)")[:, t * (GROUP + 1):(t + n - 1) * (GROUP + 1) + 1:GROUP + 1]

    def tiles(eng, body, between=None):
        with eng.Fori(0, NT) as n:
            with eng.Fori(0, 2) as q:
                body(n * PT_ + q, STEP, n * 2 + q, q)
            if between:
                between(n)
            with eng.Fori(0, 2) as q:
                body(n * PT_ + (q + 2), STEP)
        body(ITS, NS)

    with nc.Block() as block:
        @block.sync
        def _(sp):
            def load_parts(it, g, tn=GROUP):
                t0 = it * STEP + g * GROUP
                for q in range(3):
                    sp.dma_start(xp[q * GROUP:q * GROUP + tn, g], a["x1_parts"][q, bass.ds(t0, tn), :]).then_inc(xp_in[g], 16)

            def load_x(it, g, tn=GROUP):
                sp.dma_start(y[0:tn, g], a["x1_rows"][bass.ds(it * STEP + g * GROUP, tn), :]).then_inc(x_in[g], 16)

            def save(it, g):
                ahead(m, sp, y_ok, it * 2 + (g + 1))
                samples = isinstance(it, int) and it == ITS
                dst = a["y_sample"].rearrange("b o d -> (b o) d") if samples else (
                    a["y_prompt"][0, bass.ds(it * STEP + g * GROUP, GROUP), :])
                sp.dma_start(dst, y[0:dst.shape[0], g]).then_inc(saved, 16)
                ahead(m, sp, saved, it * 32 + (base + 16 * (g + 1)))

            sp.dma_start(g2, a["ln2_g"].to_broadcast([GROUP, D])).then_inc(gb_in, 16)
            sp.dma_start(b2, a["ln2_b"].to_broadcast([GROUP, D])).then_inc(gb_in, 16)
            sp.wait_ge(zeroed, 2)
            for g in range(2):
                load_parts(0, g)
                load_x(0, g)
            with sp.Fori(0, ITS - 1) as it:
                for g in range(2):
                    sp.wait_ge(xb_done, it * STEP + GROUP * (g + 1))
                    load_parts(it + 1, g)
                    save(it, g)
                    load_x(it + 1, g)
            sp.wait_ge(xb_done, ITS * STEP - GROUP)
            load_parts(ITS, 0, NS)
            save(ITS - 1, 0)
            load_x(ITS, 0, NS)
            save(ITS - 1, 1)
            save(ITS, 0)
            m["saved"] = base + 16 * (2 * ITS + 1)

        @block.gpsimd
        def _(pool):
            def gather(it, tokens):
                for t in range(tokens):
                    g = t // GROUP
                    if t % GROUP == 0:
                        n = min(tokens, GROUP)
                        nc.gpsimd.tensor_copy(ixs[:, g, 0:n], idxT[:, bass.ds(it * STEP + t, n)]).then_inc(staged, 1)
                        nc.gpsimd.tensor_copy(gs[:, g, 0:n], gateT[:, bass.ds(it * STEP + t, n)]).then_inc(staged, 1)
                        pool.wait_ge(staged, it * 4 + 2 * (g + 1))
                    ku, kv = t % RU, t % RV
                    off = lambda: bass.IndirectOffsetOnAxis(ap=ixs[:, g, t % GROUP:t % GROUP + 1], axis=0)
                    ahead(m, pool, h_done, it * STEP + (t + 1))
                    nc.gpsimd.indirect_dma_start(U[:, ku, :], None, a["peer_u"][0], off()).then_inc(u_in[ku // UB], 16)
                    ahead(m, pool, mm_done, it * STEP + (t + 1))
                    nc.gpsimd.indirect_dma_start(V[:, kv, :], None, a["peer_v"][0], off()).then_inc(v_in[kv // BATCH], 16)

            with pool.Fori(0, NT) as n:
                ahead(m, pool, taken, n * 2 + 2)
                with pool.Fori(0, PT_) as q:
                    gather(n * PT_ + q, STEP)
            pool.wait_ge(taken, 2 * NT + 2)
            gather(ITS, NS)

        @block.vector
        def _(dve):
            st = Steps(dve, sem("dve_step"), m["dve"])
            dve.sem_inc(h_done, RU)
            dve.sem_inc(ff_used, 1)
            dve.memset(hz[:], 0.0).then_inc(zeroed, 1)
            dve.memset(xp[:], 0.0).then_inc(zeroed, 1)
            st.link(dve.tensor_tensor(pick1[:], const(m, "mod16")[0:48].to_broadcast([48, GROUP]), const(m, "iota16")[0:48],
                                      ALU.is_equal))
            dve.tensor_copy(pick[:], pick1[:].unsqueeze(2).to_broadcast([48, GROUP, P])).then_inc(pick_ok, 1)
            dve.wait_ge(zeroed, 2)
            dve.wait_ge(gb_in, 32)
            choosing, norming = Steps(dve, sem("e_choose")), Steps(dve, sem("e_norm"))
            NORM, NPARTS = 7, 6

            def norm(it, g, tn, part):
                if part == 0:
                    norming.n, norming.base = 0, it * (2 * NORM) + g * NORM
                x, s = y[0:tn, g], stat[0:tn]
                two = lambda ap: ap.rearrange("p (b c) -> p b c", b=2)
                if part == 0:
                    dve.wait_ge(mm_done, it * STEP + (g * GROUP + tn + RV))
                    dve.wait_ge(x_in[g], it * 16 + 16)
                    dve.scalar_tensor_tensor(out=two(x), in0=two(x), scalar=ALPHA, in1=ps[0:tn, 4 + 2 * g:6 + 2 * g, :],
                                             op0=ALU.mult, op1=ALU.add).then_inc(ff_used, 1)
                elif part == 1:
                    dve.wait_ge(ff_used, it * 2 + (g + 2))
                    norming.link(dve.tensor_reduce(s[:, 0:1], x, AXX, ALU.add))
                    norming.link(dve.tensor_scalar(s[:, 0:1], s[:, 0:1], 1.0 / D, None, ALU.mult))
                elif part == 2:
                    norming.link(dve.tensor_scalar(x, x, s[:, 0:1], None, ALU.subtract))
                elif part == 3:
                    norming.link(dve.tensor_tensor_reduce(scrap[0:tn], x, x, 1.0, 0.0, ALU.mult, ALU.add, s[:, 1:2]))
                    dve.sem_inc(var_ok, 1)
                elif part == 4:
                    dve.wait_ge(root_ok, it * 2 + (g + 1))
                    norming.link(dve.reciprocal(s[:, 3:4], s[:, 2:3]))
                    norming.link(dve.scalar_tensor_tensor(out=x, in0=x, scalar=s[:, 3:4], in1=g2[0:tn], op0=ALU.mult, op1=ALU.mult))
                else:
                    norming.link(dve.tensor_tensor(x, x, b2[0:tn], ALU.add))
                    dve.sem_inc(y_ok, 1)
                    assert norming.n == NORM

            def weigh(it, b):
                dve.wait_ge(gelu_ok, it * (STEP // BATCH) + (b + 1))
                g, t = b * BATCH // GROUP % 2, b * BATCH % GROUP
                dve.tensor_tensor(diag(g, t, BATCH), hg[:, b % 2], gs[:, g, t:t + BATCH], ALU.mult).then_inc(hz_ok, 1)

            def dot(it, t):
                k = t % RU
                dve.wait_ge(xb_done, it * STEP + (t + 1))
                if t % UB == 0:
                    dve.wait_ge(u_in[k // UB], it * (16 * UB * STEP // RU) + 16 * UB * (t // RU + 1))
                u = U[:, k, :].rearrange("p (b c) -> p b c", b=2)
                dve.tensor_tensor_reduce(u, u, ps[:, 2 * (t % 2):2 * (t % 2) + 2, :], 1.0, 0.0, ALU.mult, ALU.add,
                                         hp[:, t % STEP:t % STEP + 1]).then_inc(h_done, 1)
                if t % BATCH == 0 and t:
                    weigh(it, t // BATCH - 1)

            def dots(it, n, chosen=None, q=None):
                if n == NS:
                    weigh(it, LEAD // BATCH - 1)
                else:
                    if chosen is not None:
                        choosing.n, choosing.base = 0, chosen * CSTEPS
                    for t in range(n):
                        dot(it, t + LEAD)
                        if chosen is not None:
                            choose(m, dve, choosing, t // 4, t % 4, chosen + 2, chosen * 8 + 16, q * CH)
                        if GROUP < t <= GROUP + NPARTS:
                            norm(it, 0, GROUP, t - GROUP - 1)
                for part in range(NPARTS):
                    norm(it, (n - 1) // GROUP, min(n, GROUP), part)
                if chosen is not None:
                    assert choosing.n == CSTEPS, choosing.n

            for t in range(LEAD):
                dot(0, t)
            CSTEPS = 8 * 5 + 1 + 5 + 4 * 5 + 3 + 7 + 3
            tiles(dve, dots)

        @block.scalar
        def _(act):
            def root(it, g, tn):
                act.wait_ge(var_ok, it * 2 + (g + 1))
                act.activation(stat[0:tn, 2:3], stat[0:tn, 1:2], ACT.Sqrt, scale=1.0 / D,
                               bias=const(m, "eps")[0:tn, EPS_LN:EPS_LN + 1]).then_inc(root_ok, 1)

            def gelu(it, b):
                act.wait_ge(h_done, it * STEP + (BATCH * b + BATCH + RU))
                c = BATCH * b % STEP
                act.activation(hg[:, b % 2], hp[:, c:c + BATCH], ACT.Gelu).then_inc(gelu_ok, 1)

            def gelus(it, n, chosen=None, q=None):
                if n == STEP:
                    for b in range(LEAD // BATCH, (STEP + LEAD) // BATCH):
                        gelu(it, b)
                        if b == 6:
                            root(it, 0, GROUP)
                        if b == 8 and chosen is not None:
                            choose_exp(m, act, chosen + 2)
                root(it, (n - 1) // GROUP, min(n, GROUP))

            def take(n):
                act.wait_ge(turned, n + 2)
                act.activation(idxT[:, bass.ds((n + 1) * P, P)], ps[:, 0, 0:P], ACT.Copy).then_inc(taken, 1)
                act.activation(gateT[:, bass.ds((n + 1) * P, P)], ps[:, 1, 0:P], ACT.Copy).then_inc(taken, 1)

            for b in range(LEAD // BATCH):
                gelu(0, b)
            tiles(act, gelus, take)

        @block.tensor
        def _(pe):
            pe.sem_inc(mm_done, RV)
            pe.wait_ge(pick_ok, 1)

            def spread(it, t):
                g = t // GROUP % 2
                if t % GROUP == 0:
                    pe.wait_ge(xp_in[g], it * 48 + 48 * (t // STEP + 1))
                pe.wait_ge(h_done, it * STEP + (t + RU - 1))
                for h in range(2):
                    mm = pe.matmul(ps[:, 2 * (t % 2) + h, :], pick[:, t % GROUP, :], xp[:, g, h * 512:(h + 1) * 512],
                                   start=True, stop=True)
                mm.then_inc(xb_done, 1)

            def add_rows(it, t, n):
                g, tg = t // GROUP, t % GROUP
                if t % BATCH == 0:
                    pe.wait_ge(hz_ok, it * (STEP // BATCH) + (t // BATCH + 1))
                    pe.wait_ge(v_in[t % RV // BATCH], it * (16 * BATCH * STEP // RV) + 16 * BATCH * (t // RV + 1))
                if tg == 0:
                    pe.wait_ge(ff_used, it * 2 + g)
                tn = min(n, GROUP)
                for h in range(2):
                    mm = pe.matmul(ps[0:tn, 4 + 2 * g + h, :], hz[:, g, tg, 0:tn], V[:, t % RV, h * 512:(h + 1) * 512],
                                   start=(tg == 0), stop=(tg == tn - 1))
                mm.then_inc(mm_done, 1)

            def tokens(it, n, chosen=None, q=None):
                for t in range(n):
                    if n == STEP:
                        spread(it, t + LEAD)
                    add_rows(it, t, n)

            def turn(n):
                pe.wait_ge(sel_done, n * 2 + 4)
                pe.wait_ge(h_done, n * P + (2 * STEP + LEAD + RU))
                turn_chosen(m, pe, 0)
                ahead(m, pe, taken, n * 2 + 4)

            for t in range(LEAD):
                spread(0, t)
            tiles(pe, tokens, turn)


_INS = ['x_prompt', 'x_sample', 'state_rwkv_shift', 'state_rwkv_wkv', 'state_gdn_conv', 'state_gdn_ssm', 'w_in', 'rwkv_mu',
        'rwkv_w0', 'rwkv_w2', 'rwkv_a0', 'rwkv_a2', 'rwkv_g2', 'rwkv_k_k', 'rwkv_k_a', 'rwkv_r_k', 'rwkv_ln_w', 'rwkv_ln_b',
        'gdn_conv_w', 'gdn_a_log', 'gdn_dt_bias', 'gdn_norm_w', 'w_branch_a', 'w_branch_b', 'w_out', 'ln1_g', 'ln1_b',
        'peer_wq', 'peer_subkeys', 'peer_u', 'peer_v', 'ln2_g', 'ln2_b']

_SHAPES = {"y_prompt": (1, NP, D), "y_sample": (NS, 1, D), "p_shift": (1, 1, RW_COLS), "p_wkv": (1, 1, HR, CR, CR),
           "p_conv": (1, 1, 3, GD_QKV), "p_ssm": (1, 1, HG, CG, CG), "s_shift": (1, NS, RW_COLS), "s_wkv": (1, NS, HR, CR, CR),
           "s_conv": (1, NS, 3, GD_QKV), "s_ssm": (1, NS, HG, CG, CG)}
_SCRATCH = {"rows_rw": (6, NS * HR, CR), "rows_gd": (3, NS * HG, CG), "rows_bg": (2, NS * HG), "o_rw": (NS * HR, CR),
            "x1_rows": (T, D), "x1_parts": ((3, T, D), "bf16")}


def kernel(**inputs):
    import numpy as _np
    import concourse.bacc as _bacc
    from concourse import mybir as _mybir
    from concourse.bass_utils import run_bass_kernel_spmd as _run

    nc = _bacc.Bacc("TRN2", target_bir_lowering=False, num_devices=1)
    arrays, a = {}, {}
    for name in _INS + ["consts"]:
        x = _np.ascontiguousarray(CONSTS if name == "consts" else inputs[name])
        arrays[name + "_dram"] = x
        a[name] = nc.dram_tensor(name + "_dram", x.shape, _mybir.dt.from_np(x.dtype), kind="ExternalInput").ap()
    for name, shape in _SHAPES.items():
        a[name] = nc.dram_tensor(name + "_dram", shape, _mybir.dt.float32, kind="ExternalOutput").ap()
    for name, shape in _SCRATCH.items():
        dt = _mybir.dt.float32
        if isinstance(shape[-1], str):
            shape, dt = shape[0], _mybir.dt.bfloat16
        a[name] = nc.dram_tensor(name + "_dram", shape, dt, kind="Internal").ap()
    program(nc, a)
    r = _run(nc, [arrays], core_ids=[0])
    return tuple(r.results[0][name + "_dram"] for name in _SHAPES)
```

```python
from contextlib import ExitStack

import numpy as np

import concourse.bass as bass
from concourse import mybir

ALU = mybir.AluOpType
ACT = mybir.ActivationFunctionType
AXX = mybir.AxisListType.X
F32 = mybir.dt.float32
BF16 = mybir.dt.bfloat16
U32 = mybir.dt.uint32

P = 128
D = 1024
KD = D // P
NP = 512
NS = 8
T = NP + NS
TH = T // 2
NT = NP // P
HR, CR = 8, 64
HG, CG = 4, 128
RW_COLS = 1792
RT_ = RW_COLS // P
QT = 12
ZT = 4
PT = RT_ + QT + ZT
GD_QKV = 1536
BA0 = PT * P
GATE0 = BA0 + 8
ALPHA = 2.0 ** 0.25
DECAY = float(np.exp(-0.5))
TAIL = 11
BG = 36

_C = {}


def _consts():
    cols = []

    def put(name, a):
        _C[name] = (sum(c.shape[1] for c in cols), a.shape[1])
        cols.append(a.astype(np.float32))

    i = np.arange(P)
    s, t = i[:, None], i[None, :]
    put("ident", np.eye(P))
    put("ones", np.ones((P, P)))
    put("blk64", (s // 64 == t // 64) * 1.0)
    for m in (1, 2, 4, 8, 16, 32, 64):
        put(f"lvl{m}", ((s // (2 * m) == t // (2 * m)) & (s // m % 2 == 0) & (t // m % 2 == 1)) * 1.0)
    one = np.ones((P, P))
    put("pair", np.concatenate([((s // 64 == t // 64) & (s < t)) * 1.0, ((s // 64 == t // 64) & (s <= t)) * 1.0], 1))
    put("incl", (s <= t) * 1.0)
    sel = np.zeros((P, 8, P))
    for h in range(4):
        sel[h, h] = 1.0
        sel[32 + h, 4 + h] = 1.0
    put("sel", sel.reshape(P, -1))
    put("keep64", np.broadcast_to((np.arange(NP) % 64 != 0) * 1.0, (P, NP)))
    put("keep128", np.broadcast_to((np.arange(NP) % 128 != 0) * 1.0, (P, NP)))
    put("sum4", (s % 32 == t % 32) * 1.0)
    put("iota16", np.broadcast_to(np.arange(16.0), (P, 16)))
    put("mod16", (s % 16) * 1.0)
    put("eps", np.broadcast_to(np.array([1e-12, 1e-6, 64e-5, 1e-5]), (P, 4)))
    return np.concatenate(cols, 1)


CONSTS = _consts()
EPS_KK, EPS_GD, EPS_GN, EPS_LN = range(4)

_PAR = {}
_n = 0
for _name, _rows in (("rwkv_mu", RT_), ("rwkv_w0", 4), ("rwkv_a0", 4), ("rwkv_k_k", 4), ("rwkv_k_a", 4),
                     ("rwkv_r_k", 4), ("rwkv_ln_w", 4), ("rwkv_ln_b", 4), ("gdn_conv_w", 4 * QT), ("gdn_norm_w", 1),
                     ("ln1_g", KD), ("ln1_b", KD)):
    _PAR[_name] = (_n, _rows)
    _n += _rows
NPAR = _n


class Steps:

    def __init__(self, eng, sem, start=0):
        self.eng, self.sem, self.n, self.base = eng, sem, start, 0

    def did(self, ins):
        ins.then_inc(self.sem, 1)
        self.n += 1

    def settled(self):
        self.eng.wait_ge(self.sem, self.base + self.n)

    def link(self, ins):
        self.did(ins)
        self.settled()


def program(nc, a):
    ctx = ExitStack()
    with ctx:
        def sb(name, shape, dt=F32):
            return ctx.enter_context(nc.sbuf_tensor(name, shape, dt))

        sems = {}

        def sem(name):
            if name not in sems:
                sems[name] = ctx.enter_context(nc.semaphore(name))
            return sems[name]

        ps = ctx.enter_context(nc.psum_tensor("ps", [P, 8, 512], F32))
        cst = sb("cst", [P, CONSTS.shape[1]])
        par = sb("par", [P, NPAR])
        xT = sb("xT", [P, KD, T])
        m = dict(nc=nc, a=a, sem=sem, ps=ps, cst=cst, par=par, xT=xT, saved=0)

        def phase(*steps):
            with ExitStack() as local:
                m["tmp"] = lambda name, shape, dt=F32: local.enter_context(nc.sbuf_tensor(name, shape, dt))
                for step in steps:
                    step(m)

        with ExitStack() as mixing:
            for name, shape in (("Praw", [P, PT, T]), ("mix", [P, RT_, T]), ("conv", [P, QT, T]), ("kk", [P, 4, T]),
                                ("scr", [P, 4, T]), ("bg", [BG, T]), ("gdpar", [BG, 4]), ("omka", [P, 4]),
                                ("Gend", [P, 4, NP // 64])):
                m[name] = mixing.enter_context(nc.sbuf_tensor(name, shape, F32))
            phase(load_inputs, project)
            phase(recur)
            phase(sample_recur)
            phase(merge, norm1)
        for name, shape, dt in (("scores", [P, (NT + 1) * HP, NK], F32), ("idxT", [P, NP + P], U32), ("gateT", [P, NP + P], F32)):
            m[name] = sb(name, shape, dt)
        choose_buffers(m, sb)
        phase(query)
        phase(experts)
    return m


def const(m, name):
    c0, n = _C[name]
    return m["cst"][:, c0:c0 + n]


def ahead(m, eng, s, value):
    if isinstance(value, int):
        eng.wait_ge(s, value)
    else:
        value = eng.to_reg(value)
        eng.wait_ge(m["sem"]("cst_in"), 16)
        eng.wait_ge(s, value)


def param(m, name, j=0):
    c = _PAR[name][0] + j
    return m["par"][:, c:c + 1]


def load_inputs(m):
    nc, a, tmp, sem, ps, cst, par, xT = (m[k] for k in ("nc", "a", "tmp", "sem", "ps", "cst", "par", "xT"))
    mix, conv, gdpar = m["mix"], m["conv"], m["gdpar"]
    m["shT"] = shT = tmp("shT", [P, RT_, NS])
    m["cbT"] = cbT = tmp("cbT", [P, QT, NS * 3])
    m["ring"] = ring = tmp("ring", [P, 3, KD, P])
    m["wba"] = wba = tmp("wba", [P, KD, BG])
    m["w2a2"] = w2a2 = tmp("w2a2", [P, 512])
    m["g2"] = g2 = tmp("g2", [P, 512])
    xrow = mix[:].rearrange("p a t -> p (a t)")[:, 0:4 * D].rearrange("p (n d) -> p n d", n=4)
    flat = conv[:].rearrange("p a t -> p (a t)")
    xsrow, shrow, cbrow = flat[0:NS, 0:D], flat[0:NS, D:D + RW_COLS], flat[0:24, 2816:2816 + GD_QKV]
    prow = flat[0:NPAR, 4352:4352 + P]
    x_in, small_in, w_in = sem("x_in"), sem("small_in"), [sem(f"weights{b}") for b in range(3)]
    ba_zero, turned, xT_ready = sem("ba_zero"), sem("turned"), sem("xT_ready")
    ident = const(m, "ident")
    n_small = 0
    with nc.Block() as block:
        @block.sync
        def _(sp):
            sp.dma_start(cst[:, 0:P], a["consts"][:, 0:P]).then_inc(x_in, 16)
            for n in range(NT):
                sp.dma_start(xrow[:, n, :], a["x_prompt"][0, n * P:(n + 1) * P, :]).then_inc(x_in, 16)
            for b in range(3):
                sp.dma_start(ring[:, b], a["w_in"][0, :, b * P:(b + 1) * P].rearrange("(k p) c -> p k c", p=P)
                             ).then_inc(w_in[b], 16)
            sp.dma_start(cst[:, P:], a["consts"][:, P:]).then_inc(sem("cst_in"), 16)

        @block.scalar
        def _(act):
            nonlocal n_small
            act.dma_start(xsrow, a["x_sample"].rearrange("b o d -> (b o) d")).then_inc(x_in, 16)
            act.dma_start(shrow, a["state_rwkv_shift"][0]).then_inc(small_in, 16)
            act.dma_start(cbrow, a["state_gdn_conv"][0].rearrange("b j c -> (b j) c")).then_inc(small_in, 16)
            n_small = 2
            for name, (r0, n) in _PAR.items():
                src = a[name][0]
                if name in ("rwkv_r_k", "gdn_conv_w"):
                    src = src.rearrange("a b -> (a b)")
                act.dma_start(prow[r0:r0 + n, :], src.rearrange("(n c) -> n c", c=P)).then_inc(small_in, 16)
                n_small += 1
            act.dma_start(w2a2[0:64, :], a["rwkv_w2"][0]).then_inc(small_in, 16)
            act.dma_start(w2a2[64:128, :], a["rwkv_a2"][0]).then_inc(small_in, 16)
            act.dma_start(g2[:], a["rwkv_g2"][0]).then_inc(small_in, 16)
            act.dma_start(gdpar[32:36, 0:1], a["gdn_a_log"].rearrange("o h -> h o")).then_inc(small_in, 16)
            act.dma_start(gdpar[32:36, 1:2], a["gdn_dt_bias"].rearrange("o h -> h o")).then_inc(small_in, 16)
            act.wait_ge(ba_zero, 1)
            ba = a["w_in"][0, :, BA0:BA0 + 8].rearrange("(k p) c -> p k c", p=P)
            act.dma_start(wba[:, :, 0:4], ba[:, :, 0:4]).then_inc(small_in, 16)
            act.dma_start(wba[:, :, 32:36], ba[:, :, 4:8]).then_inc(small_in, 16)
            n_small += 7
            m["small"] = 16 * n_small

        @block.gpsimd
        def _(pool):
            nc.gpsimd.memset(wba[:], 0.0).then_inc(ba_zero, 1)

        @block.tensor
        def _(pe):
            pe.wait_ge(x_in, 16 * (NT + 2))
            for n in range(NT):
                for k in range(KD):
                    mm = pe.transpose(ps[:, 2 * n + k // 4, (k % 4) * P:(k % 4 + 1) * P], xrow[:, n, k * P:(k + 1) * P], ident)
                mm.then_inc(turned, 1)
            pe.wait_ge(xT_ready, 1)
            for k in range(KD):
                mm = pe.transpose(ps[:, 0, k * NS:(k + 1) * NS], xsrow[:, k * P:(k + 1) * P], ident[0:NS, 0:NS])
            mm.then_inc(turned, 1)

        @block.vector
        def _(dve):
            for n in range(NT):
                dve.wait_ge(turned, n + 1)
                dve.tensor_copy(xT[:, :, n * P:(n + 1) * P], ps[:, 2 * n:2 * n + 2, :].rearrange("p b (k t) -> p (b k) t", t=P)
                                ).then_inc(xT_ready, 1)
            dve.wait_ge(turned, NT + 1)
            dve.tensor_copy(xT[:, :, NP:T], ps[:, 0, 0:64].rearrange("p (k t) -> p k t", t=NS)).then_inc(xT_ready, 1)
    m["rows"] = (prow, shrow, cbrow)


def half(ap):
    return ap.rearrange("p (h t) -> p h t", h=2)


def project(m):
    nc, a, tmp, sem, ps, par, xT = (m[k] for k in ("nc", "a", "tmp", "sem", "ps", "par", "xT"))
    Praw, mix, conv, kk, scr, shT, cbT, ring, wba, gdpar, w2a2, g2, bg, omka, Gend = (
        m[k] for k in ("Praw", "mix", "conv", "kk", "scr", "shT", "cbT", "ring", "wba", "gdpar", "w2a2", "g2", "bg", "omka", "Gend"))
    ones, blk64, ident, eps = (const(m, n) for n in ("ones", "blk64", "ident", "eps"))
    w_in = [sem(f"weights{b}") for b in range(3)]
    tile_done = sem("tile_done")
    tile_out = sem("tile_out")
    (ba_done, ba_out, bg_zero, mixed, low_in, conv_ready, silu_ready, sq_ready, norm_mm, root, low_mm, low_out, tail_mm,
     tail_out, spl_in, spl, exps, bon_in, bon_mm, bon_out, out) = (sem(n) for n in (
         "ba_done", "ba_out", "bg_zero", "mixed", "low_in", "conv_ready", "silu_ready", "sq_ready", "norm_mm", "root",
         "low_mm", "low_out", "tail_mm", "tail_out", "spl_in", "spl", "exps", "bon_in", "bon_mm", "bon_out", "saved"))
    ITS, PER = PT // 6, 6
    EARLY = 2
    m["weights"] = [16 * PT // 3] * 3 + [0]
    spx, tail = tmp("spx", [BG, T]), tmp("tail", [P, RT_ + QT, TAIL])
    lrk = tmp("lrk", [P, 2, T])
    sq = tmp("sq", [P, 8, T])
    sw, m["gg"], m["aa"] = Praw[:, 0:4], Praw[:, 4:8], Praw[:, 8:12]
    gg, aa = m["gg"], m["aa"]
    m["G"], m["Gi"], m["Gp"], m["stage"] = G, Gi, Gp, _ = Praw[:, 14:18], Praw[:, 18:22], sw, Praw[:, 22:26]
    flat = lambda ap: ap.rearrange("p a b -> p (a b)")
    rw_row, gd_row = flat(Praw[0:TAIL, 22:26])[:, 0:RW_COLS], flat(ring[0:TAIL, 0:2].rearrange("p s k c -> p (s k) c"))[:, 0:GD_QKV]
    pair2 = lambda n: ps[:, 4 + 2 * (n % 2):6 + 2 * (n % 2), 0:TH]
    k2 = mix[:, 4:8]
    TAILS = ((0, 8, rw_row, 0), (8, 14, rw_row, 0), (14, 22, gd_row, 14), (22, 26, gd_row, 14))

    with nc.Block() as block:
        @block.sync
        def _(sp):
            sp.dma_start(a["s_conv"][0, :, 0:2, :], a["state_gdn_conv"][0, :, 1:3, :]).then_inc(out, 16)
            with sp.Fori(0, ITS - 1) as it:
                for t in range(PER):
                    sp.wait_ge(tile_done, it * PER + (t + 1))
                    sp.dma_start(ring[:, t % 3], a["w_in"][0, :, bass.ds(it * (PER * P) + (t + 3) * P, P)]
                                 .rearrange("(k p) c -> p k c", p=P)).then_inc(w_in[t % 3], 16)
            for t in range(PER - 3):
                n = (ITS - 1) * PER + t
                sp.wait_ge(tile_done, n + 1)
                sp.dma_start(ring[:, t % 3], a["w_in"][0, :, (n + 3) * P:(n + 4) * P]
                             .rearrange("(k p) c -> p k c", p=P)).then_inc(w_in[t % 3], 16)
            sp.wait_ge(tail_out, 4)
            sp.dma_start(a["p_shift"][0], rw_row[2:3]).then_inc(out, 16)
            sp.dma_start(a["s_shift"][0], rw_row[3:11]).then_inc(out, 16)
            sp.dma_start(a["p_conv"][0, 0], gd_row[0:3]).then_inc(out, 16)
            sp.dma_start(a["s_conv"][0, :, 2, :], gd_row[3:11]).then_inc(out, 16)
            sp.wait_ge(out, m["saved"] + 16 * 5)
            m["saved"] += 16 * 5

        @block.tensor
        def _(pe):
            def tile(it, t):
                pe.wait_ge(w_in[t % 3], it * 32 + 16 * (t // 3 + 1))
                pe.wait_ge(tile_out, it * PER + (t + 1))
                for h in range(2):
                    for k in range(KD):
                        mm = pe.matmul(ps[:, 2 * (t % 2) + h, 0:TH], ring[:, t % 3, k, :], xT[:, k, h * TH:(h + 1) * TH],
                                       start=(k == 0), stop=(k == KD - 1))
                mm.then_inc(tile_done, 1)

            def tiles(first, n):
                with pe.Fori(0, n) as it:
                    for t in range(PER):
                        tile(it + first, t)

            def norms(n0, n1):
                for n in range(n0, n1):
                    if n >= 2:
                        pe.wait_ge(root, n - 1)
                    w, x = (blk64, scr[:, n]) if n < 4 else (ones, sq[:, n - 4])
                    for h in range(2):
                        mm = pe.matmul(ps[:, 4 + 2 * (n % 2) + h, 0:TH], w, x[:, h * TH:(h + 1) * TH], start=True, stop=True)
                    mm.then_inc(norm_mm, 1)

            tiles(0, 1)
            prow, shrow, cbrow = m["rows"]
            pe.wait_ge(sem("small_in"), m["small"])
            pe.transpose(ps[:, 4, 64:64 + NPAR], prow, ident[0:NPAR, 0:NPAR])
            for j in range(RT_):
                pe.transpose(ps[:, 4, 192 + j * NS:192 + (j + 1) * NS], shrow[:, j * P:(j + 1) * P], ident[0:NS, 0:NS])
            for j in range(QT):
                mm = pe.transpose(ps[:, 5, j * 24:(j + 1) * 24], cbrow[:, j * P:(j + 1) * P], ident[0:24, 0:24])
            mm.then_inc(sem("turned"), 1)
            tiles(1, 2)
            pe.wait_ge(sem("cst_in"), 16)
            pe.wait_ge(sq_ready, 1)
            norms(0, 4)
            pe.wait_ge(low_in, 3)
            pe.wait_ge(root, 4)
            for n in range(12):
                j, kind = n // 3, n % 3
                if n >= 2:
                    pe.wait_ge(low_out, n - 1)
                w = (w2a2[0:64], w2a2[64:128], g2[:])[kind]
                r = (lrk[0:64, 0], lrk[64:128, 0], lrk[:, 1])[kind]
                for h in range(2):
                    mm = pe.matmul(ps[:, 4 + 2 * (n % 2) + h, 0:TH], w[:, j * P:(j + 1) * P], r[:, h * TH:(h + 1) * TH],
                                   start=True, stop=True)
                mm.then_inc(low_mm, 1)
            tiles(3, 1)
            for t in range(EARLY):
                tile(ITS - 1, t)
            pe.wait_ge(low_out, 12)
            pe.wait_ge(sq_ready, 2)
            norms(4, 12)
            for t in range(EARLY, PER):
                tile(ITS - 1, t)
            pe.wait_ge(root, 12)
            for h in range(2):
                for k in range(KD):
                    mm = pe.matmul(ps[0:BG, 4 + h, 0:TH], wba[:, k, :], xT[:, k, h * TH:(h + 1) * TH],
                                   start=(k == 0), stop=(k == KD - 1))
            mm.then_inc(ba_done, 1)
            pe.wait_ge(bon_in, 1)
            pe.wait_ge(ba_out, 2)
            for n in range(4):
                if n >= 2:
                    pe.wait_ge(bon_out, n - 1)
                for h in range(2):
                    mm = pe.matmul(ps[:, 4 + 2 * (n % 2) + h, 0:TH], blk64, scr[:, n, h * TH:(h + 1) * TH], start=True, stop=True)
                mm.then_inc(bon_mm, 1)
            pe.wait_ge(tile_out, 2 + PT)
            pe.wait_ge(conv_ready, 2)
            for n, (j0, j1, _, _) in enumerate(TAILS):
                if n >= 2:
                    pe.wait_ge(tail_out, n - 1)
                for j in range(j0, j1):
                    mm = pe.transpose(ps[0:TAIL, 2 * (n % 2) + (j - j0) // 4, (j - j0) % 4 * P:((j - j0) % 4 + 1) * P],
                                      tail[:, j, :], ident)
                mm.then_inc(tail_mm, 1)

        @block.scalar
        def _(act):
            act.sem_inc(tile_out, 2)

            def roots(n0, n1):
                for n in range(n0, n1):
                    act.wait_ge(norm_mm, n + 1)
                    d, e = (scr[:, n], EPS_KK) if n < 4 else (sq[:, n - 4], EPS_GD)
                    act.activation(half(d), pair2(n), ACT.Sqrt, bias=eps[:, e:e + 1]).then_inc(root, 1)

            def tiles(first, n):
                with act.Fori(0, n) as it:
                    for t in range(PER):
                        act.wait_ge(tile_done, it * PER + (PER * first + t + 1))
                        act.activation(Praw[:, bass.ds(it * PER + (PER * first + t), 1), :].rearrange("p o (h t) -> p (o h) t", h=2),
                                       ps[:, 2 * (t % 2):2 * (t % 2) + 2, 0:TH], ACT.Copy).then_inc(tile_out, 1)

            tiles(0, 3)
            act.wait_ge(sem("cst_in"), 16)
            act.wait_ge(mixed, 1)
            act.activation(lrk[0:64, 0], mix[0:64, 12], ACT.Tanh).then_inc(low_in, 1)
            act.activation(lrk[64:128, 0], mix[64:128, 12], ACT.Copy).then_inc(low_in, 1)
            act.activation(lrk[:, 1], mix[:, 13], ACT.Sigmoid).then_inc(low_in, 1)
            roots(0, 4)
            for n in range(12):
                j, kind = n // 3, n % 3
                act.wait_ge(low_mm, n + 1)
                dst = half((sw, aa, gg)[kind][:, j, :])
                if kind < 2:
                    ins = act.activation(dst, pair2(n), ACT.Sigmoid, bias=param(m, ("rwkv_w0", "rwkv_a0")[kind], j))
                else:
                    ins = act.activation(dst, pair2(n), ACT.Copy)
                ins.then_inc(low_out, 1)
            tiles(3, 1)
            act.wait_ge(conv_ready, 1)
            for n in range(2):
                act.activation(conv[:, 4 * n:4 * n + 4, :], conv[:, 4 * n:4 * n + 4, :], ACT.Silu).then_inc(silu_ready, 1)

            def decay(n):
                if n == 0:
                    act.wait_ge(conv_ready, 1)
                    act.activation(Gi[:, :, 0:NP], G[:, :, 0:NP], ACT.Exp, scale=DECAY).then_inc(exps, 1)
                elif n == 1:
                    act.wait_ge(exps, 1)
                    act.activation(G[:, :, 0:NP], G[:, :, 0:NP], ACT.Exp, scale=-DECAY).then_inc(exps, 1)
                elif n == 2:
                    act.activation(G[:, :, NP:T], sw[:, :, NP:T], ACT.Exp, scale=-DECAY).then_inc(exps, 1)
                elif n == 3:
                    act.activation(Gp[:, :, 0:NP], Gp[:, :, 0:NP], ACT.Exp, scale=-DECAY).then_inc(exps, 1)

            def tile(t):
                n = (ITS - 1) * PER + t
                act.wait_ge(tile_done, n + 1)
                act.activation(half(Praw[:, n]), ps[:, 2 * (t % 2):2 * (t % 2) + 2, 0:TH], ACT.Copy).then_inc(tile_out, 1)

            for t in range(EARLY):
                decay(2 * t)
                decay(2 * t + 1)
                tile(t)
            roots(4, 12)
            for t in range(EARLY, PER):
                tile(t)
            act.wait_ge(ba_done, 1)
            act.wait_ge(bg_zero, 1)
            act.activation(half(bg[0:4, :]), ps[0:4, 4:6, 0:TH], ACT.Sigmoid).then_inc(ba_out, 1)
            act.activation(half(bg[32:36, :]), ps[32:36, 4:6, 0:TH], ACT.Identity, bias=gdpar[32:36, 1:2]).then_inc(ba_out, 1)
            act.wait_ge(conv_ready, 2)
            act.activation(conv[:, 8:12, :], conv[:, 8:12, :], ACT.Silu).then_inc(silu_ready, 1)
            act.wait_ge(spl_in, 1)
            act.activation(spx[32:36, :], spx[32:36, :], ACT.Exp, scale=-1.0).then_inc(spl, 1)
            act.activation(gdpar[32:36, 2:3], gdpar[32:36, 0:1], ACT.Exp).then_inc(spl, 1)
            act.wait_ge(spl, 2)
            act.activation(spx[32:36, :], spx[32:36, :], ACT.Ln, bias=1.0).then_inc(spl, 1)

        @block.gpsimd
        def _(pool):
            nc.gpsimd.memset(bg[:], 0.0).then_inc(bg_zero, 1)

        @block.vector
        def _(dve):
            st = Steps(dve, sem("dve_step"))

            def convolve(j0, j1):
                for j in range(j0, j1):
                    r = Praw[:, RT_ + j]
                    dve.wait_ge(tile_out, 2 + RT_ + j + 1)
                    st.link(dve.tensor_scalar(conv[:, j, :], r, param(m, "gdn_conv_w", 3 * QT + j), None, ALU.mult))
                    for back in (1, 2, 3):
                        tap = 3 - back
                        w = param(m, "gdn_conv_w", tap * QT + j)
                        st.did(dve.scalar_tensor_tensor(out=conv[:, j, back:NP], in0=r[:, 0:NP - back], scalar=w,
                                                        in1=conv[:, j, back:NP], op0=ALU.mult, op1=ALU.add))
                        st.link(dve.scalar_tensor_tensor(out=conv[:, j, NP:T], in0=cbT[:, j, tap:24:3], scalar=w,
                                                         in1=conv[:, j, NP:T], op0=ALU.mult, op1=ALU.add))
                st.link(dve.tensor_copy(tail[:, RT_ + j0:RT_ + j1], Praw[:, RT_ + j0:RT_ + j1, NP - 3:T]))

            dve.wait_ge(sem("turned"), NT + 2)
            st.did(dve.tensor_copy(par[:], ps[:, 4, 64:64 + NPAR]))
            st.did(dve.tensor_copy(shT[:], ps[:, 4, 192:192 + RT_ * NS].rearrange("p (k t) -> p k t", t=NS)))
            st.did(dve.tensor_copy(cbT[:], ps[:, 5, 0:24 * QT].rearrange("p (k t) -> p k t", t=24)))
            st.settled()
            dve.wait_ge(tile_out, 2 + RT_)
            st.did(dve.tensor_tensor(mix[:, :, 1:NP], Praw[:, 0:RT_, 0:NP - 1], Praw[:, 0:RT_, 1:NP], ALU.subtract))
            st.did(dve.tensor_scalar(mix[:, :, 0:1], Praw[:, 0:RT_, 0:1], -1.0, None, ALU.mult))
            st.did(dve.tensor_tensor(mix[:, :, NP:T], shT[:], Praw[:, 0:RT_, NP:T], ALU.subtract))
            c0 = _PAR["rwkv_k_a"][0]
            st.did(dve.tensor_scalar(omka[:], par[:, c0:c0 + 4], -1.0, 1.0, ALU.mult, ALU.add))
            st.did(dve.tensor_copy(tail[:, 0:RT_], Praw[:, 0:RT_, NP - 3:T]))
            st.settled()
            for j in range(RT_):
                st.did(dve.scalar_tensor_tensor(out=mix[:, j], in0=mix[:, j], scalar=param(m, "rwkv_mu", j), in1=Praw[:, j],
                                                op0=ALU.mult, op1=ALU.add))
            st.settled()
            dve.sem_inc(mixed, 1)
            for j in range(4):
                st.did(dve.tensor_scalar(kk[:, j], mix[:, 4 + j], param(m, "rwkv_k_k", j), None, ALU.mult))
            st.settled()
            st.link(dve.tensor_tensor(scr[:], kk[:], kk[:], ALU.mult))
            dve.sem_inc(sq_ready, 1)
            convolve(0, 4)
            dve.wait_ge(root, 4)
            st.link(dve.reciprocal(scr[:], scr[:]))
            st.link(dve.tensor_tensor(kk[:], kk[:], scr[:], ALU.mult))
            dve.wait_ge(sem("cst_in"), 16)
            dve.wait_ge(low_out, 12)
            for j in range(4):
                st.did(dve.tensor_tensor_scan(G[:, j, 0:NP], const(m, "keep64"), sw[:, j, 0:NP], 0.0, ALU.mult, ALU.add))
            st.settled()
            st.did(dve.tensor_tensor(Gp[:, :, 0:NP], G[:, :, 0:NP], sw[:, :, 0:NP], ALU.subtract))
            for j in range(4):
                st.did(dve.tensor_scalar(scr[:, j], aa[:, j], param(m, "rwkv_k_a", j), omka[:, j:j + 1], ALU.mult, ALU.add))
            st.settled()
            st.did(dve.tensor_tensor(k2, k2, scr[:], ALU.mult))
            st.did(dve.tensor_tensor(aa, aa, kk[:], ALU.mult))
            st.settled()
            for j in range(4):
                st.did(dve.scalar_tensor_tensor(out=scr[:, j], in0=mix[:, j], scalar=param(m, "rwkv_r_k", j), in1=k2[:, j],
                                                op0=ALU.mult, op1=ALU.mult))
            st.settled()
            dve.sem_inc(bon_in, 1)
            convolve(4, 8)
            dve.sem_inc(conv_ready, 1)
            for n in range(2):
                dve.wait_ge(silu_ready, n + 1)
                st.did(dve.tensor_tensor(sq[:, 4 * n:4 * n + 4], conv[:, 4 * n:4 * n + 4], conv[:, 4 * n:4 * n + 4], ALU.mult))
            st.settled()
            dve.sem_inc(sq_ready, 1)
            convolve(8, 8 + EARLY)
            dve.wait_ge(exps, 4)
            st.did(dve.scalar_tensor_tensor(out=Gp[:, :, 0:NP], in0=Gp[:, :, 0:NP], scalar=-1.0, in1=kk[:, :, 0:NP],
                                            op0=ALU.mult, op1=ALU.mult))
            st.did(dve.tensor_tensor(aa[:, :, 0:NP], aa[:, :, 0:NP], Gi[:, :, 0:NP], ALU.mult))
            st.did(dve.tensor_tensor(k2[:, :, 0:NP], k2[:, :, 0:NP], Gi[:, :, 0:NP], ALU.mult))
            st.did(dve.tensor_tensor(mix[:, 0:4, 0:NP], mix[:, 0:4, 0:NP], G[:, :, 0:NP], ALU.mult))
            st.did(dve.tensor_copy(Gend[:], G[:, :, 63:NP:64]))
            dve.wait_ge(root, 12)
            st.link(dve.reciprocal(sq[:], sq[:]))
            st.did(dve.tensor_tensor(conv[:, 4:8], conv[:, 4:8], sq[:, 4:8], ALU.mult))
            st.did(dve.scalar_tensor_tensor(out=conv[:, 0:4], in0=conv[:, 0:4], scalar=CG ** -0.5, in1=sq[:, 0:4],
                                            op0=ALU.mult, op1=ALU.mult))
            st.settled()
            convolve(8 + EARLY, 12)
            dve.sem_inc(conv_ready, 1)
            dve.wait_ge(ba_out, 2)
            st.link(dve.tensor_scalar(spx[32:36, :], bg[32:36, :], -1.0, None, ALU.mult))
            st.did(dve.tensor_tensor(spx[32:36, :], spx[32:36, :], bg[32:36, :], ALU.max))
            st.settled()
            st.link(dve.tensor_scalar(bg[32:36, :], bg[32:36, :], 0.0, None, ALU.max))
            dve.sem_inc(spl_in, 1)
            for n in range(4):
                dve.wait_ge(bon_mm, n + 1)
                dve.tensor_tensor(half(scr[:, n]), pair2(n), half(mix[:, 8 + n]), ALU.mult).then_inc(bon_out, 1)
            for n, (j0, j1, row, first) in enumerate(TAILS):
                dve.wait_ge(tail_mm, n + 1)
                b = 2 * (n % 2)
                if n == 0:
                    dve.wait_ge(tile_done, PT)
                c0 = (j0 - first) * P
                for h in range(0, j1 - j0, 4):
                    w = min(4, j1 - j0 - h) * P
                    ins = dve.tensor_copy(row[:, c0 + h * P:c0 + h * P + w], ps[0:TAIL, b + h // 4, 0:w])
                ins.then_inc(tail_out, 1)
            dve.wait_ge(spl, 3)
            st.link(dve.tensor_tensor(bg[32:36, :], bg[32:36, :], spx[32:36, :], ALU.add))
            st.link(dve.tensor_scalar(spx[32:36, :], bg[32:36, :], gdpar[32:36, 2:3], -1.0, ALU.mult, ALU.mult))
            st.did(dve.tensor_tensor_scan(bg[32:36, 0:NP], const(m, "keep128")[32:36], spx[32:36, 0:NP], 0.0, ALU.mult, ALU.add))
            st.did(dve.tensor_copy(bg[32:36, NP:T], spx[32:36, NP:T]))
            st.settled()
            m["dve"] = st.n


RWROW, GDROW = 6 * 512, GD_QKV + BG
ROUNDS = [(c, min(c + 1024, RWROW + GD_QKV)) for c in range(0, RWROW + GD_QKV, 1024)]


def sample_rows_turn(m, pe):
    sem, ps, mix, conv = m["sem"], m["ps"], m["mix"], m["conv"]
    tiles = [src[:, j, NP:T] for src in (mix[:, 0:4], m["G"], mix[:, 4:8], mix[:, 8:12], m["kk"], m["aa"]) for j in range(4)]
    tiles += [conv[:, j, NP:T] for j in range(QT)]
    for n, (c0, c1) in enumerate(ROUNDS):
        if n >= 4:
            pe.wait_ge(sem("rows_out"), n - 3)
        for c in range(c0, c1, P):
            mm = pe.transpose(ps[0:NS, 2 * (n % 4) + (c - c0) // 512, (c - c0) % 512:(c - c0) % 512 + P], tiles[c // P],
                              const(m, "ident"))
        mm.then_inc(sem("rows_mm"), 1)
    pe.wait_ge(sem("rows_out"), len(ROUNDS))
    pe.transpose(ps[0:NS, 0, 0:BG], m["bg"][:, NP:T], const(m, "ident")[0:BG, 0:BG]).then_inc(sem("rows_mm"), 1)
    pe.wait_ge(sem("rows_out"), len(ROUNDS) + 1)


def sample_rows_copy(m, dve, srow, srow2):
    sem, ps = m["sem"], m["ps"]
    for n, (c0, c1) in enumerate(ROUNDS):
        dve.wait_ge(sem("rows_mm"), n + 1)
        for h in range((c1 - c0) // 512):
            dst = srow[:, c0 + 512 * h:c0 + 512 * (h + 1)] if n < 4 else srow2[:, 0:512]
            ins = dve.tensor_copy(dst, ps[0:NS, 2 * (n % 4) + h, :])
        ins.then_inc(sem("rows_out"), 1)
    dve.wait_ge(sem("rows_mm"), len(ROUNDS) + 1)
    dve.tensor_copy(srow2[:, 512:512 + BG], ps[0:NS, 0, 0:BG]).then_inc(sem("rows_out"), 1)


def sample_rows_save(m, sp, srow, srow2):
    a, sem = m["a"], m["sem"]
    saved = sem("saved")
    sp.wait_ge(sem("rows_out"), len(ROUNDS) + 1)
    sp.dma_start(a["rows_rw"].rearrange("q (b h) c -> b q (h c)", b=NS),
                 srow[:, 0:RWROW].rearrange("b (q c) -> b q c", q=6)).then_inc(saved, 16)
    sp.dma_start(a["rows_gd"][0:2].rearrange("q (b h) c -> b q (h c)", b=NS),
                 srow[:, RWROW:RWROW + 1024].rearrange("b (q c) -> b q c", q=2)).then_inc(saved, 16)
    sp.dma_start(a["rows_gd"][2].rearrange("(b h) c -> b (h c)", b=NS), srow2[:, 0:512]).then_inc(saved, 16)
    for n, c in enumerate((0, 32)):
        sp.dma_start(a["rows_bg"][n].rearrange("(b h) -> b h", b=NS), srow2[:, 512 + c:512 + c + HG]).then_inc(saved, 16)
    m["saved"] += 80


def recur(m):
    nc, a, sem, ps, tmp = (m[k] for k in ("nc", "a", "sem", "ps", "tmp"))
    Praw, mix, conv, kk, bg, Gend = (m[k] for k in ("Praw", "mix", "conv", "kk", "bg", "Gend"))
    ident, pair, incl, sel = (const(m, n) for n in ("ident", "pair", "incl", "sel"))
    selv = sel.rearrange("p (h c) -> p h c", c=P)
    over4 = lambda ap: ap.unsqueeze(1).to_broadcast([P, 4, ap.shape[1]])
    flat = lambda ap, n: ap.rearrange("p a t -> p (a t)")[:, 0:n]
    AT, BT, KT, RT, VT = m["Gp"], m["aa"], mix[:, 4:8], mix[:, 0:4], mix[:, 8:12]
    oTr, oTg = m["oTr"], m["oTg"] = m["Gp"], conv[:, 0:4]
    AR = flat(Praw[:, 12:14], 1024).rearrange("p (j k t) -> p j k t", j=4, k=2)
    BK = flat(mix[:, 12:14], 1024).rearrange("p (j k t) -> p j k t", j=4, k=2)
    TTm = flat(m["stage"], 1536).rearrange("p (g h t) -> p g h t", g=3, h=4)
    TM = flat(m["Gi"], 1536).rearrange("p (g h t) -> p g h t", g=3, h=4)
    X = flat(m["G"], 1536).rearrange("p (g h t) -> p g h t", g=3, h=4)
    LM = flat(kk[:], 1536).rearrange("p (g h t) -> p g h t", g=3, h=4)
    VS, QKV, bgS = tmp("VS", [P, 4, P]), tmp("QKV", [P, QT, P]), tmp("bgS", [BG, P])
    Vt, Kt, Bt = tmp("Vt", [P, 512]), tmp("Kt", [P, 512]), tmp("Bt", [P, 512])
    rest = lambda ap: ap.rearrange("p a t -> p (a t)")[:, 1536:2048].rearrange("p (h t) -> p h t", h=4)
    gvt, gkd, kE, LG = rest(m["stage"]), rest(m["Gi"]), rest(m["G"]), rest(kk[:])
    bgt, E, qE = tmp("bgt", [P, BG]), tmp("E", [P, 4, P]), tmp("qE", [P, 4, P])
    dc, eC = tmp("dc", [P, 4]), tmp("eC", [P, 4])
    PR = tmp("PR", [P, HR, 4, P])
    W, U, gW, gU = tmp("W", [P, 512]), VS[:].rearrange("p j t -> p (j t)"), QKV[:, 8:12], QKV[:, 0:4]
    ST, S = tmp("ST", [P, 2, 4, 64]), tmp("S", [P, 4, P])
    wkv = W[0:64].rearrange("p (j k) -> p j k", j=4)
    srow, srow2 = PR[0:NS].rearrange("p h k t -> p (h k t)"), tmp("srow2", [NS, 512 + BG])
    LT = [PR[:, 0:4, 0], PR[:, 4:8, 0], LG]
    LEVELS = (2, 4, 8, 16, 32, 64)
    order = [(l, g) for l in range(6) for g in range(3) if l < 5 or g == 2]
    idx = {lg: n for n, lg in enumerate(order)}
    last = {0: 4, 1: 4, 2: 5}
    NL = len(order)
    K = dict(st_a=3, st_p=6, turn=4, tok=3, e_in=2, e_out=3, gv=1, pairs=3, pr=2, lg=1, intra=1, tt0=3, t_mm=3, t0=3,
             lm=NL, x_mm=NL, x_ev=NL, xt_mm=NL, upd=NL, wv_mm=1, wv=1, as_mm=2, w_ok=2, u_mm=2, u_ok=2, s_mm=2, s_ok=2,
             ost_mm=2, ost=4, ouv_mm=2, o_ok=2, gw_mm=1, gw=1, gu_mm=1, gu=1, go_mm=1, go=1, gs_mm=1, gs=1,
             bgt_ok=1, gkd_ok=1, qe=1, ke=1, ec=1)
    S_ = {n: sem("r_" + n) for n in K}

    SEED = dict(pairs=1, gs_mm=1, ouv_mm=1, o_ok=1, gs=1, s_ok=1, go=1)

    def seed(eng, *names):
        for n in names:
            eng.sem_inc(S_[n], SEED[n])

    def wait(eng, it, name, n):
        eng.wait_ge(S_[name], it * K[name] + (n + SEED.get(name, 0)))

    def wait_ahead(eng, it, signal):
        ahead(m, eng, S_[signal[0]], it * K[signal[0]] + (signal[1] + SEED.get(signal[0], 0)))

    tcols = lambda it: bass.ds(it * P, P)

    with nc.Block() as block:
        @block.scalar
        def _(act):
            cp = lambda o, i: act.activation(o, i, ACT.Copy)
            seed(act, "go")
            with act.Fori(0, NT) as it:
                wait_ahead(act, it, ("ouv_mm", 0))
                cp(AR[:, :, 0], AT[:, :, tcols(it)]).then_inc(S_["st_a"], 1)
                cp(AR[:, :, 1], RT[:, :, tcols(it)]).then_inc(S_["st_a"], 1)
                cp(VS[:], VT[:, :, tcols(it)]).then_inc(S_["st_a"], 1)
                for n, o in enumerate((Kt, Bt, Vt)):
                    wait(act, it, "turn", 1 if n < 2 else 4)
                    cp(o[:], ps[:, n, :]).then_inc(S_["tok"], 1)
                wait(act, it, "e_in", 2)
                act.activation(kE, ps[:, 7, :].rearrange("p (h t) -> p h t", h=4), ACT.Exp).then_inc(S_["e_out"], 1)
                act.activation(E[:], E[:], ACT.Exp).then_inc(S_["e_out"], 1)
                act.activation(dc[:], dc[:], ACT.Exp).then_inc(S_["e_out"], 1)
                for g in range(3):
                    wait(act, it, "t_mm", g + 1)
                    cp(TM[:, g], ps[:, 3 + g, :].rearrange("p (h t) -> p h t", h=4)).then_inc(S_["t0"], 1)

                def x_evac(n):
                    g = order[n][1]
                    wait(act, it, "x_mm", n + 1)
                    cp(X[:, g], ps[:, g, :].rearrange("p (h t) -> p h t", h=4)).then_inc(S_["x_ev"], 1)

                for n in range(NL):
                    x_evac(n)
                wait(act, it, "wv_mm", 1)
                cp(W[:], ps[:, 0, :]).then_inc(S_["wv"], 1)

                def u_evac(c):
                    wait(act, it, "u_mm", c + 1)
                    cp(U[64 * c:64 * c + 64, :], ps[64 * c:64 * c + 64, 2, :]).then_inc(S_["u_ok"], 1)

                def o_evac(c):
                    wait_ahead(act, it, ("ost_mm", c + 1))
                    for par, b in ((0, 1), (1, 5)):
                        r = slice(64 * par, 64 * par + 64)
                        cp(oTr[r, :, bass.ds(it * P + 64 * c, 64)], ps[r, b, 256:512].rearrange("p (j t) -> p j t", j=4)
                           ).then_inc(S_["ost"], 1)

                u_evac(0)
                wait(act, it, "gu_mm", 1)
                cp(gU, ps[:, 7, :].rearrange("p (h t) -> p h t", h=4)).then_inc(S_["gu"], 1)
                o_evac(0)
                wait_ahead(act, it, ("go_mm", 1))
                cp(oTg[:, :, tcols(it)], ps[:, 6, :].rearrange("p (h t) -> p h t", h=4)).then_inc(S_["go"], 1)
                u_evac(1)
                o_evac(1)

        @block.gpsimd
        def _(pool):
            cp = nc.gpsimd.tensor_copy
            with pool.Fori(0, NT) as it:
                wait(pool, it, "pairs", 0)
                cp(BK[:, :, 1], KT[:, :, tcols(it)]).then_inc(S_["st_p"], 1)
                cp(BK[:, :, 0], BT[:, :, tcols(it)]).then_inc(S_["st_p"], 1)
                cp(QKV[:, 4:8], conv[:, 4:8, tcols(it)]).then_inc(S_["st_p"], 1)
                cp(bgS[:], bg[:, tcols(it)]).then_inc(S_["st_p"], 1)
                wait(pool, it, "gs_mm", 0)
                cp(QKV[:, 8:12], conv[:, 8:12, tcols(it)]).then_inc(S_["st_p"], 1)
                cp(QKV[:, 0:4], conv[:, 0:4, tcols(it)]).then_inc(S_["st_p"], 1)
                for n, (l, g) in enumerate(order):
                    if l == 0:
                        wait(pool, it, "tt0", g + 1)
                    else:
                        wait(pool, it, "x_mm", idx[l - 1, g] + 1)
                    nc.gpsimd.tensor_tensor(LM[:, g], LT[g], over4(const(m, f"lvl{LEVELS[l]}")), ALU.mult
                                            ).then_inc(S_["lm"], 1)

        @block.vector
        def _(dve):
            st = Steps(dve, sem("r_dve"))
            by4 = lambda b: ps[:, b, :].rearrange("p (h t) -> p h t", h=4)
            percol = lambda ap: ap.unsqueeze(2).to_broadcast([P, 4, P])
            KS = 10
            seed(dve, "o_ok", "gs", "s_ok")
            dve.memset(ST[:], 0.0).then_inc(sem("r_zero"), 1)
            dve.memset(S[:], 0.0).then_inc(sem("r_zero"), 1)
            sample_rows_copy(m, dve, srow, srow2)
            dve.wait_ge(sem("r_zero"), 2)
            dve.wait_ge(sem("saved"), m["saved"] + 80)
            with dve.Fori(0, NT) as it:
                st.n, st.base = 0, it * KS
                wait(dve, it, "turn", 2)
                dve.tensor_copy(bgt[:], ps[:, 5, 0:BG]).then_inc(S_["bgt_ok"], 1)
                wait(dve, it, "bgt_ok", 1)
                dve.tensor_tensor(gvt, by4(3), percol(bgt[:, 0:4]), ALU.mult).then_inc(S_["gv"], 1)
                wait(dve, it, "turn", 3)
                st.did(dve.tensor_tensor(E[:], by4(7), percol(bgt[:, 32:36]), ALU.subtract))
                dve.tensor_tensor(dc[:], by4(7)[:, :, P - 1], bgt[:, 32:36], ALU.subtract).then_inc(S_["e_in"], 1)
                st.settled()
                dve.tensor_scalar(E[:], E[:], 0.0, None, ALU.min).then_inc(S_["e_in"], 1)
                wait(dve, it, "e_out", 3)
                dve.tensor_tensor(gkd, by4(4), percol(dc[:]), ALU.mult).then_inc(S_["gkd_ok"], 1)
                dve.tensor_tensor(qE[:], QKV[:, 0:4], kE, ALU.mult).then_inc(S_["qe"], 1)
                dve.tensor_copy(eC[:], kE[:, :, P - 1]).then_inc(S_["ec"], 1)
                wait(dve, it, "qe", 1)
                wait(dve, it, "ec", 1)
                st.link(dve.scalar_tensor_tensor(out=kE, in0=kE, scalar=-1.0, in1=QKV[:, 4:8], op0=ALU.mult, op1=ALU.mult))
                dve.tensor_tensor(kE, kE, by4(6), ALU.mult).then_inc(S_["ke"], 1)
                st.link(dve.scalar_tensor_tensor(out=LG, in0=E[:], scalar=-1.0, in1=by4(6), op0=ALU.mult, op1=ALU.mult))
                st.link(dve.tensor_tensor(E[:], E[:], over4(incl), ALU.mult))
                wait(dve, it, "pairs", 1)
                mask = pair.unsqueeze(1).to_broadcast([P, 8, 2 * P])
                prv = lambda h0: PR[:, h0:h0 + 4].rearrange("p h (x k) t -> p (h x) (k t)", x=2)
                dve.tensor_tensor(prv(0), ps[:, 0:4, :].rearrange("p h (x c) -> p (h x) c", x=2), mask, ALU.mult
                                  ).then_inc(S_["pr"], 1)
                wait(dve, it, "pairs", 2)
                dve.tensor_tensor(LG, LG, by4(4), ALU.mult).then_inc(S_["lg"], 1)
                dve.tensor_tensor(E[:], E[:], by4(5), ALU.mult).then_inc(S_["intra"], 1)
                wait(dve, it, "pairs", 3)
                dve.tensor_tensor(prv(4), ps[:, 4:8, :].rearrange("p h (x c) -> p (h x) c", x=2), mask, ALU.mult
                                  ).then_inc(S_["pr"], 1)
                for g in range(3):
                    wait(dve, it, *(("pr", 1), ("pr", 2), ("lg", 1))[g])
                    st.link(dve.tensor_tensor(LM[:, g], LT[g], over4(const(m, "lvl1")), ALU.mult))
                    dve.tensor_tensor(TTm[:, g], LM[:, g], over4(ident), ALU.add).then_inc(S_["tt0"], 1)
                for n, (l, g) in enumerate(order):
                    wait(dve, it, "xt_mm", n + 1)
                    if l < last[g]:
                        dve.tensor_tensor(TM[:, g], TM[:, g], by4(3 + g), ALU.add)
                    dve.tensor_tensor(TTm[:, g], TTm[:, g], by4(g), ALU.add).then_inc(S_["upd"], 1)

                def w_add(c):
                    wait(dve, it, "as_mm", c + 1)
                    wait(dve, it, "wv", 1)
                    r = slice(64 * c, 64 * c + 64)
                    for par, b in ((0, 1), (1, 5)):
                        w = W[r].rearrange("p (j q v) -> p j q v", j=4, q=2)[:, :, par]
                        ins = dve.tensor_tensor(w, w, ps[r, b, 0:256].rearrange("p (j v) -> p j v", j=4), ALU.add)
                        if par:
                            ins.then_inc(S_["w_ok"], 1)
                        else:
                            ins.then_inc(sem("r_w_even"), 1)

                def state(c):
                    wait(dve, it, "s_mm", c + 1)
                    st.link(dve.tensor_tensor(ST[:, 1 - c], ST[:, c], ps[:, 3, 0:256].rearrange("p (j v) -> p j v", j=4), ALU.add))
                    ge = Gend[:, :, bass.ds(it * 2 + c, 1)].to_broadcast([P, 4, 64])
                    dve.tensor_tensor(ST[:, 1 - c], ST[:, 1 - c], ge, ALU.mult).then_inc(S_["s_ok"], 1)

                def o_add(c):
                    wait(dve, it, "ouv_mm", c + 1)
                    wait(dve, it, "ost", 2 * c + 2)
                    o = oTr[:, :, bass.ds(it * P + 64 * c, 64)]
                    dve.tensor_tensor(o, o, ps[:, 4, 0:256].rearrange("p (j t) -> p j t", j=4), ALU.add).then_inc(S_["o_ok"], 1)

                w_add(0)
                wait(dve, it, "gw_mm", 1)
                dve.tensor_tensor(gW, gvt, by4(6), ALU.add).then_inc(S_["gw"], 1)
                state(0)
                o_add(0)
                wait(dve, it, "gs_mm", 1)
                st.link(dve.tensor_tensor(S[:], S[:], percol(eC[:]), ALU.mult))
                dve.tensor_tensor(S[:], S[:], by4(7), ALU.add).then_inc(S_["gs"], 1)
                w_add(1)
                state(1)
                o_add(1)
                assert st.n == KS, st.n
            st.n, st.base = 0, 0
            dve.wait_ge(sem("wkv_mm"), 1)
            dve.tensor_copy(wkv, ps[0:64, 0, :].rearrange("p (j k) -> p j k", j=4)).then_inc(sem("wkv_ok"), 1)

        @block.tensor
        def _(pe):
            by4 = lambda b: ps[:, b, :].rearrange("p (h t) -> p h t", h=4)
            seed(pe, "pairs", "gs_mm", "ouv_mm")
            sample_rows_turn(m, pe)
            pe.wait_ge(sem("r_zero"), 2)
            with pe.Fori(0, NT) as it:
                wait(pe, it, "o_ok", 0)
                wait(pe, it, "go", 0)
                wait(pe, it, "gs", 0)
                wait(pe, it, "s_ok", 0)
                wait(pe, it, "st_p", 6)
                for n, src in enumerate((BK[:, :, 1], BK[:, :, 0])):
                    for j in range(4):
                        mm = pe.transpose(ps[:, n, j * P:(j + 1) * P], src[:, j], ident)
                mm.then_inc(S_["turn"], 1)
                for n, j0 in ((3, 8), (4, 4)):
                    for j in range(4):
                        pe.transpose(ps[:, n, j * P:(j + 1) * P], QKV[:, j0 + j], ident)
                pe.transpose(ps[:, 5, 0:BG], bgS[:], ident[0:BG, 0:BG]).then_inc(S_["turn"], 1)
                for n in range(8):
                    mm = pe.matmul(ps[:, 6 + n // 4, (n % 4) * P:(n % 4 + 1) * P], selv[0:BG, n], bgS[:], start=True, stop=True)
                mm.then_inc(S_["turn"], 1)
                wait(pe, it, "st_a", 3)
                for j in range(4):
                    mm = pe.transpose(ps[:, 2, j * P:(j + 1) * P], VS[:, j], ident)
                mm.then_inc(S_["turn"], 1)

                def pairs(h0, b0):
                    for h in range(h0, h0 + 4):
                        r, j = slice(64 * (h % 2), 64 * (h % 2) + 64), h // 2
                        ar = AR[r, j].rearrange("p k t -> p (k t)")
                        pe.matmul(ps[:, b0 + h - h0, 0:256], BK[r, j, 0], ar, start=True, stop=True)
                        mm = pe.matmul(ps[:, b0 + h - h0, 256:512], BK[r, j, 1], ar, start=True, stop=True)
                    mm.then_inc(S_["pairs"], 1)

                wait(pe, it, "tok", 3)
                wait(pe, it, "gv", 1)
                pairs(0, 0)
                wait(pe, it, "gkd_ok", 1)
                for h in range(4):
                    pe.matmul(by4(4)[:, h], QKV[:, 4 + h], QKV[:, 4 + h], start=True, stop=True)
                    mm = pe.matmul(by4(5)[:, h], QKV[:, 4 + h], QKV[:, h], start=True, stop=True)
                mm.then_inc(S_["pairs"], 1)
                wait(pe, it, "lg", 1)
                wait(pe, it, "intra", 1)
                wait(pe, it, "ke", 1)
                pairs(4, 4)
                for g in range(3):
                    wait(pe, it, "tt0", g + 1)
                    if g == 0:
                        wait(pe, it, "pr", 2)
                    for h in range(4):
                        mm = pe.transpose(by4(3 + g)[:, h], TTm[:, g, h], ident)
                    mm.then_inc(S_["t_mm"], 1)

                def x_mm(n):
                    l, g = order[n]
                    wait(pe, it, "lm", n + 1)
                    if l == 0:
                        wait(pe, it, "t0", g + 1)
                    else:
                        wait(pe, it, "upd", idx[l - 1, g] + 1)
                    for h in range(4):
                        mm = pe.matmul(by4(g)[:, h], LM[:, g, h], TM[:, g, h], start=True, stop=True)
                    mm.then_inc(S_["x_mm"], 1)

                def xt_mm(n):
                    l, g = order[n]
                    wait(pe, it, "x_ev", n + 1)
                    for h in range(4):
                        if l < last[g]:
                            pe.matmul(by4(3 + g)[:, h], TTm[:, g, h], X[:, g, h], start=True, stop=True)
                        mm = pe.matmul(by4(g)[:, h], X[:, g, h], TTm[:, g, h], start=True, stop=True)
                    mm.then_inc(S_["xt_mm"], 1)

                for l in range(5):
                    for g in range(3):
                        x_mm(idx[l, g])
                    for g in range(3):
                        xt_mm(idx[l, g])
                x_mm(idx[5, 2])
                wait(pe, it, "upd", idx[4, 2] + 1)
                for h in range(HR):
                    mm = pe.matmul(ps[:, 0, h * 64:(h + 1) * 64], PR[:, h, 2], Vt[:, h * 64:(h + 1) * 64], start=True, stop=True)
                mm.then_inc(S_["wv_mm"], 1)

                def a_state(c):
                    if c == 1:
                        wait_ahead(pe, it, ("s_ok", 1))
                    for par, b in ((0, 1), (1, 5)):
                        r = slice(64 * par, 64 * par + 64)
                        for j in range(4):
                            mm = pe.matmul(ps[64 * c:64 * c + 64, b, j * 64:(j + 1) * 64], AR[r, j, 0, 64 * c:64 * c + 64],
                                           ST[r, c, j], start=True, stop=True)
                    mm.then_inc(S_["as_mm"], 1)

                def chunk(c):
                    r = slice(64 * c, 64 * c + 64)
                    wait_ahead(pe, it, ("w_ok", c + 1))
                    for h in range(HR):
                        mm = pe.matmul(ps[r, 2, h * 64:(h + 1) * 64], TTm[r, h // 4, h % 4, 64 * c:64 * c + 64],
                                       W[r, h * 64:(h + 1) * 64], start=True, stop=True)
                    mm.then_inc(S_["u_mm"], 1)

                def chunk_state(c):
                    r = slice(64 * c, 64 * c + 64)
                    wait_ahead(pe, it, ("u_ok", c + 1))
                    for h in range(HR):
                        o = ps[64 * (h % 2):64 * (h % 2) + 64, 3, (h // 2) * 64:(h // 2 + 1) * 64]
                        hc = slice(h * 64, (h + 1) * 64)
                        pe.matmul(o, Bt[r, hc], U[r, hc], start=True, stop=False)
                        mm = pe.matmul(o, Kt[r, hc], Vt[r, hc], start=False, stop=True)
                    mm.then_inc(S_["s_mm"], 1)
                    for par, b in ((0, 1), (1, 5)):
                        q = slice(64 * par, 64 * par + 64)
                        for j in range(4):
                            mm = pe.matmul(ps[q, b, 256 + j * 64:256 + (j + 1) * 64], ST[q, c, j], AR[q, j, 1, 64 * c:64 * c + 64],
                                           start=True, stop=True)
                    mm.then_inc(S_["ost_mm"], 1)
                    if c == 1:
                        wait_ahead(pe, it, ("o_ok", 1))
                    for h in range(HR):
                        o = ps[64 * (h % 2):64 * (h % 2) + 64, 4, (h // 2) * 64:(h // 2 + 1) * 64]
                        hc, tc = slice(h * 64, (h + 1) * 64), slice(64 * c, 64 * c + 64)
                        pe.matmul(o, U[r, hc], PR[r, h, 1, tc], start=True, stop=False)
                        mm = pe.matmul(o, Vt[r, hc], PR[r, h, 3, tc], start=False, stop=True)
                    mm.then_inc(S_["ouv_mm"], 1)

                a_state(0)
                for h in range(4):
                    mm = pe.matmul(by4(6)[:, h], kE[:, h], S[:, h], start=True, stop=True)
                mm.then_inc(S_["gw_mm"], 1)
                xt_mm(idx[5, 2])
                wait(pe, it, "gw", 1)
                wait(pe, it, "upd", NL)
                for h in range(4):
                    mm = pe.matmul(by4(7)[:, h], TTm[:, 2, h], gW[:, h], start=True, stop=True)
                mm.then_inc(S_["gu_mm"], 1)
                chunk(0)
                chunk_state(0)
                wait(pe, it, "gu", 1)
                wait(pe, it, "ost", 2)
                for h in range(4):
                    pe.matmul(by4(6)[:, h], S[:, h], qE[:, h], start=True, stop=False)
                    mm = pe.matmul(by4(6)[:, h], gU[:, h], E[:, h], start=False, stop=True)
                mm.then_inc(S_["go_mm"], 1)
                for h in range(4):
                    mm = pe.matmul(by4(7)[:, h], gkd[:, h], gU[:, h], start=True, stop=True)
                mm.then_inc(S_["gs_mm"], 1)
                a_state(1)
                chunk(1)
                chunk_state(1)
            pe.wait_ge(S_["s_ok"], 2 * NT + SEED["s_ok"])
            pe.wait_ge(S_["upd"], NL * NT)
            pe.wait_ge(S_["wv"], NT)
            for j in range(4):
                mm = pe.transpose(ps[0:64, 0, j * P:(j + 1) * P], ST[:, 0, j], ident)
            mm.then_inc(sem("wkv_mm"), 1)

        @block.sync
        def _(sp):
            sample_rows_save(m, sp, srow, srow2)
            done = sem("saved")
            sp.wait_ge(sem("wkv_ok"), 1)
            sp.dma_start(a["p_wkv"][0, 0].rearrange("h v k -> v h k"), wkv.rearrange("v j (q k) -> v (j q) k", q=2)
                         ).then_inc(done, 16)
            sp.wait_ge(S_["gs"], NT + SEED["gs"])
            sp.dma_start(a["p_ssm"][0, 0].rearrange("h k v -> k h v"), S[:]).then_inc(done, 16)
            sp.wait_ge(done, m["saved"] + 32)
            m["saved"] += 32


def sample_recur(m):
    nc, a, sem, ps, tmp = (m[k] for k in ("nc", "a", "sem", "ps", "tmp"))
    oTr, oTg, ident, sum4 = m["oTr"], m["oTg"], const(m, "ident"), const(m, "sum4")
    SR, rv, vh = tmp("SR", [P, 32, CR]), tmp("rv", [P, 6, CR]), tmp("vh", [P, 32])
    TR = m["mix"][:, 8:12].rearrange("p a t -> p (a t)")[:, 0:32 * CR].rearrange("p (v k) -> p v k", v=32)
    TG = m["mix"][:, 0:8].rearrange("p a t -> p (a t)")[:, 0:32 * CG].rearrange("p (k v) -> p k v", k=32)
    SG, gqk, gv, gb = tmp("SG", [P, 32, CG]), tmp("gqk", [P, 2, 32]), tmp("gv", [P, CG]), tmp("gb", [P, 3])
    spare = m["mix"][:, 12:14].rearrange("p a t -> p (a t)")
    sa, oR, part, oG, dl, oRrow = tmp("sa", [P, 32]), tmp("oR", [P, 32]), spare[:, 0:CG], spare[:, CG:2 * CG], spare[:, 2 * CG:3 * CG], (
        spare[0:NS, 3 * CG:3 * CG + 512])
    rin, gin, o_back = sem("s_rin"), sem("s_gin"), sem("s_oback")
    new_rw, new_gd, o_ready, part_ready, sum_mm, saved = (sem(n) for n in (
        "s_new_rw", "s_new_gd", "s_o_ready", "s_part", "s_sum", "s_saved"))
    NB = NS * HG
    GT = 2 * D // P
    m["gate_a"], m["gate_b"] = gates = m["Praw"][:, 8:8 + KD], m["Praw"][:, 16:16 + KD]
    GR = 4
    WG, w_ready, base = tmp("WG", [P, GR, KD, P]), [sem(f"weights{b}") for b in range(GR)], m["weights"]
    gate_mm, gate_out = sem("g_mm"), sem("g_out")
    with nc.Block() as block:
        @block.sync
        def _(sp):
            def load(b, col):
                sp.dma_start(WG[:, b], m["a"]["w_in"][0, :, bass.ds(col + GATE0, P)].rearrange("(k p) c -> p k c", p=P)
                             ).then_inc(w_ready[b], 16)

            for b in range(GR):
                load(b, b * P)
            with sp.Fori(0, GT // GR - 1) as it:
                for b in range(GR):
                    sp.wait_ge(gate_mm, it * GR + (b + 1))
                    load(b, it * (GR * P) + (GR + b) * P)

        @block.gpsimd
        def _(pool):
            for v in range(2):
                p = slice(64 * v, 64 * v + 64)
                nc.gpsimd.dma_start(SR[p], a["state_rwkv_wkv"][0].rearrange("b h v k -> (b h) v k")[:, 32 * v:32 * v + 32]).then_inc(rin, 16)
                nc.gpsimd.dma_start(rv[p], a["rows_rw"].rearrange("q p c -> p q c")).then_inc(rin, 16)
                nc.gpsimd.dma_start(vh[p], a["rows_rw"][3][:, 32 * v:32 * v + 32]).then_inc(rin, 16)
            for k in range(4):
                p = slice(NB * k, NB * k + NB)
                nc.gpsimd.dma_start(SG[p], a["state_gdn_ssm"][0].rearrange("b h k v -> (b h) k v")[:, 32 * k:32 * k + 32]).then_inc(gin, 16)
                nc.gpsimd.dma_start(gqk[p], a["rows_gd"][0:2, :, 32 * k:32 * k + 32].rearrange("q p c -> p q c")).then_inc(gin, 16)
                nc.gpsimd.dma_start(gv[p], a["rows_gd"][2]).then_inc(gin, 16)
                with nc.allow_non_contiguous_dma(reason="64 numbers"):
                    nc.gpsimd.dma_start(gb[p, 0:2], a["rows_bg"].rearrange("q p -> p q")).then_inc(gin, 16)
            pool.wait_ge(new_rw, 1)
            for v in range(2):
                p = slice(64 * v, 64 * v + 64)
                nc.gpsimd.dma_start(a["s_wkv"][0].rearrange("b h v k -> (b h) v k")[:, 32 * v:32 * v + 32], SR[p]).then_inc(saved, 16)
            pool.wait_ge(o_ready, 1)
            for v in range(2):
                nc.gpsimd.dma_start(a["o_rw"][:, 32 * v:32 * v + 32], oR[64 * v:64 * v + 64]).then_inc(o_back, 16)
            pool.wait_ge(o_back, 32)
            nc.gpsimd.dma_start(oRrow, a["o_rw"].rearrange("(b h) c -> b (h c)", b=NS)).then_inc(o_back, 16)
            pool.wait_ge(new_gd, 1)
            for k in range(4):
                p = slice(NB * k, NB * k + NB)
                nc.gpsimd.dma_start(a["s_ssm"][0].rearrange("b h k v -> (b h) k v")[:, 32 * k:32 * k + 32], SG[p]).then_inc(saved, 16)
            pool.wait_ge(saved, 16 * 6)

        @block.scalar
        def _(act):

            def gate_tiles(first, n):
                g, c = divmod(first, KD)
                with act.Fori(0, n) as it:
                    for b in range(2):
                        act.wait_ge(gate_mm, it * 2 + (first + b + 1))
                        act.activation(gates[g][:, bass.ds(it * 2 + (c + b), 1)].rearrange("p o (h t) -> p (o h) t", h=2),
                                       ps[:, 4 + 2 * b:6 + 2 * b, 0:TH], ACT.Sigmoid).then_inc(gate_out, 1)

            gate_tiles(0, 2)
            act.wait_ge(gin, 16 * 16)
            act.activation(gb[:, 2:3], gb[:, 1:2], ACT.Exp).then_inc(sem("s_exp_silu"), 1)
            gate_tiles(4, 2)
            act.wait_ge(sem("s_done"), 1)
            act.activation(norm_buffers(m)["zs"], m["Praw"][:, 26:30], ACT.Silu).then_inc(sem("s_exp_silu"), 1)
            norm_roots(m, act, 0)
            gate_tiles(8, 1)
            norm_roots(m, act, 2)
            gate_tiles(10, 3)

        @block.tensor
        def _(pe):
            def gate_tiles(first, n):
                for i in range(first, first + n):
                    b = i % GR
                    pe.wait_ge(w_ready[b], base[b] + 16 * (i // GR + 1))
                    pe.wait_ge(gate_out, i + 1)
                    for h in range(2):
                        for k in range(KD):
                            mm = pe.matmul(ps[:, 4 + 2 * (i % 2) + h, 0:TH], WG[:, b, k], m["xT"][:, k, h * TH:(h + 1) * TH],
                                           start=(k == 0), stop=(k == KD - 1))
                    mm.then_inc(gate_mm, 1)

            pe.sem_inc(gate_out, 2)
            gate_tiles(0, 6)
            for n in range(2):
                if n:
                    gate_tiles(6, 2)
                pe.wait_ge(part_ready, n + 1)
                pe.matmul(ps[:, n, 0:CG], sum4, part, start=True, stop=True).then_inc(sum_mm, 1)
            pe.wait_ge(sem("s_oG"), 1)
            pe.transpose(ps[:, 2, 0:NB], oG[0:NB, :], ident[0:NB, 0:NB]).then_inc(sum_mm, 1)
            pe.wait_ge(o_back, 48)
            for j in range(4):
                mm = pe.transpose(ps[:, 3, j * NS:(j + 1) * NS], oRrow[:, j * P:(j + 1) * P], ident[0:NS, 0:NS])
            mm.then_inc(sum_mm, 1)
            pe.wait_ge(sem("s_done"), 1)
            norm_sums(m, pe, (0, 1))
            gate_tiles(8, 2)
            norm_sums(m, pe, (2,))
            gate_tiles(10, 6)

        @block.vector
        def _(dve):
            st = Steps(dve, sem("dve_step"), m["dve"])
            TT = lambda o, x, y, op: st.link(dve.tensor_tensor(o, x, y, op))
            keys = lambda n: rv[:, n].unsqueeze(1).to_broadcast([P, 32, CR])
            vals = lambda ap: ap.unsqueeze(2).to_broadcast([P, 32, CR])
            dve.wait_ge(rin, 16 * 6)
            TT(TR, SR[:], keys(4), ALU.mult)
            st.did(dve.tensor_reduce(sa[:], TR, AXX, ALU.add))
            TT(SR[:], SR[:], keys(1), ALU.mult)
            TT(TR, vals(sa[:]), keys(5), ALU.mult)
            TT(SR[:], SR[:], TR, ALU.subtract)
            TT(TR, vals(vh[:]), keys(2), ALU.mult)
            TT(SR[:], SR[:], TR, ALU.add)
            dve.sem_inc(new_rw, 1)
            TT(TR, SR[:], keys(0), ALU.mult)
            st.link(dve.tensor_reduce(oR[:], TR, AXX, ALU.add))
            dve.sem_inc(o_ready, 1)
            dve.wait_ge(sem("s_exp_silu"), 1)
            gk = lambda n: gqk[:, n].unsqueeze(2).to_broadcast([P, 32, CG])
            gvv = lambda ap: ap.unsqueeze(1).to_broadcast([P, 32, CG])
            st.link(dve.tensor_scalar(SG[:], SG[:], gb[:, 2:3], None, ALU.mult))
            TT(TG, SG[:], gk(1), ALU.mult)
            dve.tensor_reduce(part, TG.rearrange("p k v -> p v k"), AXX, ALU.add).then_inc(part_ready, 1)
            dve.wait_ge(sum_mm, 1)
            TT(dl, gv[:], ps[:, 0, 0:CG], ALU.subtract)
            st.link(dve.tensor_scalar(dl, dl, gb[:, 0:1], None, ALU.mult))
            TT(TG, gk(1), gvv(dl), ALU.mult)
            TT(SG[:], SG[:], TG, ALU.add)
            dve.sem_inc(new_gd, 1)
            TT(TG, SG[:], gk(0), ALU.mult)
            dve.tensor_reduce(part, TG.rearrange("p k v -> p v k"), AXX, ALU.add).then_inc(part_ready, 1)
            dve.wait_ge(sum_mm, 2)
            dve.tensor_copy(oG, ps[:, 1, 0:CG]).then_inc(sem("s_oG"), 1)
            dve.wait_ge(sum_mm, 4)
            st.did(dve.tensor_copy(oTg[:, :, NP:T], ps[:, 2, 0:NB].rearrange("p (b h) -> p h b", b=NS)))
            st.did(dve.tensor_copy(oTr[:, :, NP:T], ps[:, 3, 0:4 * NS].rearrange("p (j b) -> p j b", j=4)))
            st.settled()
            dve.sem_inc(sem("s_done"), 1)
            norm_values(m, dve, st)
    m["weights"] = [w + 16 * GT // GR for w in m["weights"]]


def norm_buffers(m):
    mix = m["mix"]
    return dict(sqr=mix[:, 0:4], sqg=mix[:, 4:8], zs=mix[:, 8:12])


def norm_sums(m, pe, kinds):
    sem, ps, b = m["sem"], m["ps"], norm_buffers(m)
    ones, blk64 = const(m, "ones"), const(m, "blk64")
    for n in range(4 * kinds[0], 4 * kinds[-1] + 4):
        kind, j = n // 4, n % 4
        if n >= 2:
            pe.wait_ge(sem("n_out"), n - 1)
        if kind == 0:
            pe.wait_ge(sem("n_sqg"), 1)
        if kind == 2:
            pe.wait_ge(sem("n_sqr"), j + 1)
        w, x = ((ones, b["sqg"]), (blk64, m["oTr"]), (blk64, b["sqr"]))[kind]
        for h in range(2):
            mm = pe.matmul(ps[:, 2 * (n % 2) + h, 0:TH], w, x[:, j, h * TH:(h + 1) * TH], start=True, stop=True)
        mm.then_inc(sem("n_mm"), 1)


def norm_roots(m, act, kind):
    sem, ps, b, eps = m["sem"], m["ps"], norm_buffers(m), const(m, "eps")
    for n in range(4 * kind, 4 * kind + 4):
        act.wait_ge(sem("n_mm"), n + 1)
        act.wait_ge(sem("n_out"), n)
        d, w, e = (b["sqg"], CG, EPS_GD) if kind == 0 else (b["sqr"], CR, EPS_GN)
        act.activation(half(d[:, n % 4]), ps[:, 2 * (n % 2):2 * (n % 2) + 2, 0:TH], ACT.Sqrt, scale=1.0 / w,
                       bias=eps[:, e:e + 1]).then_inc(sem("n_out"), 1)


def norm_values(m, dve, st):
    sem, ps, b = m["sem"], m["ps"], norm_buffers(m)
    oTr, oTg, sqr, sqg, out = m["oTr"], m["oTg"], b["sqr"], b["sqg"], sem("n_out")
    dve.tensor_tensor(sqg, oTg, oTg, ALU.mult).then_inc(sem("n_sqg"), 1)
    for j in range(4):
        dve.wait_ge(sem("n_mm"), 5 + j)
        dve.wait_ge(out, 4 + j)
        dve.scalar_tensor_tensor(out=half(oTr[:, j]), in0=ps[:, 2 * (j % 2):2 * (j % 2) + 2, 0:TH], scalar=-1.0 / CR,
                                 in1=half(oTr[:, j]), op0=ALU.mult, op1=ALU.add).then_inc(out, 1)
        dve.wait_ge(out, 5 + j)
        dve.tensor_tensor(sqr[:, j], oTr[:, j], oTr[:, j], ALU.mult).then_inc(sem("n_sqr"), 1)
    st.link(dve.reciprocal(sqg, sqg))
    st.link(dve.tensor_tensor(oTg, oTg, sqg, ALU.mult))
    dve.wait_ge(sem("s_exp_silu"), 2)
    st.did(dve.scalar_tensor_tensor(out=oTg, in0=oTg, scalar=param(m, "gdn_norm_w"), in1=b["zs"], op0=ALU.mult, op1=ALU.mult))
    dve.wait_ge(out, 12)
    st.link(dve.reciprocal(sqr, sqr))
    st.link(dve.tensor_tensor(oTr, oTr, sqr, ALU.mult))
    for j in range(4):
        st.did(dve.tensor_scalar(oTr[:, j], oTr[:, j], param(m, "rwkv_ln_w", j), param(m, "rwkv_ln_b", j), ALU.mult, ALU.add))
    st.settled()
    st.link(dve.tensor_tensor(oTr, oTr, m["scr"][:], ALU.add))
    st.link(dve.tensor_tensor(oTr, oTr, m["gg"], ALU.mult))
    m["dve"] = st.n


def merge(m):
    nc, a, sem, ps, tmp, par, xT = (m[k] for k in ("nc", "a", "sem", "ps", "tmp", "par", "xT"))
    oTr, oTg, gates = m["oTr"], m["oTg"], (m["gate_a"], m["gate_b"])
    merged = m["mix"][:, 0:KD]
    WB, WO = tmp("WB", [P, 2, 2, 4, P]), tmp("WO", [P, 2, KD, P])
    w_ready, wo_ready = [sem(f"weights{b}") for b in range(2)], [sem(f"weights{b}") for b in (2, 3)]
    base, base_o = [m["weights"][b] for b in range(2)], [m["weights"][b] for b in (2, 3)]
    mm_done, y_out, t_sum, o_mm, o_out, x_sum = (sem("m_" + n) for n in ("mm", "y", "sum", "o_mm", "o_out", "x_sum"))
    m["xsum"] = xsum = m["kk"][:, 0:1]

    with nc.Block() as block:
        @block.sync
        def _(sp):
            def load(b, col):
                for n, src in enumerate((a["w_branch_a"], a["w_branch_b"])):
                    sp.dma_start(WB[:, b, n], src[0, :, bass.ds(col, P)].rearrange("(k p) c -> p k c", p=P)).then_inc(w_ready[b], 16)

            load(0, 0)
            load(1, P)
            for b in range(2):
                sp.dma_start(WO[:, b], a["w_out"][0, :, b * P:(b + 1) * P].rearrange("(k p) c -> p k c", p=P)).then_inc(wo_ready[b], 16)
            with sp.Fori(0, KD // 2 - 1) as it:
                for b in range(2):
                    sp.wait_ge(mm_done, it * 4 + (2 * b + 2))
                    load(b, it * (2 * P) + (2 + b) * P)
            with sp.Fori(0, KD // 2 - 1) as it:
                for b in range(2):
                    sp.wait_ge(o_mm, it * 2 + (b + 1))
                    sp.dma_start(WO[:, b], a["w_out"][0, :, bass.ds(it * (2 * P) + (2 + b) * P, P)]
                                 .rearrange("(k p) c -> p k c", p=P)).then_inc(wo_ready[b], 16)

        @block.tensor
        def _(pe):
            with pe.Fori(0, KD // 2) as it:
                for b in range(2):
                    pe.wait_ge(w_ready[b], it * 32 + (base[b] + 32))
                    pe.wait_ge(t_sum, it * 2 + (b + 1))
                    for n, x in enumerate((oTr, oTg)):
                        for h in range(2):
                            for k in range(4):
                                mm = pe.matmul(ps[:, 4 * b + 2 * n + h, 0:TH], WB[:, b, n, k], x[:, k, h * TH:(h + 1) * TH],
                                               start=(k == 0), stop=(k == 3))
                        mm.then_inc(mm_done, 1)
            pe.wait_ge(t_sum, KD + 2)
            with pe.Fori(0, KD // 2) as it:
                for b in range(2):
                    pe.wait_ge(wo_ready[b], it * 16 + (base_o[b] + 16))
                    pe.wait_ge(o_out, it * 2 + (b + 1))
                    for h in range(2):
                        for k in range(KD):
                            mm = pe.matmul(ps[:, 2 * b + h, 0:TH], WO[:, b, k], merged[:, k, h * TH:(h + 1) * TH],
                                           start=(k == 0), stop=(k == KD - 1))
                    mm.then_inc(o_mm, 1)

        @block.gpsimd
        def _(pool):
            nc.gpsimd.memset(xsum, 0.0).then_inc(x_sum, 1)
            with pool.Fori(0, KD // 2) as it:
                for b in range(2):
                    pool.wait_ge(x_sum, it * 2 + (b + 1))
                    pool.wait_ge(o_out, it * 2 + (b + 3))
                    nc.gpsimd.tensor_tensor(xsum, xsum, xT[:, bass.ds(it * 2 + b, 1)], ALU.add).then_inc(x_sum, 1)

        @block.vector
        def _(dve):
            dve.sem_inc(t_sum, 2)
            with dve.Fori(0, KD // 2) as it:
                for b in range(2):
                    g = [x[:, bass.ds(it * 2 + b, 1)] for x in gates]
                    for n in range(2):
                        dve.wait_ge(mm_done, it * 4 + (2 * b + n + 1))
                        x = g[n].rearrange("p o (h t) -> p (o h) t", h=2)
                        dve.tensor_tensor(x, x, ps[:, 4 * b + 2 * n:4 * b + 2 * n + 2, 0:TH], ALU.mult).then_inc(y_out, 1)
                    dve.wait_ge(y_out, it * 4 + (2 * b + 2))
                    dve.tensor_tensor(merged[:, bass.ds(it * 2 + b, 1)], g[0], g[1], ALU.add).then_inc(t_sum, 1)
            dve.sem_inc(o_out, 2)
            with dve.Fori(0, KD // 2) as it:
                for b in range(2):
                    dve.wait_ge(o_mm, it * 2 + (b + 1))
                    xt = xT[:, bass.ds(it * 2 + b, 1)].rearrange("p o (h t) -> p (o h) t", h=2)
                    dve.scalar_tensor_tensor(out=xt, in0=xt, scalar=ALPHA, in1=ps[:, 2 * b:2 * b + 2, 0:TH],
                                             op0=ALU.mult, op1=ALU.add).then_inc(o_out, 1)
    m["weights"] = [w + n * KD // 2 for w, n in zip(m["weights"], (32, 32, 16, 16))]


def norm1(m):
    nc, sem, ps, tmp, xT = (m[k] for k in ("nc", "sem", "ps", "tmp", "xT"))
    ones, eps = const(m, "ones"), const(m, "eps")
    sq, rt = tmp("n1_sq", [P, KD, T]), tmp("n1_rt", [P, T])
    mm_, centred, squared, rooted = (sem("n1_" + n) for n in ("mm", "centred", "squared", "rooted"))
    hs = [slice(h * TH, (h + 1) * TH) for h in range(2)]
    with nc.Block() as block:
        @block.tensor
        def _(pe):
            for h in range(2):
                pe.matmul(ps[:, h, 0:TH], ones, m["xsum"][:, 0, hs[h]], start=True, stop=True).then_inc(mm_, 1)
            for h in range(2):
                pe.wait_ge(squared, h + 1)
                for k in range(KD):
                    mm = pe.matmul(ps[:, 2 + h, 0:TH], ones, sq[:, k, hs[h]], start=(k == 0), stop=(k == KD - 1))
                mm.then_inc(mm_, 1)

        @block.scalar
        def _(act):
            for h in range(2):
                act.wait_ge(centred, h + 1)
                act.activation(sq[:, :, hs[h]], xT[:, :, hs[h]], ACT.Square).then_inc(squared, 1)
            for h in range(2):
                act.wait_ge(mm_, 3 + h)
                act.activation(rt[:, hs[h]], ps[:, 2 + h, 0:TH], ACT.Sqrt, scale=1.0 / D, bias=eps[:, EPS_LN:EPS_LN + 1]
                               ).then_inc(rooted, 1)

        @block.vector
        def _(dve):
            st = Steps(dve, sem("dve_step"), m["dve"])
            over = lambda ap: ap.unsqueeze(1).to_broadcast([P, KD, TH])
            for h in range(2):
                dve.wait_ge(mm_, h + 1)
                dve.scalar_tensor_tensor(out=xT[:, :, hs[h]], in0=over(ps[:, h, 0:TH]), scalar=-1.0 / D, in1=xT[:, :, hs[h]],
                                         op0=ALU.mult, op1=ALU.add).then_inc(centred, 1)
            for h in range(2):
                dve.wait_ge(rooted, h + 1)
                dve.wait_ge(squared, 2)
                st.link(dve.reciprocal(rt[:, hs[h]], rt[:, hs[h]]))
                st.link(dve.tensor_tensor(xT[:, :, hs[h]], xT[:, :, hs[h]], over(rt[:, hs[h]]), ALU.mult))
            for k in range(KD):
                st.did(dve.tensor_scalar(xT[:, k], xT[:, k], param(m, "ln1_g", k), param(m, "ln1_b", k), ALU.mult, ALU.add))
            st.settled()
            m["dve"] = st.n


HP = 16
NK = 128
TK = 16
PH = 8
TILES = [(n * P, P) for n in range(NT)] + [(NP, NS)]


def query(m):
    nc, a, sem, ps, tmp, xT = (m[k] for k in ("nc", "a", "sem", "ps", "tmp", "xT"))
    R = 4
    ring, qT = tmp("q_ring", [P, R, KD, P]), tmp("qT", [P, HP, T])
    keys, keysT = tmp("keys", [P, HP, P]), tmp("keysT", [P, HP, NK])
    x1row, parts, left = tmp("x1row", [P, NT + 1, D]), tmp("parts", [P, 2, 3, D], BF16), tmp("left", [P, 2, D])
    scores = m["scores"]
    base = m["weights"]
    w_in, k_in, k_mm, k_out = [sem(f"weights{b}") for b in range(R)], sem("q_kin"), sem("q_kmm"), sem("q_kout")
    q_mm, q_out, s_mm, s_out = (sem("q_" + n) for n in ("mm", "out", "smm", "sout"))
    r_mm, r_out = sem("x1_mm"), sem("x1_out")
    x1_saved = [sem(f"x1_saved{b}") for b in range(2)]
    sel_done, turned, taken = (sem("sel_" + n) for n in ("done", "turned", "taken"))

    with nc.Block() as block:
        @block.sync
        def _(sp):
            wq = a["peer_wq"]
            sp.dma_start(keys[:], a["peer_subkeys"][0].rearrange("h q n c -> n (h q) c")).then_inc(k_in, 16)
            for b in range(R):
                sp.dma_start(ring[:, b], wq[0, :, b * P:(b + 1) * P].rearrange("(k p) c -> p k c", p=P)).then_inc(w_in[b], 16)
            with sp.Fori(0, HP // R - 1) as it:
                for b in range(R):
                    sp.wait_ge(q_mm, it * R + (b + 1))
                    sp.dma_start(ring[:, b], wq[0, :, bass.ds(it * (R * P) + (R + b) * P, P)].rearrange("(k p) c -> p k c", p=P)
                                 ).then_inc(w_in[b], 16)

        @block.tensor
        def _(pe):
            for n, (t0, tn) in enumerate(TILES):
                if n >= 2:
                    pe.wait_ge(r_out, n - 1)
                for k in range(KD):
                    mm = pe.transpose(ps[0:tn, 4 + 2 * (n % 2) + k // 4, (k % 4) * P:(k % 4 + 1) * P], xT[:, k, t0:t0 + tn],
                                      const(m, "ident"))
                mm.then_inc(r_mm, 1)

            def queries(first, n):
                with pe.Fori(0, n) as it:
                    for b in range(R):
                        pe.wait_ge(w_in[b], it * 16 + (base[b] + 16 * first + 16))
                        pe.wait_ge(q_out, it * R + (R * first + b + 1))
                        for h in range(2):
                            for k in range(KD):
                                mm = pe.matmul(ps[:, 2 * (b % 2) + h, 0:TH], ring[:, b, k], xT[:, k, h * TH:(h + 1) * TH],
                                               start=(k == 0), stop=(k == KD - 1))
                        mm.then_inc(q_mm, 1)

            def score(n, halves, bank):
                t0, tn = TILES[n]
                for j in range(halves[0], halves[1]):
                    c = j - halves[0]
                    mm = pe.matmul(ps[0:tn, bank + c // 4, (c % 4) * P:(c % 4 + 1) * P], qT[:, j, t0:t0 + tn],
                                   keysT[:, j], start=True, stop=True)
                mm.then_inc(s_mm, 1)

            pe.wait_ge(k_in, 16)
            pe.wait_ge(r_out, NT + 1)
            for j in range(HP):
                mm = pe.transpose(ps[:, 4 + j // 4, (j % 4) * P:(j % 4 + 1) * P], keys[:, j], const(m, "ident"))
            mm.then_inc(k_mm, 1)
            queries(0, 2)
            pe.wait_ge(k_out, 1)
            pe.wait_ge(q_out, 2 + HP // 2)
            score(0, (0, HP // 2), 4)
            queries(2, 2)
            pe.wait_ge(q_out, 2 + HP)
            score(0, (HP // 2, HP), 6)
            for n in range(1, NT + 1):
                if n >= 2:
                    pe.wait_ge(s_out, n)
                score(n, (0, HP), 4 * ((n + 1) % 2))
            pe.wait_ge(s_out, NT + 2)
            pe.wait_ge(sel_done, 2)
            turn_chosen(m, pe, 4)

        @block.gpsimd
        def _(pool):
            nc.gpsimd.memset(scores[:, NT * HP:], 0.0).then_inc(sem("q_zero"), 1)
            st = Steps(pool, sem("x1_pool"))
            for n, (t0, tn) in enumerate(TILES):
                b = n % 2
                pool.wait_ge(r_out, n + 1)
                if n >= 2:
                    pool.wait_ge(x1_saved[b], 64 * (n // 2))
                src = x1row[0:tn, n]
                for q in range(3):
                    st.link(nc.gpsimd.tensor_copy(parts[0:tn, b, q], src))
                    if q < 2:
                        st.link(nc.gpsimd.tensor_tensor(left[0:tn, b], src, parts[0:tn, b, q], ALU.subtract))
                        src = left[0:tn, b]
                nc.gpsimd.dma_start(a["x1_rows"][t0:t0 + tn, :], x1row[0:tn, n]).then_inc(x1_saved[b], 16)
                for q in range(3):
                    nc.gpsimd.dma_start(a["x1_parts"][q, t0:t0 + tn, :], parts[0:tn, b, q]).then_inc(x1_saved[b], 16)
            for b in range(2):
                pool.wait_ge(x1_saved[b], 64 * len(TILES[b::2]))

        @block.scalar
        def _(act):
            act.sem_inc(q_out, 2)
            for n, (t0, tn) in enumerate(TILES):
                act.wait_ge(r_mm, n + 1)
                b = 4 + 2 * (n % 2)
                act.activation(x1row[0:tn, n].rearrange("p (b c) -> p b c", b=2), ps[0:tn, b:b + 2, :], ACT.Copy
                               ).then_inc(r_out, 1)
            act.wait_ge(sem("q_zero"), 1)

            def queries(first, n):
                with act.Fori(0, n) as it:
                    for b in range(R):
                        act.wait_ge(q_mm, it * R + (R * first + b + 1))
                        act.activation(qT[:, bass.ds(it * R + (R * first + b), 1), :].rearrange("p o (h t) -> p (o h) t", h=2),
                                       ps[:, 2 * (b % 2):2 * (b % 2) + 2, 0:TH], ACT.Copy).then_inc(q_out, 1)

            def score(count, n, halves, bank):
                tn, banks = TILES[n][1], (halves[1] - halves[0]) // 4
                act.wait_ge(s_mm, count)
                act.activation(scores[0:tn, n * HP + halves[0]:n * HP + halves[1]].rearrange("p (b j) n -> p b (j n)", b=banks),
                               ps[0:tn, bank:bank + banks, :], ACT.Copy).then_inc(s_out, 1)

            act.wait_ge(k_mm, 1)
            act.activation(keysT[:].rearrange("p (b j) n -> p b (j n)", b=4), ps[:, 4:8, :], ACT.Copy).then_inc(k_out, 1)
            queries(0, 2)
            score(1, 0, (0, HP // 2), 4)
            queries(2, 1)
            choose_exp(m, act, 0)
            queries(3, 1)
            score(2, 0, (HP // 2, HP), 6)
            for n in range(1, NT + 1):
                score(n + 2, n, (0, HP), 4 * ((n + 1) % 2))
            choose_exp(m, act, 1)
            act.wait_ge(turned, 1)
            act.activation(m["idxT"][:, 0:P], ps[:, 4, 0:P], ACT.Copy).then_inc(taken, 1)
            act.activation(m["gateT"][:, 0:P], ps[:, 5, 0:P], ACT.Copy).then_inc(taken, 1)

        @block.vector
        def _(dve):
            st = Steps(dve, sem("dve_step"), m["dve"])
            for n in range(2):
                dve.wait_ge(s_out, n + 1)
                for k in range(32):
                    choose(m, dve, st, k // 4, k % 4, n, 8 * n, 4 * n)
            m["dve"] = st.n


CH = 4
LOWEST = -3.0e38


def choose_buffers(m, sb):
    for name, shape, dt in (("work", [P, 2 * CH, NK], F32), ("top", [P, 2 * CH, TK], F32), ("topi", [P, 2 * CH, TK], U32),
                            ("topf", [P, 2 * CH, TK], F32), ("cand", [P, CH, TK * TK], F32), ("one", [P, CH, TK, TK], F32),
                            ("best", [P, CH, TK], F32), ("besti", [P, CH, TK], U32), ("pos", [P, 2, CH, TK], U32),
                            ("posf", [P, 2, CH, TK], F32), ("pair_ids", [P, 2, CH, TK], F32), ("ex", [P, CH, TK], F32),
                            ("exsum", [P, CH], F32), ("ids", [P, PH, TK], F32), ("gates", [P, PH, TK], F32)):
        m["c_" + name] = sb("c_" + name, shape, dt)


def choose(m, dve, st, stage, part, n, row, head):
    sem = m["sem"]
    (work, top, topi, topf, cand, one, best, besti, pos, posf, pair_ids, ex, exsum, ids, gates) = (m["c_" + k][:] for k in (
        "work", "top", "topi", "topf", "cand", "one", "best", "besti", "pos", "posf", "pair_ids", "ex", "exsum", "ids", "gates"))
    full = [P, CH, TK, TK]
    iota = const(m, "iota16").unsqueeze(1).unsqueeze(1).to_broadcast(full)
    keys = topf.rearrange("p (h q) k -> p h q k", q=2)
    pair = (2 * part, 2 * part + 1)
    r = part

    def settled():
        ahead(m, dve, st.sem, st.base + st.n)

    def link(ins):
        st.did(ins)
        settled()

    if stage == 0:
        if part == 0:
            link(dve.tensor_copy(work, m["scores"][:, bass.ds(row, 2 * CH)]))
        for k in pair:
            st.did(dve.max(top[:, k, 0:8], work[:, k]))
        settled()
    elif stage == 1:
        for k in pair:
            st.did(dve.max_index(topi[:, k, 0:8], top[:, k, 0:8], work[:, k]))
        settled()
    elif stage == 2:
        for k in pair:
            st.did(dve.match_replace(work[:, k], top[:, k, 0:8], work[:, k], LOWEST))
        settled()
    elif stage == 3:
        for k in pair:
            st.did(dve.max(top[:, k, 8:16], work[:, k]))
        settled()
    elif stage == 4:
        for k in pair:
            st.did(dve.max_index(topi[:, k, 8:16], top[:, k, 8:16], work[:, k]))
        h = slice(part, part + 1)
        v = top[:, 2 * part:2 * part + 2].rearrange("p (h q) k -> p h q k", q=2)
        st.did(dve.tensor_tensor(cand[:, h].rearrange("p h (i j) -> p h i j", i=TK),
                                 v[:, :, 0].unsqueeze(3).to_broadcast([P, 1, TK, TK]),
                                 v[:, :, 1].unsqueeze(2).to_broadcast([P, 1, TK, TK]), ALU.add))
        settled()
        if part == 3:
            link(dve.tensor_copy(topf, topi))
    elif stage == 5:
        link(dve.max(best[:, r, 0:8], cand[:, r]))
        link(dve.max_index(besti[:, r, 0:8], best[:, r, 0:8], cand[:, r]))
        link(dve.match_replace(cand[:, r], best[:, r, 0:8], cand[:, r], LOWEST))
    elif stage == 6:
        link(dve.max(best[:, r, 8:16], cand[:, r]))
        link(dve.max_index(besti[:, r, 8:16], best[:, r, 8:16], cand[:, r]))
        if part == 3:
            dve.tensor_tensor(ex, best, best[:, :, 0:1].to_broadcast([P, CH, TK]), ALU.subtract).then_inc(sem("sel_tops"), 1)
            st.did(dve.tensor_scalar(pos[:, 0], besti, 4, None, ALU.logical_shift_right))
            st.did(dve.tensor_scalar(pos[:, 1], besti, 15, None, ALU.bitwise_and))
            settled()
            link(dve.tensor_copy(posf, pos))
    elif stage == 7:
        q = part // 2
        if part % 2 == 0:
            link(dve.tensor_tensor(one, posf[:, q].unsqueeze(3).to_broadcast(full), iota, ALU.is_equal))
            link(dve.tensor_tensor(one, one, keys[:, :, q].unsqueeze(2).to_broadcast(full), ALU.mult))
        else:
            link(dve.tensor_reduce(pair_ids[:, q], one, AXX, ALU.add))
        if part == 3:
            st.did(dve.scalar_tensor_tensor(out=ids[:, bass.ds(head, CH)], in0=pair_ids[:, 0], scalar=float(NK),
                                            in1=pair_ids[:, 1], op0=ALU.mult, op1=ALU.add))
            ahead(m, dve, sem("sel_exps"), n + 1)
            link(dve.tensor_reduce(exsum, ex, AXX, ALU.add))
            link(dve.reciprocal(exsum, exsum))
            link(dve.tensor_tensor(gates[:, bass.ds(head, CH)], ex, exsum.unsqueeze(2).to_broadcast([P, CH, TK]), ALU.mult))
            dve.sem_inc(sem("sel_done"), 1)


def choose_exp(m, act, n):
    act.wait_ge(m["sem"]("sel_tops"), n + 1)
    act.activation(m["c_ex"][:], m["c_ex"][:], ACT.Exp).then_inc(m["sem"]("sel_exps"), 1)


def turn_chosen(m, pe, bank):
    for q, name in enumerate(("c_ids", "c_gates")):
        mm = pe.transpose(m["ps"][:, bank + q, 0:P], m[name][:].rearrange("p h k -> p (h k)"), const(m, "ident"))
    mm.then_inc(m["sem"]("sel_turned"), 1)


STEP, GROUP = 32, 16
RU, RV = 8, 16
BATCH = 4
UB = 2
LEAD = 8


def experts(m):
    assert LEAD == RU == NS and LEAD % BATCH == 0
    nc, a, sem, ps, tmp, idxT, gateT = (m[k] for k in ("nc", "a", "sem", "ps", "tmp", "idxT", "gateT"))
    U, V = tmp("U_rows", [P, RU, D]), tmp("V_rows", [P, RV, D])
    ixs, gs = tmp("ixs", [P, 2, GROUP], U32), tmp("gs", [P, 2, GROUP])
    pick = tmp("pick", [48, GROUP, P], BF16)
    pick1 = tmp("pick1", [48, GROUP])
    xp = tmp("xp", [48, 2, D], BF16)
    hp, hg, hz = tmp("hp", [P, STEP]), tmp("hg", [P, 2, BATCH]), tmp("hz", [P, 2, GROUP, GROUP])
    free = m["xT"][0:GROUP].rearrange("p k t -> p (k t)")
    y, g2, b2 = free[:, 0:2 * D].rearrange("p (g d) -> p g d", g=2), free[:, 2 * D:3 * D], free[:, 3 * D:4 * D]
    scrap = m["c_work"][0:GROUP].rearrange("p h n -> p (h n)")
    stat = tmp("stat", [GROUP, 4])
    u_in, v_in = [sem(f"e_u{k}") for k in range(RU // UB)], [sem(f"e_v{k}") for k in range(RV // BATCH)]
    xp_in, x_in = [sem(f"e_xp{g}") for g in range(2)], [sem(f"e_x{g}") for g in range(2)]
    (zeroed, staged, xb_done, h_done, gelu_ok, hz_ok, mm_done, ff_used, y_ok, var_ok, root_ok, gb_in) = (
        sem("e_" + n) for n in ("zeroed", "staged", "xb", "h", "gelu", "hz", "mm", "ff_used", "y", "var", "root", "gb"))
    sel_done, turned, taken = (sem("sel_" + n) for n in ("done", "turned", "taken"))
    saved, base = sem("saved"), m["saved"]
    ITS, PT_ = NP // STEP, P // STEP
    diag = lambda g, t, n: hz[:, g].rearrange("p t m -> p (t m)")[:, t * (GROUP + 1):(t + n - 1) * (GROUP + 1) + 1:GROUP + 1]

    def tiles(eng, body, between=None):
        with eng.Fori(0, NT) as n:
            with eng.Fori(0, 2) as q:
                body(n * PT_ + q, STEP, n * 2 + q, q)
            if between:
                between(n)
            with eng.Fori(0, 2) as q:
                body(n * PT_ + (q + 2), STEP)
        body(ITS, NS)

    with nc.Block() as block:
        @block.sync
        def _(sp):
            def load_parts(it, g, tn=GROUP):
                t0 = it * STEP + g * GROUP
                for q in range(3):
                    sp.dma_start(xp[q * GROUP:q * GROUP + tn, g], a["x1_parts"][q, bass.ds(t0, tn), :]).then_inc(xp_in[g], 16)

            def load_x(it, g, tn=GROUP):
                sp.dma_start(y[0:tn, g], a["x1_rows"][bass.ds(it * STEP + g * GROUP, tn), :]).then_inc(x_in[g], 16)

            def save(it, g):
                ahead(m, sp, y_ok, it * 2 + (g + 1))
                samples = isinstance(it, int) and it == ITS
                dst = a["y_sample"].rearrange("b o d -> (b o) d") if samples else (
                    a["y_prompt"][0, bass.ds(it * STEP + g * GROUP, GROUP), :])
                sp.dma_start(dst, y[0:dst.shape[0], g]).then_inc(saved, 16)
                ahead(m, sp, saved, it * 32 + (base + 16 * (g + 1)))

            sp.dma_start(g2, a["ln2_g"].to_broadcast([GROUP, D])).then_inc(gb_in, 16)
            sp.dma_start(b2, a["ln2_b"].to_broadcast([GROUP, D])).then_inc(gb_in, 16)
            sp.wait_ge(zeroed, 2)
            for g in range(2):
                load_parts(0, g)
                load_x(0, g)
            with sp.Fori(0, ITS - 1) as it:
                for g in range(2):
                    sp.wait_ge(xb_done, it * STEP + GROUP * (g + 1))
                    load_parts(it + 1, g)
                    save(it, g)
                    load_x(it + 1, g)
            sp.wait_ge(xb_done, ITS * STEP - GROUP)
            load_parts(ITS, 0, NS)
            save(ITS - 1, 0)
            load_x(ITS, 0, NS)
            save(ITS - 1, 1)
            save(ITS, 0)
            m["saved"] = base + 16 * (2 * ITS + 1)

        @block.gpsimd
        def _(pool):
            def gather(it, tokens):
                for t in range(tokens):
                    g = t // GROUP
                    if t % GROUP == 0:
                        n = min(tokens, GROUP)
                        nc.gpsimd.tensor_copy(ixs[:, g, 0:n], idxT[:, bass.ds(it * STEP + t, n)]).then_inc(staged, 1)
                        nc.gpsimd.tensor_copy(gs[:, g, 0:n], gateT[:, bass.ds(it * STEP + t, n)]).then_inc(staged, 1)
                        pool.wait_ge(staged, it * 4 + 2 * (g + 1))
                    ku, kv = t % RU, t % RV
                    off = lambda: bass.IndirectOffsetOnAxis(ap=ixs[:, g, t % GROUP:t % GROUP + 1], axis=0)
                    ahead(m, pool, h_done, it * STEP + (t + 1))
                    nc.gpsimd.indirect_dma_start(U[:, ku, :], None, a["peer_u"][0], off()).then_inc(u_in[ku // UB], 16)
                    ahead(m, pool, mm_done, it * STEP + (t + 1))
                    nc.gpsimd.indirect_dma_start(V[:, kv, :], None, a["peer_v"][0], off()).then_inc(v_in[kv // BATCH], 16)

            with pool.Fori(0, NT) as n:
                ahead(m, pool, taken, n * 2 + 2)
                with pool.Fori(0, PT_) as q:
                    gather(n * PT_ + q, STEP)
            pool.wait_ge(taken, 2 * NT + 2)
            gather(ITS, NS)

        @block.vector
        def _(dve):
            st = Steps(dve, sem("dve_step"), m["dve"])
            dve.sem_inc(h_done, RU)
            dve.sem_inc(ff_used, 2)
            dve.memset(hz[:], 0.0).then_inc(zeroed, 1)
            dve.memset(xp[:], 0.0).then_inc(zeroed, 1)
            st.link(dve.tensor_tensor(pick1[:], const(m, "mod16")[0:48].to_broadcast([48, GROUP]), const(m, "iota16")[0:48],
                                      ALU.is_equal))
            dve.tensor_copy(pick[:], pick1[:].unsqueeze(2).to_broadcast([48, GROUP, P])).then_inc(zeroed, 1)
            dve.wait_ge(zeroed, 3)
            dve.wait_ge(gb_in, 32)
            choosing, norming = Steps(dve, sem("e_choose")), Steps(dve, sem("e_norm"))
            NORM, NPARTS = 7, 6

            def norm(it, g, tn, part):
                if part == 0:
                    norming.n, norming.base = 0, it * (2 * NORM) + g * NORM
                x, s = y[0:tn, g], stat[0:tn]
                two = lambda ap: ap.rearrange("p (b c) -> p b c", b=2)
                if part == 0:
                    dve.wait_ge(mm_done, it * STEP + (g * GROUP + tn + RV))
                    dve.wait_ge(x_in[g], it * 16 + 16)
                    dve.scalar_tensor_tensor(out=two(x), in0=two(x), scalar=ALPHA, in1=ps[0:tn, 4 + 2 * g:6 + 2 * g, :],
                                             op0=ALU.mult, op1=ALU.add).then_inc(ff_used, 1)
                elif part == 1:
                    dve.wait_ge(ff_used, it * 2 + (g + 3))
                    norming.link(dve.tensor_reduce(s[:, 0:1], x, AXX, ALU.add))
                    norming.link(dve.tensor_scalar(s[:, 0:1], s[:, 0:1], 1.0 / D, None, ALU.mult))
                elif part == 2:
                    norming.link(dve.tensor_scalar(x, x, s[:, 0:1], None, ALU.subtract))
                elif part == 3:
                    norming.link(dve.tensor_tensor_reduce(scrap[0:tn], x, x, 1.0, 0.0, ALU.mult, ALU.add, s[:, 1:2]))
                    dve.sem_inc(var_ok, 1)
                elif part == 4:
                    dve.wait_ge(root_ok, it * 2 + (g + 1))
                    norming.link(dve.reciprocal(s[:, 3:4], s[:, 2:3]))
                    norming.link(dve.scalar_tensor_tensor(out=x, in0=x, scalar=s[:, 3:4], in1=g2[0:tn], op0=ALU.mult, op1=ALU.mult))
                else:
                    norming.link(dve.tensor_tensor(x, x, b2[0:tn], ALU.add))
                    dve.sem_inc(y_ok, 1)
                    assert norming.n == NORM

            def weigh(it, b):
                dve.wait_ge(gelu_ok, it * (STEP // BATCH) + (b + 1))
                g, t = b * BATCH // GROUP % 2, b * BATCH % GROUP
                dve.tensor_tensor(diag(g, t, BATCH), hg[:, b % 2], gs[:, g, t:t + BATCH], ALU.mult).then_inc(hz_ok, 1)

            def dot(it, t):
                k = t % RU
                dve.wait_ge(xb_done, it * STEP + (t + 1))
                if t % UB == 0:
                    dve.wait_ge(u_in[k // UB], it * (16 * UB * STEP // RU) + 16 * UB * (t // RU + 1))
                u = U[:, k, :].rearrange("p (b c) -> p b c", b=2)
                dve.tensor_tensor_reduce(u, u, ps[:, 2 * (t % 2):2 * (t % 2) + 2, :], 1.0, 0.0, ALU.mult, ALU.add,
                                         hp[:, t % STEP:t % STEP + 1]).then_inc(h_done, 1)
                if t % BATCH == 0 and t:
                    weigh(it, t // BATCH - 1)

            def dots(it, n, chosen=None, q=None):
                if n == NS:
                    weigh(it, LEAD // BATCH - 1)
                else:
                    if chosen is not None:
                        choosing.n, choosing.base = 0, chosen * CSTEPS
                    for t in range(n):
                        dot(it, t + LEAD)
                        if chosen is not None:
                            choose(m, dve, choosing, t // 4, t % 4, chosen + 2, chosen * 8 + 16, q * CH)
                        if GROUP < t <= GROUP + NPARTS:
                            norm(it, 0, GROUP, t - GROUP - 1)
                for part in range(NPARTS):
                    norm(it, (n - 1) // GROUP, min(n, GROUP), part)
                if chosen is not None:
                    assert choosing.n == CSTEPS, choosing.n

            for t in range(LEAD):
                dot(0, t)
            CSTEPS = 8 * 5 + 1 + 5 + 4 * 5 + 3 + 7 + 3
            tiles(dve, dots)

        @block.scalar
        def _(act):
            def root(it, g, tn):
                act.wait_ge(var_ok, it * 2 + (g + 1))
                act.activation(stat[0:tn, 2:3], stat[0:tn, 1:2], ACT.Sqrt, scale=1.0 / D,
                               bias=const(m, "eps")[0:tn, EPS_LN:EPS_LN + 1]).then_inc(root_ok, 1)

            def gelu(it, b):
                act.wait_ge(h_done, it * STEP + (BATCH * b + BATCH + RU))
                c = BATCH * b % STEP
                act.activation(hg[:, b % 2], hp[:, c:c + BATCH], ACT.Gelu).then_inc(gelu_ok, 1)

            def gelus(it, n, chosen=None, q=None):
                if n == STEP:
                    for b in range(LEAD // BATCH, (STEP + LEAD) // BATCH):
                        gelu(it, b)
                        if b == 6:
                            root(it, 0, GROUP)
                        if b == 8 and chosen is not None:
                            choose_exp(m, act, chosen + 2)
                root(it, (n - 1) // GROUP, min(n, GROUP))

            def take(n):
                act.wait_ge(turned, n + 2)
                act.activation(idxT[:, bass.ds((n + 1) * P, P)], ps[:, 0, 0:P], ACT.Copy).then_inc(taken, 1)
                act.activation(gateT[:, bass.ds((n + 1) * P, P)], ps[:, 1, 0:P], ACT.Copy).then_inc(taken, 1)

            for b in range(LEAD // BATCH):
                gelu(0, b)
            tiles(act, gelus, take)

        @block.tensor
        def _(pe):
            pe.sem_inc(mm_done, RV)
            pe.wait_ge(zeroed, 3)

            def spread(it, t):
                g = t // GROUP % 2
                if t % GROUP == 0:
                    pe.wait_ge(xp_in[g], it * 48 + 48 * (t // STEP + 1))
                pe.wait_ge(h_done, it * STEP + (t + RU - 1))
                for h in range(2):
                    mm = pe.matmul(ps[:, 2 * (t % 2) + h, :], pick[:, t % GROUP, :], xp[:, g, h * 512:(h + 1) * 512],
                                   start=True, stop=True)
                mm.then_inc(xb_done, 1)

            def add_rows(it, t, n):
                g, tg = t // GROUP, t % GROUP
                if t % BATCH == 0:
                    pe.wait_ge(hz_ok, it * (STEP // BATCH) + (t // BATCH + 1))
                    pe.wait_ge(v_in[t % RV // BATCH], it * (16 * BATCH * STEP // RV) + 16 * BATCH * (t // RV + 1))
                if tg == 0:
                    pe.wait_ge(ff_used, it * 2 + (g + 1))
                tn = min(n, GROUP)
                for h in range(2):
                    mm = pe.matmul(ps[0:tn, 4 + 2 * g + h, :], hz[:, g, tg, 0:tn], V[:, t % RV, h * 512:(h + 1) * 512],
                                   start=(tg == 0), stop=(tg == tn - 1))
                mm.then_inc(mm_done, 1)

            def tokens(it, n, chosen=None, q=None):
                for t in range(n):
                    if n == STEP:
                        spread(it, t + LEAD)
                    add_rows(it, t, n)

            def turn(n):
                pe.wait_ge(sel_done, n * 2 + 4)
                pe.wait_ge(h_done, n * P + (2 * STEP + LEAD + RU))
                turn_chosen(m, pe, 0)
                ahead(m, pe, taken, n * 2 + 4)

            for t in range(LEAD):
                spread(0, t)
            tiles(pe, tokens, turn)


_INS = ['x_prompt', 'x_sample', 'state_rwkv_shift', 'state_rwkv_wkv', 'state_gdn_conv', 'state_gdn_ssm', 'w_in', 'rwkv_mu',
        'rwkv_w0', 'rwkv_w2', 'rwkv_a0', 'rwkv_a2', 'rwkv_g2', 'rwkv_k_k', 'rwkv_k_a', 'rwkv_r_k', 'rwkv_ln_w', 'rwkv_ln_b',
        'gdn_conv_w', 'gdn_a_log', 'gdn_dt_bias', 'gdn_norm_w', 'w_branch_a', 'w_branch_b', 'w_out', 'ln1_g', 'ln1_b',
        'peer_wq', 'peer_subkeys', 'peer_u', 'peer_v', 'ln2_g', 'ln2_b']

_SHAPES = {"y_prompt": (1, NP, D), "y_sample": (NS, 1, D), "p_shift": (1, 1, RW_COLS), "p_wkv": (1, 1, HR, CR, CR),
           "p_conv": (1, 1, 3, GD_QKV), "p_ssm": (1, 1, HG, CG, CG), "s_shift": (1, NS, RW_COLS), "s_wkv": (1, NS, HR, CR, CR),
           "s_conv": (1, NS, 3, GD_QKV), "s_ssm": (1, NS, HG, CG, CG)}
_SCRATCH = {"rows_rw": (6, NS * HR, CR), "rows_gd": (3, NS * HG, CG), "rows_bg": (2, NS * HG), "o_rw": (NS * HR, CR),
            "x1_rows": (T, D), "x1_parts": ((3, T, D), "bf16")}


def kernel(**inputs):
    import numpy as _np
    import concourse.bacc as _bacc
    from concourse import mybir as _mybir
    from concourse.bass_utils import run_bass_kernel_spmd as _run

    nc = _bacc.Bacc("TRN2", target_bir_lowering=False, num_devices=1)
    arrays, a = {}, {}
    for name in _INS + ["consts"]:
        x = _np.ascontiguousarray(CONSTS if name == "consts" else inputs[name])
        arrays[name + "_dram"] = x
        a[name] = nc.dram_tensor(name + "_dram", x.shape, _mybir.dt.from_np(x.dtype), kind="ExternalInput").ap()
    for name, shape in _SHAPES.items():
        a[name] = nc.dram_tensor(name + "_dram", shape, _mybir.dt.float32, kind="ExternalOutput").ap()
    for name, shape in _SCRATCH.items():
        dt = _mybir.dt.float32
        if isinstance(shape[-1], str):
            shape, dt = shape[0], _mybir.dt.bfloat16
        a[name] = nc.dram_tensor(name + "_dram", shape, dt, kind="Internal").ap()
    program(nc, a)
    r = _run(nc, [arrays], core_ids=[0])
    return tuple(r.results[0][name + "_dram"] for name in _SHAPES)
```
